# Optimizing a Trainium2 kernel written in Bass

```python
import math
import jax, jax.numpy as jnp
from jax import lax
import numpy as np

D_MODEL = 1024
BATCH = 1
SEQ = 512
DEPTH = 1

CHUNK = 64
N_MEM = 256
EPS = 1e-6
ROPE_THETA = 10000.0
NEG = -1e30

A_HEADS = 4
A_DK = 64
A_DV = 2 * A_DK
A_QK_W = A_HEADS * 2 * A_DK
A_WIDTH = A_HEADS * A_DV
Q_BLOCK = 128

B_HEADS = 8
B_DH = 64
B_WIDTH = B_HEADS * B_DH
B_LEFT_CHUNKS = 8
B_MAX_REL = 256

X_HEADS = 4
X_DH = D_MODEL // X_HEADS

D_FF = -(-(8 * D_MODEL) // (3 * 256)) * 256

OFF_QA = 0
OFF_KA = OFF_QA + A_QK_W
OFF_VA = OFF_KA + A_QK_W
OFF_QB = OFF_VA + A_WIDTH
OFF_KB = OFF_QB + B_WIDTH
OFF_VB = OFF_KB + B_WIDTH
OFF_GA = OFF_VB + B_WIDTH
OFF_GB = OFF_GA + D_MODEL
IN_COLS = OFF_GB + D_MODEL


def rmsnorm(x, g):
    xf = x.astype(jnp.float32)
    y = xf * lax.rsqrt(jnp.mean(xf * xf, axis=-1, keepdims=True) + EPS)
    return (y * g.astype(jnp.float32)).astype(x.dtype)

def rope_tables(seq, dim):
    inv = 1.0 / (ROPE_THETA ** (jnp.arange(0, dim, 2, dtype=jnp.float32) / dim))
    ang = jnp.arange(seq, dtype=jnp.float32)[:, None] * inv[None, :]
    return jnp.cos(ang), jnp.sin(ang)

def apply_rope(x, cos, sin):
    x1, x2 = jnp.split(x.astype(jnp.float32), 2, axis=-1)
    out = jnp.concatenate([x1 * cos - x2 * sin, x2 * cos + x1 * sin], axis=-1)
    return out.astype(x.dtype)

def diff_attention(q, k, v, lam, subln_g, lam_init):
    b, s = q.shape[0], q.shape[1]
    nqb = s // Q_BLOCK
    scale = A_DK ** -0.5
    k_chunk = jnp.arange(s) // CHUNK
    qb = q.reshape(b, nqb, Q_BLOCK, A_HEADS, 2, A_DK).transpose(1, 0, 2, 3, 4, 5)

    def one_block(args):
        qi, blk = args
        sc = jnp.einsum('bqhcd,bkhcd->bchqk', qi, k).astype(jnp.float32) * scale
        q_chunk = (blk * Q_BLOCK + jnp.arange(Q_BLOCK)) // CHUNK
        mask = k_chunk[None, :] <= q_chunk[:, None]
        sc = jnp.where(mask[None, None, None], sc, NEG)
        p = jax.nn.softmax(sc, axis=-1)
        attn = p[:, 0] - lam * p[:, 1]
        return jnp.einsum('bhqk,bkhd->bqhd', attn.astype(v.dtype), v)

    o = lax.map(one_block, (qb, jnp.arange(nqb)))
    o = o.transpose(1, 0, 2, 3, 4).reshape(b, s, A_HEADS, A_DV)
    o = rmsnorm(o, subln_g) * (1.0 - lam_init)
    return o.reshape(b, s, A_WIDTH)

def chunk_band_attention(q, k, v, rel_bias):
    b, s = q.shape[0], q.shape[1]
    nc = s // CHUNK
    pad = B_LEFT_CHUNKS * CHUNK
    band = pad + CHUNK
    scale = B_DH ** -0.5
    kp = jnp.pad(k, ((0, 0), (pad, 0), (0, 0), (0, 0)))
    vp = jnp.pad(v, ((0, 0), (pad, 0), (0, 0), (0, 0)))
    i = jnp.arange(CHUNK)
    j = jnp.arange(band)
    dist = i[:, None] + pad - j[None, :]
    idx = jnp.clip(dist, -B_MAX_REL, B_MAX_REL) + B_MAX_REL
    bias = rel_bias[:, idx].astype(jnp.float32)
    qc = q.reshape(b, nc, CHUNK, B_HEADS, B_DH).transpose(1, 0, 2, 3, 4)

    def one_chunk(args):
        qi, c = args
        start = c * CHUNK
        kb = lax.dynamic_slice_in_dim(kp, start, band, axis=1)
        vb = lax.dynamic_slice_in_dim(vp, start, band, axis=1)
        sc = jnp.einsum('bqhd,bkhd->bhqk', qi, kb).astype(jnp.float32) * scale + bias[None]
        valid = (start + j) >= pad
        sc = jnp.where(valid[None, None, None, :], sc, NEG)
        p = jax.nn.softmax(sc, axis=-1)
        return jnp.einsum('bhqk,bkhd->bqhd', p.astype(vb.dtype), vb)

    o = lax.map(one_chunk, (qc, jnp.arange(nc)))
    return o.transpose(1, 0, 2, 3, 4).reshape(b, s, B_WIDTH)

def memory_cross_attention(h, m, w_cq, w_ckv, w_co):
    b, s = h.shape[0], h.shape[1]
    nm = m.shape[1]
    q = (h @ w_cq).reshape(b, s, X_HEADS, X_DH)
    k, v = jnp.split(m @ w_ckv, 2, axis=-1)
    k = k.reshape(b, nm, X_HEADS, X_DH)
    v = v.reshape(b, nm, X_HEADS, X_DH)
    sc = jnp.einsum('bshd,bmhd->bhsm', q, k).astype(jnp.float32) * (X_DH ** -0.5)
    p = jax.nn.softmax(sc, axis=-1)
    o = jnp.einsum('bhsm,bmhd->bshd', p.astype(v.dtype), v).reshape(b, s, D_MODEL)
    return o @ w_co

def swiglu(h, w_gate_up, w_down):
    g, u = jnp.split(h @ w_gate_up, 2, axis=-1)
    return (jax.nn.silu(g) * u) @ w_down

def first_inputs(seed: int = 0) -> dict:
    key = jax.random.key(seed)
    ks = jax.random.split(key, 24)
    nrm = lambda k, shape, sc: jax.random.normal(k, shape, jnp.float32) * sc
    gain = lambda k, shape: 1.0 + 0.05 * jax.random.normal(k, shape, jnp.float32)
    L = DEPTH
    return {
        "x": nrm(ks[0], (BATCH, SEQ, D_MODEL), 1.0),
        "mem": nrm(ks[1], (BATCH, N_MEM, D_MODEL), 1.0),
        "norm_mix_g": gain(ks[2], (L, D_MODEL)),
        "w_in": nrm(ks[3], (L, D_MODEL, IN_COLS), D_MODEL ** -0.5),
        "lam_q1": nrm(ks[4], (L, A_DK), 0.1),
        "lam_k1": nrm(ks[5], (L, A_DK), 0.1),
        "lam_q2": nrm(ks[6], (L, A_DK), 0.1),
        "lam_k2": nrm(ks[7], (L, A_DK), 0.1),
        "subln_g": gain(ks[8], (L, A_DV)),
        "rel_bias": nrm(ks[9], (L, B_HEADS, 2 * B_MAX_REL + 1), 0.1),
        "w_up_a": nrm(ks[10], (L, A_WIDTH, D_MODEL), A_WIDTH ** -0.5),
        "w_up_b": nrm(ks[11], (L, B_WIDTH, D_MODEL), B_WIDTH ** -0.5),
        "w_out": nrm(ks[12], (L, D_MODEL, D_MODEL), D_MODEL ** -0.5),
        "norm_cross_g": gain(ks[13], (L, D_MODEL)),
        "norm_mem_g": gain(ks[14], (L, D_MODEL)),
        "w_cq": nrm(ks[15], (L, D_MODEL, D_MODEL), D_MODEL ** -0.5),
        "w_ckv": nrm(ks[16], (L, D_MODEL, 2 * D_MODEL), D_MODEL ** -0.5),
        "w_co": nrm(ks[17], (L, D_MODEL, D_MODEL), D_MODEL ** -0.5),
        "norm_ffn_g": gain(ks[18], (L, D_MODEL)),
        "w_gate_up": nrm(ks[19], (L, D_MODEL, 2 * D_FF), D_MODEL ** -0.5),
        "w_down": nrm(ks[20], (L, D_FF, D_MODEL), D_FF ** -0.5),
        "norm_final_g": gain(ks[21], (D_MODEL,)),
    }

def first_block(x, mem, norm_mix_g, w_in, lam_q1, lam_k1, lam_q2, lam_k2, subln_g,
              rel_bias, w_up_a, w_up_b, w_out, norm_cross_g, norm_mem_g, w_cq,
              w_ckv, w_co, norm_ffn_g, w_gate_up, w_down, norm_final_g):
    b, s = x.shape[0], x.shape[1]
    cos, sin = rope_tables(s, A_DK)
    cos_a = cos[None, :, None, None, :]
    sin_a = sin[None, :, None, None, :]
    for layer in range(DEPTH):
        lam_init = 0.8 - 0.6 * math.exp(-0.3 * layer)
        h = rmsnorm(x, norm_mix_g[layer])
        z = h @ w_in[layer]
        qa = z[..., OFF_QA:OFF_KA].reshape(b, s, A_HEADS, 2, A_DK)
        ka = z[..., OFF_KA:OFF_VA].reshape(b, s, A_HEADS, 2, A_DK)
        va = z[..., OFF_VA:OFF_QB].reshape(b, s, A_HEADS, A_DV)
        qb = z[..., OFF_QB:OFF_KB].reshape(b, s, B_HEADS, B_DH)
        kb = z[..., OFF_KB:OFF_VB].reshape(b, s, B_HEADS, B_DH)
        vb = z[..., OFF_VB:OFF_GA].reshape(b, s, B_HEADS, B_DH)
        ga = z[..., OFF_GA:OFF_GB]
        gb = z[..., OFF_GB:IN_COLS]
        qa = apply_rope(qa, cos_a, sin_a)
        ka = apply_rope(ka, cos_a, sin_a)
        lam = (jnp.exp(jnp.sum(lam_q1[layer].astype(jnp.float32) * lam_k1[layer].astype(jnp.float32)))
               - jnp.exp(jnp.sum(lam_q2[layer].astype(jnp.float32) * lam_k2[layer].astype(jnp.float32)))
               + lam_init)
        ya = diff_attention(qa, ka, va, lam, subln_g[layer], lam_init)
        yb = chunk_band_attention(qb, kb, vb, rel_bias[layer])
        merged = (jax.nn.sigmoid(ga) * (ya @ w_up_a[layer])
                  + jax.nn.sigmoid(gb) * (yb @ w_up_b[layer]))
        x = x + merged @ w_out[layer]
        hc = rmsnorm(x, norm_cross_g[layer])
        mn = rmsnorm(mem, norm_mem_g[layer])
        x = x + memory_cross_attention(hc, mn, w_cq[layer], w_ckv[layer], w_co[layer])
        hf = rmsnorm(x, norm_ffn_g[layer])
        x = x + swiglu(hf, w_gate_up[layer], w_down[layer])
    return rmsnorm(x, norm_final_g)


GRID_W = 64
CTX_LEN = 256
D_HYENA = 512
D_GLA = D_MODEL - D_HYENA
GLA_HEADS = 4
GLA_DK = D_GLA // 2
GLA_DV = D_GLA
GLA_HEAD_DK = GLA_DK // GLA_HEADS
GLA_HEAD_DV = GLA_DV // GLA_HEADS
GATE_RANK = 16
GATE_NORMALIZER = 16.0
GLA_CHUNK = 64
SHORT_CONV = 3
FILTER_EMB = 33
FILTER_BANDS = (FILTER_EMB - 1) // 2
FILTER_HIDDEN = 64
FAST_DECAY_PCT = 0.3
SLOW_DECAY_PCT = 1.5
DECAY_TARGET = 1e-2
D_FF_2 = 4 * D_MODEL
PROJ_WIDTHS = (3 * D_HYENA, GLA_DK, GLA_DK, GLA_DV, GLA_DV, GATE_RANK, GATE_RANK)
PROJ_SPLITS = tuple(int(s) for s in np.cumsum(PROJ_WIDTHS)[:-1])
N_IN = sum(PROJ_WIDTHS)


def _rms_norm(x, g):
    xf = x.astype(jnp.float32)
    y = xf * lax.rsqrt(jnp.mean(xf * xf, axis=-1, keepdims=True) + EPS)
    return (y * g.astype(jnp.float32)).astype(x.dtype)

def _sq_relu_mlp(h, w1, w2):
    return jnp.square(jax.nn.relu(h @ w1)) @ w2

def _short_conv(u, w, b):
    t = u.shape[-2]
    pad = SHORT_CONV // 2
    up = jnp.pad(u, [(0, 0)] * (u.ndim - 2) + [(pad, pad), (0, 0)])
    out = b
    for j in range(SHORT_CONV):
        out = out + w[j] * up[..., j:j + t, :]
    return out

def _hyena_spectrum(length, w1, b1, w2, b2, w3, b3, freq, wout):
    f32 = jnp.float32
    t = jnp.linspace(0.0, 1.0, length, dtype=f32)[:, None]
    w = 2.0 * math.pi * jnp.arange(length, dtype=f32) / length
    f = jnp.linspace(1e-4, FILTER_BANDS - 1, FILTER_BANDS, dtype=f32)
    ang = w[:, None] * f[None, :]
    z = jnp.concatenate([t, jnp.cos(ang), -jnp.sin(ang)], axis=-1)
    fr = freq.astype(f32)
    hdn = jnp.sin(fr * (z @ w1.astype(f32) + b1.astype(f32)))
    hdn = jnp.sin(fr * (hdn @ w2.astype(f32) + b2.astype(f32)))
    hdn = jnp.sin(fr * (hdn @ w3.astype(f32) + b3.astype(f32)))
    h = (hdn @ wout.astype(f32)).reshape(length, 2, D_HYENA)
    min_decay = math.log(DECAY_TARGET) / SLOW_DECAY_PCT
    max_decay = math.log(DECAY_TARGET) / FAST_DECAY_PCT
    deltas = jnp.abs(jnp.linspace(min_decay, max_decay, D_HYENA, dtype=f32))
    h = h * jnp.exp(-t * deltas)[:, None, :]
    kern = jnp.concatenate([h[:, 0], jnp.zeros((1, D_HYENA), f32), h[:0:-1, 1]], axis=0)
    kern = kern * lax.rsqrt(jnp.sum(kern * kern, axis=0, keepdims=True) + EPS)
    return jnp.fft.rfft(kern, axis=0)

def _long_conv(u, spec, bias):
    length = u.shape[1]
    uf = u.astype(jnp.float32)
    y = jnp.fft.irfft(jnp.fft.rfft(uf, n=2 * length, axis=1) * spec, n=2 * length, axis=1)[:, :length]
    return (y + uf * bias.astype(jnp.float32)).astype(u.dtype)

def _hyena_gate_conv(u, spec, bias):
    x0, x1, v = jnp.split(u, 3, axis=-1)
    return x0 * _long_conv(x1 * v, spec, bias)

def _to_heads(z, n_heads):
    b, t, w = z.shape
    return z.reshape(b, t, n_heads, w // n_heads).transpose(0, 2, 1, 3)

def _log_gate(gr, w, b):
    lg = jax.nn.log_sigmoid(gr.astype(jnp.float32) @ w.astype(jnp.float32) + b.astype(jnp.float32))
    return _to_heads(lg / GATE_NORMALIZER, GLA_HEADS)

def _gla_chunked(q, k, v, lg, s0):
    bsz, nh, t, dk = q.shape
    dv = v.shape[-1]
    n = t // GLA_CHUNK
    q = q.reshape(bsz, nh, n, GLA_CHUNK, dk)
    k = k.reshape(bsz, nh, n, GLA_CHUNK, dk)
    lg = lg.reshape(bsz, nh, n, GLA_CHUNK, dk)
    v = v.reshape(bsz, nh, n, GLA_CHUNK, dv)
    b = jnp.cumsum(lg, axis=3)
    b_last = b[:, :, :, -1:, :]
    q_in = q * jnp.exp(b)
    k_in = k * jnp.exp(-b)
    k_end = k * jnp.exp(b_last - b)
    mask = jnp.tril(jnp.ones((GLA_CHUNK, GLA_CHUNK), dtype=bool))
    att = jnp.where(mask, jnp.einsum('bhncd,bhnsd->bhncs', q_in, k_in), 0.0)
    o_intra = jnp.einsum('bhncs,bhnse->bhnce', att, v)
    ds = jnp.einsum('bhnsd,bhnse->nbhde', k_end, v)
    decay = jnp.moveaxis(jnp.exp(b_last[:, :, :, 0, :]), 2, 0)

    def step(s, inp):
        d, dsn = inp
        return d[..., None] * s + dsn, s

    s_final, s_start = lax.scan(step, s0, (decay, ds))
    o_inter = jnp.einsum('bhncd,nbhde->bhnce', q_in, s_start)
    return (o_intra + o_inter).reshape(bsz, nh, t, dv), s_final

def _gla_final_state(k, v, lg):
    b = jnp.cumsum(lg, axis=2)
    return jnp.einsum('bhtd,bhte->bhde', k * jnp.exp(b[:, :, -1:] - b), v)

def _rev(a):
    return jnp.flip(a, axis=2)

def _gla_bidir(q, k, v, lg_f, lg_b, s_f0, s_b0):
    o_f, s_f = _gla_chunked(q, k, v, lg_f, s_f0)
    o_b, s_b = _gla_chunked(_rev(q), _rev(k), _rev(v), _rev(lg_b), s_b0)
    return o_f + _rev(o_b), s_f, s_b

def _gla_heads(q, k, v):
    f32 = jnp.float32
    qh = _to_heads(q.astype(f32), GLA_HEADS) * (GLA_HEAD_DK ** -0.5)
    return qh, _to_heads(k.astype(f32), GLA_HEADS), _to_heads(v.astype(f32), GLA_HEADS)

def _gla_output(o, og, g_norm):
    on = o * lax.rsqrt(jnp.mean(o * o, axis=-1, keepdims=True) + EPS) * g_norm.astype(jnp.float32)
    bsz, _, t, _ = o.shape
    y = on.transpose(0, 2, 1, 3).reshape(bsz, t, GLA_DV)
    return (y * jax.nn.silu(og.astype(jnp.float32))).astype(og.dtype)

def second_inputs(seed: int = 0) -> dict:
    key = jax.random.key(seed)
    ks = jax.random.split(key, 29)
    D = D_MODEL
    L = DEPTH

    def nrm(i, shape, scale):
        return scale * jax.random.normal(ks[i], shape, jnp.float32)

    return {
        'x': nrm(0, (BATCH, SEQ, D), 1.0),
        'c': nrm(1, (BATCH, D), 1.0),
        'ctx': nrm(2, (BATCH, CTX_LEN, D), 1.0),
        'c_ctx': nrm(3, (D,), 1.0),
        'w_ada': nrm(4, (L, D, 6 * D), 0.5 * D ** -0.5),
        'b_ada': nrm(5, (L, 6 * D), 0.02),
        'norm_mix': 1.0 + nrm(6, (L, D), 0.05),
        'norm_mlp': 1.0 + nrm(7, (L, D), 0.05),
        'w_in': nrm(8, (L, D, N_IN), D ** -0.5),
        'conv_w': nrm(9, (L, SHORT_CONV, 3 * D_HYENA), SHORT_CONV ** -0.5),
        'conv_b': nrm(10, (L, 3 * D_HYENA), 0.02),
        'filt_w1': nrm(11, (L, FILTER_EMB, FILTER_HIDDEN), FILTER_EMB ** -0.5),
        'filt_b1': nrm(12, (L, FILTER_HIDDEN), 0.1),
        'filt_w2': nrm(13, (L, FILTER_HIDDEN, FILTER_HIDDEN), FILTER_HIDDEN ** -0.5),
        'filt_b2': nrm(14, (L, FILTER_HIDDEN), 0.1),
        'filt_w3': nrm(15, (L, FILTER_HIDDEN, FILTER_HIDDEN), FILTER_HIDDEN ** -0.5),
        'filt_b3': nrm(16, (L, FILTER_HIDDEN), 0.1),
        'filt_freq': 1.0 + nrm(17, (L, FILTER_HIDDEN), 0.1),
        'filt_wout': nrm(18, (L, FILTER_HIDDEN, 2 * D_HYENA), FILTER_HIDDEN ** -0.5),
        'hyena_bias': nrm(19, (L, D_HYENA), 0.5),
        'gk_w_fwd': nrm(20, (L, GATE_RANK, GLA_DK), GATE_RANK ** -0.5),
        'gk_b_fwd': nrm(21, (L, GLA_DK), 0.1),
        'gk_w_bwd': nrm(22, (L, GATE_RANK, GLA_DK), GATE_RANK ** -0.5),
        'gk_b_bwd': nrm(23, (L, GLA_DK), 0.1),
        'gla_norm': 1.0 + nrm(24, (L, GLA_HEAD_DV), 0.05),
        'w_out': nrm(25, (L, D, D), D ** -0.5),
        'w_mlp1': nrm(26, (L, D, D_FF_2), D ** -0.5),
        'w_mlp2': nrm(27, (L, D_FF_2, D), D_FF_2 ** -0.5),
        'norm_final': 1.0 + nrm(28, (D,), 0.05),
    }

def second_block(x, c, ctx, c_ctx, w_ada, b_ada, norm_mix, norm_mlp, w_in, conv_w, conv_b,
              filt_w1, filt_b1, filt_w2, filt_b2, filt_w3, filt_b3, filt_freq, filt_wout,
              hyena_bias, gk_w_fwd, gk_b_fwd, gk_w_bwd, gk_b_bwd, gla_norm, w_out,
              w_mlp1, w_mlp2, norm_final):
    bsz, seq, _ = x.shape
    rows = seq // GRID_W
    ctx_len = ctx.shape[1]
    for l in range(DEPTH):
        last = l == DEPTH - 1
        filt = (filt_w1[l], filt_b1[l], filt_w2[l], filt_b2[l], filt_w3[l], filt_b3[l], filt_freq[l], filt_wout[l])
        mod = jax.nn.silu(c) @ w_ada[l] + b_ada[l]
        mod_c = jax.nn.silu(c_ctx) @ w_ada[l] + b_ada[l]
        sh1, sc1, g1, sh2, sc2, g2 = jnp.split(mod[:, None, :], 6, axis=-1)
        csh1, csc1, cg1, csh2, csc2, cg2 = jnp.split(mod_c, 6)

        h_lat = _rms_norm(x, norm_mix[l]) * (1.0 + sc1) + sh1
        h_ctx = _rms_norm(ctx, norm_mix[l]) * (1.0 + csc1) + csh1
        hy_l, q_l, k_l, v_l, og_l, gf_l, gb_l = jnp.split(h_lat @ w_in[l], PROJ_SPLITS, axis=-1)
        hy_c, q_c, k_c, v_c, og_c, gf_c, gb_c = jnp.split(h_ctx @ w_in[l], PROJ_SPLITS, axis=-1)

        qh_c, kh_c, vh_c = _gla_heads(q_c, k_c, v_c)
        lgf_c = _log_gate(gf_c, gk_w_fwd[l], gk_b_fwd[l])
        lgb_c = _log_gate(gb_c, gk_w_bwd[l], gk_b_bwd[l])
        if last:
            s_f = _gla_final_state(kh_c, vh_c, lgf_c)
            s_b = _gla_final_state(_rev(kh_c), _rev(vh_c), _rev(lgb_c))
        else:
            zeros = jnp.zeros((bsz, GLA_HEADS, GLA_HEAD_DK, GLA_HEAD_DV), jnp.float32)
            o_c, s_f, s_b = _gla_bidir(qh_c, kh_c, vh_c, lgf_c, lgb_c, zeros, zeros)

        qh_l, kh_l, vh_l = _gla_heads(q_l, k_l, v_l)
        lgf_l = _log_gate(gf_l, gk_w_fwd[l], gk_b_fwd[l])
        lgb_l = _log_gate(gb_l, gk_w_bwd[l], gk_b_bwd[l])
        o_l, _, _ = _gla_bidir(qh_l, kh_l, vh_l, lgf_l, lgb_l, s_f, s_b)
        y_gla_l = _gla_output(o_l, og_l, gla_norm[l])

        u_l = _short_conv(hy_l.reshape(bsz, rows, GRID_W, 3 * D_HYENA), conv_w[l], conv_b[l])
        u_l = u_l.reshape(bsz, seq, 3 * D_HYENA)
        y_hy_l = _hyena_gate_conv(u_l, _hyena_spectrum(seq, *filt), hyena_bias[l])

        x = x + g1 * (jnp.concatenate([y_hy_l, y_gla_l], axis=-1) @ w_out[l])
        h2 = _rms_norm(x, norm_mlp[l]) * (1.0 + sc2) + sh2
        x = x + g2 * _sq_relu_mlp(h2, w_mlp1[l], w_mlp2[l])

        if not last:
            u_c = _short_conv(hy_c, conv_w[l], conv_b[l])
            y_hy_c = _hyena_gate_conv(u_c, _hyena_spectrum(ctx_len, *filt), hyena_bias[l])
            y_gla_c = _gla_output(o_c, og_c, gla_norm[l])
            ctx = ctx + cg1 * (jnp.concatenate([y_hy_c, y_gla_c], axis=-1) @ w_out[l])
            h2c = _rms_norm(ctx, norm_mlp[l]) * (1.0 + csc2) + csh2
            ctx = ctx + cg2 * _sq_relu_mlp(h2c, w_mlp1[l], w_mlp2[l])
    return _rms_norm(x, norm_final)


def setup_inputs(seed=0):
    out = dict(first_inputs(seed))
    for name, value in second_inputs(seed + 1).items():
        if name != "x":
            out[name + "_2"] = value
    return out


def reference(
    x, mem, norm_mix_g, w_in, lam_q1, lam_k1, lam_q2, lam_k2, subln_g, rel_bias, w_up_a, w_up_b,
    w_out, norm_cross_g, norm_mem_g, w_cq, w_ckv, w_co, norm_ffn_g, w_gate_up, w_down,
    norm_final_g, c_2, ctx_2, c_ctx_2, w_ada_2, b_ada_2, norm_mix_2, norm_mlp_2, w_in_2,
    conv_w_2, conv_b_2, filt_w1_2, filt_b1_2, filt_w2_2, filt_b2_2, filt_w3_2, filt_b3_2,
    filt_freq_2, filt_wout_2, hyena_bias_2, gk_w_fwd_2, gk_b_fwd_2, gk_w_bwd_2, gk_b_bwd_2,
    gla_norm_2, w_out_2, w_mlp1_2, w_mlp2_2, norm_final_2,
):
    x = first_block(
        x, mem, norm_mix_g, w_in, lam_q1, lam_k1, lam_q2, lam_k2, subln_g, rel_bias, w_up_a,
        w_up_b, w_out, norm_cross_g, norm_mem_g, w_cq, w_ckv, w_co, norm_ffn_g, w_gate_up,
        w_down, norm_final_g,
    )
    return second_block(
        x, c_2, ctx_2, c_ctx_2, w_ada_2, b_ada_2, norm_mix_2, norm_mlp_2, w_in_2, conv_w_2,
        conv_b_2, filt_w1_2, filt_b1_2, filt_w2_2, filt_b2_2, filt_w3_2, filt_b3_2, filt_freq_2,
        filt_wout_2, hyena_bias_2, gk_w_fwd_2, gk_b_fwd_2, gk_w_bwd_2, gk_b_bwd_2, gla_norm_2,
        w_out_2, w_mlp1_2, w_mlp2_2, norm_final_2,
    )


_drawn_inputs = setup_inputs


def setup_inputs(seed=0):
    import zlib

    import numpy as np

    out = dict(_drawn_inputs(seed))
    spreads = {}
    factors = {'lam_k1': 3.595,
     'lam_q2': 3.807,
     'rel_bias': 8.0,
     'norm_cross_g': 8.0,
     'norm_mem_g': 6.595,
     'ctx_2': 3.68,
     'c_ctx_2': 4.791,
     'conv_b_2': 3.777,
     'gk_b_fwd_2': 8.0,
     'gk_w_bwd_2': 3.787,
     'gk_b_bwd_2': 8.0,
     'gla_norm_2': 8.0,
     'norm_ffn_g': 5.65,
     'norm_mlp_2': 3.799}
    for name, (base, spread) in spreads.items():
        noise = np.random.default_rng([zlib.crc32(name.encode()), seed]).standard_normal(out[name].shape)
        drawn = base * np.exp(spread * noise) if base else spread * noise
        out[name] = __import__('jax').numpy.asarray(drawn.astype(out[name].dtype))
    for name, factor in factors.items():
        out[name] = (out[name] * factor).astype(out[name].dtype)
    return out
```

```python
from contextlib import ExitStack

import concourse.bass as bass
import numpy as np
from concourse import mybir

ALU = mybir.AluOpType
ACT = mybir.ActivationFunctionType
AX = mybir.AxisListType
F32 = mybir.dt.float32
F32R = mybir.dt.float32r

P = 128
D = 1024
DT = D // P
S = 512
ST = S // P
MEM = 256
EPS = 1e-6
NEG = -1e30
CHUNK = 64
NCH = S // CHUNK
A_HEADS, A_DK = 4, 64
B_HEADS, B_DH = 8, 64
X_HEADS = 4
D_FF = 2816
FT = D_FF // P
HALF = FT // 2
LAM_INIT = 0.8 - 0.6
MAX_REL = 256
REL = 2 * MAX_REL + 1
D_HY = 512
HT = D_HY // P
G_HEADS = 4
RANK = 16
LOG_SCALE = 1.0 / 16.0
D_MLP = 4 * D
N_IN_2 = 3104
EMB, HID = 33, 64
TWO_PI_HI = 6.28125
TWO_PI_LO = 2 * np.pi - 6.28125
ROUND = 1.5 * 2.0 ** 23
PI_SAFE = 3.1415925

SLOTS = 3
SLAB_KT = 8

VEC_ROWS = [("norm_mix_g", 8), ("norm_cross_g", 8), ("norm_mem_g", 8), ("norm_ffn_g", 8),
            ("norm_final_g", 8), ("norm_mix_2", 8), ("norm_mlp_2", 8), ("norm_final_2", 8),
            ("subln_g", 1), ("gla_norm_2", 1), ("hyena_bias_2", 4), ("gk_b_fwd_2", 2),
            ("gk_b_bwd_2", 2), ("c_2", 8), ("c_ctx_2", 8), ("b_ada_2", 48), ("conv_w_2", 36),
            ("conv_b_2", 12)]
VEC_AT, _at = {}, 0
for _name, _n in VEC_ROWS:
    VEC_AT[_name] = _at
    _at += _n
VECS = _at
VEC_SPLIT = VEC_AT["b_ada_2"]


class Stage:

    def __init__(self, name, n, kt, source, unroll=3):
        self.name, self.n, self.kt, self.source, self.unroll, self.base = name, n, kt, source, unroll, 0


class Pos:

    def __init__(self, stage, it, j, lo):
        self.it, self.j, self.lo = it, j, lo
        self.pair = it * (stage.unroll // 2) + (lo + j) // 2
        self.i = it * stage.unroll + (lo + j)
        b = stage.base + lo + j
        self.slot = b % SLOTS
        self.turn = it * (stage.unroll // SLOTS) + b // SLOTS
        self.u = self.i + stage.base


def each_unit(eng, stage, body, lo=0, hi=None):
    hi = stage.n if hi is None else hi
    k = stage.unroll
    start = lo
    if stage.base + lo < SLOTS:
        for j in range(k):
            body(Pos(stage, 0, j, lo))
        start = lo + k
    n = (hi - start) // k
    if n >= 2:
        with eng.Fori(0, n, 1) as it:
            for j in range(k):
                body(Pos(stage, it, j, start))
        start += n * k
    for j in range(hi - start):
        body(Pos(stage, j // k, j % k, start))


class Own:

    def __init__(self, eng, sem):
        self.eng, self.sem, self.n, self.at = eng, sem, 0, 0

    def mark(self, ins):
        ins.then_inc(self.sem, 1)
        self.n += 1

    def settle(self):
        self.eng.wait_ge(self.sem, self.at + self.n)

    def step(self, ins):
        self.mark(ins)
        self.settle()

    def group(self, first, index, per):
        self.at, self.n = index * per + first, 0

    def leave(self, total):
        self.at, self.n = 0, total


def build(nc, t, out):
    ctx = ExitStack()
    with ctx:
        top = [16512]

        def place(name, shape, dt=F32, at=None):
            size = int(np.prod(shape[1:])) * 4
            if at is None:
                at = top[0]
                top[0] += (size + 31) // 32 * 32
            assert at + size <= 229344, (name, at + size)
            return nc.alloc_sbuf_tensor_at(name, shape, dt, offset=at)

        def sem(name):
            return ctx.enter_context(nc.semaphore(name))

        raw = [place(f"raw{i}", [P, SLAB_KT, P]) for i in range(SLOTS)]
        WH = [place(f"WH{i}", [P, SLAB_KT, P], F32R) for i in range(SLOTS)]
        WL = [place(f"WL{i}", [P, SLAB_KT, P], F32R) for i in range(SLOTS)]
        x = place("x", [P, DT, S])
        h_at = top[0]
        hH = place("hH", [P, DT, S], F32R)
        hL = place("hL", [P, DT, S], F32R)
        r = place("r", [P, S])
        acc = place("acc", [P, S])
        tmp = [place(f"tmp{i}", [P, S]) for i in range(4)]
        ident = place("ident", [P, P])
        ones = place("ones", [P, P])
        swap = place("swap", [P, P])
        anti = place("anti", [P, P])
        vec = place("vec", [P, VECS])
        cS = place("cS", [P, DT, 2])
        cR = place("cR", [P, DT, 4], F32R)
        mod = place("mod", [P, 48, 2])
        gain = place("gain", [P, 4, DT])
        lam_parts = place("lam_parts", [P, 4, A_DK])
        lam_s = place("lam_s", [P, 8])
        tiny = place("tiny", [P, 16])
        mask_row = place("mask_row", [1, P + CHUNK])
        nrm = place("nrm", [P, HT])
        gate_w = place("gate_w", [2 * RANK, 2, 256])
        Z = top[0]

        def z(name, kb, shape, dt=F32):
            return place(name, shape, dt, at=Z + int(kb * 1024))

        def hz(name, kb, shape, dt=F32):
            return place(name, shape, dt, at=h_at + int(kb * 1024))

        qA = z("qA", 0, [P, 4, S])
        kA = z("kA", 8, [P, 4, S])
        qB = z("qB", 16, [P, 4, S])
        kB = z("kB", 24, [P, 4, S])
        vA = z("vA", 32, [P, ST, S])
        vB = z("vB", 40, [P, ST, S])
        gates = z("gates", 48, [P, 2 * DT, S])
        tok = z("tok", 48, [P, ST, D])
        rope = z("rope", 64, [P, 2, S])
        vecload = z("vecload", 68, [P, 2, P])
        bias_t = z("bias_t", 80, [P, B_HEADS, S])
        rows = [z(f"rows{i}", 96 + 2 * i, [4, S]) for i in range(4)]
        mod_rows = z("mod_rows", 96, [48, 4, P])
        hankel = z("hankel", 0, [P, B_HEADS, S])
        rel_ext = z("rel_ext", 16, [B_HEADS, 768])
        attT = [hz(f"attT{i}", 8 * i, [P, ST, S]) for i in range(2)]
        pA = [hz(f"pA{i}", 16 + 4 * i, [P, 2, S]) for i in range(2)]
        pB = [hz(f"pB{i}", 16 + 2 * i, [P, S]) for i in range(4)]
        mgH = z("mgH", 0, [P, DT, S], F32R)
        mgL = z("mgL", 16, [P, DT, S], F32R)
        memtok = z("memtok", 32, [P, 2, D])
        memH = z("memH", 40, [P, DT, MEM], F32R)
        memL = z("memL", 80, [P, DT, MEM], F32R)
        rm = z("rm", 88, [P, MEM])
        kc = z("kc", 48, [P, DT, MEM])
        vc = z("vc", 56, [P, 2, D])
        qc = z("qc", 64, [P, DT, S])
        oH = z("oH", 0, [P, DT, S], F32R)
        oL = z("oL", 16, [P, DT, S], F32R)
        pC = [z(f"pC{i}", 32 + i, [P, MEM]) for i in range(4)]
        pcT = [z(f"pcT{i}", 36 + 4 * i, [P, 2, S]) for i in range(2)]
        fH = z("fH", 0, [P, FT, S], F32R)
        fL = z("fL", 44, [P, FT, S], F32R)
        ctxtok = z("ctxtok", 88, [P, 2, D])
        ctxT = z("ctxT", 96, [P, DT, MEM])
        rc = z("rc", 88, [P, MEM])
        acc2 = z("acc2", 89, [P, S])
        r2 = z("r2", 91, [P, S])
        hy = z("hy", 0, [P, 12, S])
        qG = z("qG", 24, [P, 2, S])
        kG = z("kG", 28, [P, 2, S])
        masks = z("masks", 32, [P, 2, P])
        reset = z("reset", 34, [P, S])
        vG = z("vG", 40, [P, ST, S])
        kGc = z("kGc", 48, [P, 2, MEM])
        vGc = z("vGc", 50, [P, 2, S])
        gr = z("gr", 54, [2 * RANK, S + MEM])
        cH = z("cH", 65, [P, DT, MEM], F32R)
        cL = z("cL", 73, [P, DT, MEM], F32R)
        vfT = [z(f"vfT{i}", 81 + 2 * i, [P, S]) for i in range(2)]
        vfTc = [z(f"vfTc{i}", 85 + i, [P, MEM]) for i in range(2)]
        og = z("og", 96, [P, 4, S])
        kin = [hz(f"kin{i}", 2 * i, [P, S]) for i in range(4)]
        qin = [hz(f"qin{i}", 8 + 2 * i, [P, S]) for i in range(4)]
        kend = [hz(f"kend{i}", 16 + 2 * i, [P, S]) for i in range(4)]
        oG = kend
        kendT = [hz(f"kendT{i}", 24 + 2 * i, [P, ST, P]) for i in range(4)]
        att = [z(f"att{i}", 36 + 2 * i, [P, S]) for i in range(2)]
        state = [z(f"state{i}", 57 + 4 * i, [P, NCH, P]) for i in range(4)]
        lg = [z(f"lg{i}", 73 + 3 * i, [P, S + MEM]) for i in range(2)]
        la = [z(f"la{i}", 79 + 3 * i, [P, S + MEM]) for i in range(2)]
        ex = [z(f"ex{i}", 85 + 2 * i, [P, S]) for i in range(2)]
        kendc = [z(f"kendc{i}", 89 + i, [P, MEM]) for i in range(4)]
        last = z("last", 93, [P, 4, NCH])
        tot = z("tot", 93.25, [P, 4])
        kendcT = [z(f"kendcT{i}", at_, [P, 2, P]) for i, at_ in enumerate((33, 94, 95, 54))]
        zT = z("zT", 24, [EMB, S])
        fw = z("fw", 26, [HID, 3, HID])
        fvec = z("fvec", 26.75, [HID, 4])
        fout = z("fout", 27, [HID, 2 * D_HY])
        decay = z("decay", 73, [P, HT, S])
        fh = [z(f"fh{i}", 81 + 2 * i, [HID, S]) for i in range(2)]
        ft = [z(f"ft{i}", 85 + 2 * i, [HID, S]) for i in range(2)]
        hb = [z(f"hb{i}", 83 + 2 * i, [P, S]) for i in range(2)]
        nyq = z("nyq", 89, [1, S])
        ab = hz("ab", 0, [P, 2, HT, S])
        spec = hz("spec", 16, [P, 2 * HT, S])
        abH = z("abH", 57, [P, 2, HT, S], F32R)
        abL = z("abL", 40, [P, 2, HT, S], F32R)
        wk = z("wk", 24, [P, HT, S])
        x0c = z("x0c", 32, [P, HT, S])
        wtH = z("wtH", 8, [P, HT, S], F32R)
        wtL = z("wtL", 16, [P, HT, S], F32R)
        U = hz("U", 0, [P, 2 * HT, S])
        YH = z("YH", 57, [P, 2 * HT, S], F32R)
        YL = z("YL", 40, [P, 2 * HT, S], F32R)
        yt = z("yt", 16, [P, HT, S])
        yH = z("yH", 0, [P, DT, S], F32R)
        yL = z("yL", 73, [P, DT, S], F32R)
        mH = [z(f"mH{i}", 32 * i, [P, DT, S], F32R) for i in range(2)]
        mL = [z(f"mL{i}", 32 * i + 16, [P, DT, S], F32R) for i in range(2)]
        final = z("final", 64, [P, ST, D])

        ps = ctx.enter_context(nc.psum_tensor("ps", [P, 8, S], F32))

        def bank(i, n=S, m=P):
            return ps[0:m, i, 0:n]

        mod_dram = nc.dram_tensor("mod_rows_dram", (4, 6 * D), F32, kind="Internal")
        bias_dram = nc.dram_tensor("bias_ext", (B_HEADS, 768), F32, kind="Internal")

        def columns(w, k0=0, kt=DT, c0=0):
            v = w.rearrange("(k p) n -> p k n", p=P)[:, k0:k0 + kt, :]
            return lambda pos: v[:, :, bass.ds(pos.i * P + c0 * P, P)]

        def pairs(even, odd):
            return lambda pos: (odd if (pos.lo + pos.j) % 2 else even)[:, :, bass.ds(pos.pair * P, P)]

        w_in = t["w_in"][0]
        w_ada = t["w_ada_2"][0].rearrange("(k p) n -> p k n", p=P)
        w_ckv = t["w_ckv"][0]
        gu = t["w_gate_up"][0].rearrange("(k p) n -> p k n", p=P)
        up_a = t["w_up_a"][0].rearrange("(k p) n -> p k n", p=P)
        up_b = t["w_up_b"][0].rearrange("(k p) n -> p k n", p=P)
        w_in2 = t["w_in_2"][0]
        w_m1, w_m2 = t["w_mlp1_2"][0], t["w_mlp2_2"][0]
        gates_slab = w_in2.rearrange("(k p) n -> p k n", p=P)[:, :, N_IN_2 - 2 * RANK:N_IN_2]
        stages = [
            Stage("rope", 8, DT, columns(w_in)),
            Stage("va", 4, DT, columns(w_in, c0=8)),
            Stage("qkb", 8, DT, columns(w_in, c0=12)),
            Stage("vb", 4, DT, columns(w_in, c0=20)),
            Stage("gate", 16, DT, columns(w_in, c0=24)),
            Stage("ada", 48, DT, lambda pos: w_ada[:, 2 * (pos.j % 4):2 * (pos.j % 4) + 2,
                                                   bass.ds((pos.it * 3 + pos.j // 4) * S, S)], 12),
            Stage("up", 16, 4, pairs(up_a, up_b), 6),
            Stage("out", 8, DT, columns(t["w_out"][0])),
            Stage("mk", 8, DT, columns(w_ckv)),
            Stage("mv", 8, DT, columns(w_ckv, c0=8)),
            Stage("cq", 8, DT, columns(t["w_cq"][0])),
            Stage("co", 8, DT, columns(t["w_co"][0])),
            Stage("gu", 44, DT, pairs(gu[:, :, 0:D_FF], gu[:, :, D_FF:2 * D_FF]), 6),
            Stage("dn0", 8, 8, columns(t["w_down"][0], 0, 8)),
            Stage("dn1", 8, 7, columns(t["w_down"][0], 8, 7)),
            Stage("dn2", 8, 7, columns(t["w_down"][0], 15, 7)),
            Stage("hyp", 12, DT, columns(w_in2)),
            Stage("qp", 2, DT, columns(w_in2, c0=12)),
            Stage("kp", 2, DT, columns(w_in2, c0=14)),
            Stage("vp", 4, DT, columns(w_in2, c0=16)),
            Stage("ogp", 4, DT, columns(w_in2, c0=20)),
            Stage("grp", 1, DT, lambda pos: gates_slab),
            Stage("sa", 5, 4, columns(t["k_dft"], kt=4)),
            Stage("sb", 4, 4, columns(t["k_dft"], kt=4, c0=4)),
            Stage("uu", 8, 4, columns(t["k_dft"], kt=4)),
            Stage("inv", 4, 8, columns(t["k_inv"])),
            Stage("wo", 8, DT, columns(t["w_out_2"][0])),
        ] + [Stage(f"m1_{q}", 8, DT, columns(w_m1, c0=8 * q)) for q in (0, 1)] + [
            Stage("m2_0", 8, DT, columns(w_m2, 0)),
            Stage("m1_2", 8, DT, columns(w_m1, c0=16)),
            Stage("m2_1", 8, DT, columns(w_m2, 8)),
            Stage("m1_3", 8, DT, columns(w_m1, c0=24)),
            Stage("m2_2", 8, DT, columns(w_m2, 16)),
            Stage("m2_3", 8, DT, columns(w_m2, 24)),
        ]
        total = 0
        for s_ in stages:
            s_.base = total
            total += s_.n
        st = {s_.name: s_ for s_ in stages}
        all_units = [(s_, i) for s_ in stages for i in range(s_.n)]
        width = lambda s_: 2 * RANK if s_.name == "grp" else P

        slab_in = [sem(f"slab_in{i}") for i in range(SLOTS)]
        high_done = sem("high_done")
        low_done = sem("low_done")
        unit_done = sem("unit_done")
        bank_free = sem("bank_free")
        res = {n: sem("res_" + n) for n in
               ("rope", "up", "out", "co", "gu", "dn2", "wo", "m1", "m2_3")}
        tok_in, const_in, vec_in, lam_in, rope_in, rel_in = (
            sem(n) for n in ("tok_in", "const_in", "vec_in", "lam_in", "rope_in", "rel_in"))
        vec_t, vec_ok, x_t, x_sq, x_c, x_acc, stat_sum, stat_v, stat_r = (
            sem(n) for n in ("vec_t", "vec_ok", "x_t", "x_sq", "x_c", "x_acc", "stat_sum",
                             "stat_v", "stat_r"))
        silu_c, rel_ok, rel_out, rel_back, rel_mm, bias_ok = (
            sem(n) for n in ("silu_c", "rel_ok", "rel_out", "rel_back", "rel_mm", "bias_ok"))
        rot_done, roped, v_turned, v_kept, sig_done = (
            sem(n) for n in ("rot_done", "roped", "v_turned", "v_kept", "sig_done"))
        cond_ok, mod_in, mod_mm, lam_exp, lam_ok = (
            sem(n) for n in ("cond_ok", "mod_in", "mod_mm", "lam_exp", "lam_ok"))
        row_out = [sem(f"row_out{i}") for i in range(4)]
        scored, maxed, exped, normed, turned, kept, pv_done, pv_out = (
            {k: sem(f"{k}_{n}") for k in "abc"} for n in
            ("scored", "maxed", "exped", "normed", "turned", "kept", "pv_done", "pv_out"))
        head_sq, head_mm, head_v, head_r = (sem(n) for n in ("head_sq", "head_mm", "head_v", "head_r"))
        y_ok, silu_done, mem_in, own_v, own_a, mod_ok = (
            sem(n) for n in ("y_ok", "silu_done", "mem_in", "own_v", "own_a", "mod_ok"))
        ctx_in, gate_in, gla_in, filt_in = (sem(n) for n in ("ctx_in", "gate_in", "gla_in", "filt_in"))
        md_t, md_h, md_ok = (sem(n) for n in ("md_t", "md_h", "md_ok"))
        g_mm, g_y, g_ln, g_cum, g_ex, g_arg, g_ex2, g_qk, g_done = (
            sem("gla_" + n) for n in ("mm", "y", "ln", "cum", "ex", "arg", "ex2", "qk", "done"))
        kend_mm, kend_kept, state_mm, state_ok, fb_mm, att_ok, o_mm, o_sq = (
            sem(n) for n in ("kend_mm", "kend_kept", "state_mm", "state_ok", "fb_mm", "att_ok", "o_mm", "o_sq"))
        gh_mm, gh_v, gh_r, gh_y = (sem("gla_head_" + n) for n in ("mm", "v", "r", "y"))
        f_mm, f_arg, f_sin, f_out = (sem("filt_" + n) for n in ("mm", "arg", "sin", "out"))
        ab_done, ab_sq, ab_h, ab_l, nrm_mm, nrm_v, nrm_r = (
            sem(n) for n in ("ab_done", "ab_sq", "ab_h", "ab_l", "nrm_mm", "nrm_v", "nrm_r"))
        w_ok, wt_mm, wt_h, wt_l, y_t, y_h, y_l, yt_mm, y2_ok = (
            sem(n) for n in ("w_ok", "wt_mm", "wt_h", "wt_l", "y_t", "y_h", "y_l", "yt_mm", "y2_ok"))
        fin_h, fin_t, fin_c, fin_out = (sem(n) for n in ("fin_h", "fin_t", "fin_c", "fin_out"))
        STATS = ["x", "mem", "cross", "ctx", "ffn", "fin1", "mix2", "mlp2", "fin2"]
        stat_no = {n: i for i, n in enumerate(STATS)}

        def wide(a):
            return a[:].rearrange("p (a b) c -> p a (b c)", a=2)

        def vcol(name, i=0):
            c = VEC_AT[name]
            if isinstance(i, int):
                return vec[:, c + i:c + i + 1]
            return vec[:, c:c + 8][:, bass.ds(i, 1)]

        ATT = {"a": (A_HEADS * ST, 2, 3), "b": (B_HEADS * ST, 3, 4), "c": (X_HEADS * ST, 3, 4)}

        def keys_of(kind, qt):
            return 2 if kind == "c" else qt + 1

        block = ctx.enter_context(nc.Block())

        CONSTS_IN = 16 * 3 + 5

        @block.sync
        def _(sp):
            sp.dma_start(tok[:], t["x"][0].rearrange("(t p) d -> p t d", p=P)).then_inc(tok_in, 16)
            for k, dst in enumerate((ident, swap, anti)):
                sp.dma_start(dst[:], t["k_square"][k]).then_inc(const_in, 16)

            def stream(stage, lo=0, hi=None):
                def load(pos):
                    if not isinstance(pos.u, int) or pos.u >= SLOTS:
                        sp.wait_ge(low_done, pos.u - (SLOTS - 1))
                    dst = wide(raw[pos.slot]) if stage.name == "ada" else raw[pos.slot][:, 0:stage.kt, 0:width(stage)]
                    sp.dma_start(dst, stage.source(pos)).then_inc(slab_in[pos.slot], 16)
                each_unit(sp, stage, load, lo, hi)

            for name in ("rope", "va", "qkb", "vb", "gate"):
                stream(st[name])
            sp.wait_ge(const_in, CONSTS_IN)
            for d, name in enumerate(("gk_w_fwd_2", "gk_w_bwd_2")):
                sp.dma_start(gate_w[d * RANK:(d + 1) * RANK, d, :], t[name][0]).then_inc(gate_in, 16)
            stream(st["ada"])
            stream(st["up"], 0, 3)
            sp.wait_ge(pv_out["b"], B_HEADS // 2)
            sp.dma_start(memtok[:], t["mem"][0].rearrange("(t p) d -> p t d", p=P)).then_inc(mem_in, 16)
            stream(st["up"], 3)
            for name in ("out", "mk", "mv", "cq"):
                stream(st[name])
            sp.wait_ge(bank_free, st["cq"].base)
            sp.dma_start(ctxtok[:], t["ctx_2"][0].rearrange("(t p) d -> p t d", p=P)).then_inc(ctx_in, 16)
            for name in ("co", "gu", "dn0", "dn1", "dn2"):
                stream(st[name])
            stream(st["hyp"])
            sp.wait_ge(unit_done, st["hyp"].base)
            sp.dma_start(masks[:], t["k_square"][3:5].rearrange("k p c -> p k c")).then_inc(gla_in, 16)
            sp.dma_start(reset[:], t["k_reset"]).then_inc(gla_in, 16)
            for name in ("qp", "kp", "vp", "ogp", "grp"):
                stream(st[name])
            stream(st["sa"], 0, 3)
            sp.wait_ge(g_done, 4)
            sp.dma_start(zT[:], t["k_z"]).then_inc(filt_in, 16)
            sp.dma_start(fw[0:EMB, 0, :], t["filt_w1_2"][0]).then_inc(filt_in, 16)
            sp.dma_start(fw[:, 1, :], t["filt_w2_2"][0]).then_inc(filt_in, 16)
            sp.dma_start(fw[:, 2, :], t["filt_w3_2"][0]).then_inc(filt_in, 16)
            sp.dma_start(fout[:], t["filt_wout_2"][0]).then_inc(filt_in, 16)
            for k, name in enumerate(("filt_b1_2", "filt_b2_2", "filt_b3_2", "filt_freq_2")):
                sp.dma_start(fvec[:, k:k + 1], t[name].rearrange("a p -> p a")).then_inc(filt_in, 16)
            sp.dma_start(decay[:], t["k_decay"].rearrange("(t p) c -> p t c", p=P)).then_inc(filt_in, 16)
            stream(st["sa"], 3)
            for name in ("sb", "uu", "inv", "wo", "m1_0", "m1_1", "m2_0", "m1_2", "m2_1", "m1_3", "m2_2", "m2_3"):
                stream(st[name])
            for k in range(2):
                c = slice(k * D // 2, (k + 1) * D // 2)
                sp.wait_ge(fin_c, (k + 1) * DT // 2)
                sp.dma_start(out[0].rearrange("(t p) d -> p t d", p=P)[:, :, c], final[:, :, c]).then_inc(fin_out, 16)
            sp.wait_ge(fin_out, 32)

        @block.gpsimd
        def _(pool):
            pool.memset(ones[:], 1.0).then_inc(const_in, 1)
            pool.memset(gate_w[:], 0.0).then_inc(const_in, 1)
            pool.memset(mask_row[0:1, 0:CHUNK], NEG).then_inc(const_in, 1)
            pool.memset(mask_row[0:1, CHUNK:P], 0.0).then_inc(const_in, 1)
            pool.memset(mask_row[0:1, P:P + CHUNK], 1.0).then_inc(const_in, 1)
            pool.wait_ge(rel_ok, 1)
            pool.dma_start(bias_dram[:, :], rel_ext[:]).then_inc(rel_out, 16)
            pool.wait_ge(rel_out, 16)
            pool.dma_start(hankel[:], bass.AP(bias_dram, MAX_REL - P + 1, [[1, P], [768, B_HEADS], [1, S]])).then_inc(rel_back, 16)

            def low(stage):
                n = width(stage)

                def one(pos):
                    pool.wait_ge(high_done, pos.u + 1)
                    pool.tensor_tensor(WL[pos.slot][:, 0:stage.kt, 0:n], raw[pos.slot][:, 0:stage.kt, 0:n],
                                       WH[pos.slot][:, 0:stage.kt, 0:n].bitcast(F32),
                                       ALU.subtract).then_inc(low_done, 1)
                each_unit(pool, stage, one)
            for stage in stages:
                low(stage)


        @block.scalar
        def _(act):
            own = Own(act, own_a)
            for name, n in VEC_ROWS:
                c = VEC_AT[name]
                side, c = (0, c) if c < VEC_SPLIT else (1, c - VEC_SPLIT)
                src = t[name]
                while len(src.shape) > 1:
                    src = src.rearrange("a b -> (a b)") if len(src.shape) == 2 else src.rearrange("a b c -> (a b c)")
                act.dma_start(vecload[c:c + n, side, :], src.rearrange("(n p) -> n p", p=P)).then_inc(vec_in, 16)
            act.dma_start(rel_ext[:, 0:REL], t["rel_bias"][0]).then_inc(rel_in, 16)
            act.dma_start(rope[:], t["k_rope"].rearrange("a p s -> p a s")).then_inc(rope_in, 16)
            for k, name in enumerate(("lam_q1", "lam_k1", "lam_q2", "lam_k2")):
                act.dma_start(lam_parts[:, k, :], t[name][0].partition_broadcast(P)).then_inc(lam_in, 16)

            def high(s_, slot, turn, result=None, value=None):
                act.wait_ge(slab_in[slot], turn * 16 + 16)
                if value is not None:
                    act.wait_ge(result or unit_done, value)
                n = width(s_)
                act.activation(WH[slot][:, 0:s_.kt, 0:n], raw[slot][:, 0:s_.kt, 0:n],
                               ACT.Copy).then_inc(high_done, 1)

            def follow(stage, after=None, result=None, lo=0):
                def inner(pos):
                    high(stage, pos.slot, pos.turn + 1, result, pos.u + 1)
                    if after:
                        after(pos)
                inside = max(lo, stage.n - SLOTS)
                if inside > lo and stage.n > SLOTS:
                    each_unit(act, stage, inner, lo, inside)
                for i in range(max(inside, lo), stage.n):
                    pos = Pos(stage, i // stage.unroll, i % stage.unroll, 0)
                    high_at(stage.base + i + SLOTS, result)
                    if after:
                        after(pos)

            def high_at(u, result=None):
                if u < len(all_units):
                    high(all_units[u][0], u % SLOTS, u // SLOTS, result, u - SLOTS + 1)

            def prep(tiles, n0, keep):
                n = tiles * P
                for k in range(DT):
                    act.wait_ge(x_t, n0 + k + 1)
                    if k >= 2:
                        act.wait_ge(x_acc, n0 + k - 1)
                    dst = keep[:, k, :] if keep is not None else tmp[k % 2][:, 0:n]
                    act.activation(dst, bank(3 + k % 2, n), ACT.Copy).then_inc(x_c, 1)
                    act.wait_ge(x_c, n0 + k + 1)
                    act.activation(tmp[2 + k % 2][:, 0:n], dst, ACT.Square).then_inc(x_sq, 1)

            def stat(name, dst, n=S):
                act.wait_ge(stat_v, stat_no[name] + 1)
                act.activation(dst[:, 0:n], tmp[3][:, 0:n], ACT.Sqrt).then_inc(stat_r, 1)

            def finish(stat_name):
                stat(stat_name, r)
                for k in range(DT):
                    act.wait_ge(fin_t, k + 1)
                    act.activation(final[:, :, k * P:(k + 1) * P],
                                   bank(3 + k % 2).rearrange("p (t c) -> p t c", c=P), ACT.Copy).then_inc(fin_c, 1)

            for u in range(SLOTS):
                high(st["rope"], u, 0)
            prep(ST, 0, x)
            act.wait_ge(vec_ok, 1)
            act.activation(cS[:, :, 0], vec[:, VEC_AT["c_2"]:VEC_AT["c_2"] + DT], ACT.Silu).then_inc(silu_c, 1)
            act.activation(cS[:, :, 1], vec[:, VEC_AT["c_ctx_2"]:VEC_AT["c_ctx_2"] + DT], ACT.Silu).then_inc(silu_c, 1)
            act.wait_ge(lam_ok, 2)
            act.activation(lam_s[:, 2:4], lam_s[:, 0:2], ACT.Exp).then_inc(lam_exp, 1)
            stat("x", r)
            follow(st["rope"])

            def keep_v(dst, n0, which, tt=ST):
                def one(i):
                    act.wait_ge(v_turned, n0 + i + 1)
                    act.activation(dst[:, 0:tt, i * P:(i + 1) * P],
                                   bank(5 + (n0 + i) % 2, tt * P).rearrange("p (t c) -> p t c", c=P),
                                   ACT.Copy).then_inc(v_kept, 1)
                return one

            def values(stage, dst, n0, tt=ST):
                one = keep_v(dst, n0, stage, tt)
                for i in range(stage.n):
                    high_at(stage.base + i + SLOTS)
                    if i >= 1:
                        one(i - 1)
                one(stage.n - 1)

            values(st["va"], vA, 0)
            follow(st["qkb"])
            values(st["vb"], vB, 4)

            def sigmoid(pos):
                act.activation(gates[:, bass.ds(pos.i, 1), :], tmp[pos.slot][:], ACT.Sigmoid).then_inc(sig_done, 1)
            follow(st["gate"], sigmoid, bank_free)

            def ada_step(i):
                high_at(st["ada"].base + i + SLOTS)
                if i % 4 == 3:
                    b = i // 4
                    if b >= 4:
                        act.wait_ge(row_out[b % 4], 16 * (b // 4))
                    act.activation(rows[b % 4][:], bank(1, S, 4), ACT.Copy).then_inc(bank_free, 4)
                    act.wait_ge(bank_free, st["ada"].base + 4 * b + 4)
                    act.dma_start(mod_dram[:, b * S:(b + 1) * S], rows[b % 4][:]).then_inc(row_out[b % 4], 16)

            def attend(kind):
                items, lag, ahead = ATT[kind]
                comps = 2 if kind == "a" else 1
                for s_ in range(items + lag):
                    if s_ < items:
                        n, qt = s_, s_ % ST
                        nk = keys_of(kind, qt) * P
                        act.wait_ge(maxed[kind], n + 1)
                        for c in range(comps):
                            j = 2 * (n % 2) + c
                            if kind == "a":
                                src, dst = bank(3 + j, nk), pA[n % 2][:, c, 0:nk]
                                if n >= 2:
                                    act.wait_ge(turned["a"], n - 1)
                                scale = A_DK ** -0.5
                            elif kind == "b":
                                src, dst, scale = pB[n % 4][:, 0:nk], pB[n % 4][:, 0:nk], 1.0
                            else:
                                src, dst, scale = bank(3 + n % 4, nk), pC[n % 4][:, 0:nk], 1.0 / 16
                                if n >= 4:
                                    act.wait_ge(turned["c"], n - 3)
                            k = 2 * (n % 4) + c
                            ins = act.activation(dst, src, ACT.Exp, bias=tiny[:, k:k + 1], scale=scale,
                                                 accum_out=tiny[:, 8 + k:9 + k])
                        ins.then_inc(exped[kind], 1)
                    m = s_ - lag
                    if m >= 0:
                        h, qt = m // ST, m % ST
                        kn = keys_of(kind, qt)
                        act.wait_ge(turned[kind], m + 1)
                        if h >= 2:
                            act.wait_ge(pv_done[kind], h - 1)
                        dst = (pcT if kind == "c" else attT)[h % 2]
                        act.activation(dst[:, 0:kn, qt * P:(qt + 1) * P],
                                       bank((7, 2)[m % 2], kn * P).rearrange("p (t c) -> p t c", c=P),
                                       ACT.Copy).then_inc(kept[kind], 1)
                    if kind != "c" and s_ < items:
                        ada_step(s_ + (0 if kind == "a" else A_HEADS * ST))
            attend("a")
            attend("b")
            for i in range(4):
                act.wait_ge(row_out[i], 16 * 3)
            act.dma_start(mod_rows[:], mod_dram[:, :].rearrange("c (m p) -> m c p", p=P)).then_inc(mod_in, 16)
            for h in range(A_HEADS):
                act.wait_ge(head_v, h + 1)
                act.activation(tmp[h][:], tmp[h][:], ACT.Sqrt).then_inc(head_r, 1)
            act.wait_ge(y_ok, 2)
            prep(2, 8, None)
            stat("mem", rm, MEM)
            follow(st["up"])
            follow(st["out"])
            stat("cross", r)
            follow(st["mk"])
            values(st["mv"], vc, 8, 2)
            follow(st["cq"])
            attend("c")
            prep(2, 16, ctxT)
            stat("ctx", rc, MEM)
            follow(st["co"])
            stat("ffn", r)

            def silu(pos):
                if (pos.lo + pos.j) % 2 == 0:
                    act.wait_ge(bank_free, pos.u + 1)
                    act.activation(tmp[pos.slot][:], tmp[pos.slot][:], ACT.Silu).then_inc(silu_done, 1)
            follow(st["gu"], silu)
            for name in ("dn0", "dn1", "dn2"):
                follow(st[name])
            act.wait_ge(stat_v, stat_no["fin1"] + 1)
            act.activation(r[:], tmp[2][:], ACT.Sqrt).then_inc(stat_r, 1)
            stat("mix2", r2)

            def modulate(n0, n, shift, dh):
                for k in range(DT):
                    act.wait_ge(md_t, n0 + k + 1)
                    act.activation(dh[:, k, :], tmp[k % 3][:, 0:n], ACT.Identity, bias=shift(k)).then_inc(md_h, 1)
            modulate(0, S, lambda k: mod[:, k, 0:1], hH)
            modulate(8, MEM, lambda k: mod[:, k, 1:2], cH)
            for name in ("hyp", "qp", "kp"):
                follow(st[name])

            def keep_gla_v(i):
                act.wait_ge(v_turned, 16 + i + 1)
                c = slice(i * P, (i + 1) * P)
                act.activation(vG[:, :, c], bank(6).rearrange("p (t c) -> p t c", c=P), ACT.Copy)
                act.activation(vGc[:, :, c], bank(7, MEM).rearrange("p (t c) -> p t c", c=P), ACT.Copy).then_inc(v_kept, 1)
            for i in range(4):
                high_at(st["vp"].base + i + SLOTS)
                if i >= 1:
                    keep_gla_v(i - 1)
            keep_gla_v(3)

            def silu_og(pos):
                own.mark(act.activation(og[:, pos.i, :], og[:, pos.i, :], ACT.Silu))
            follow(st["ogp"], silu_og, bank_free)
            follow(st["grp"])

            def soft(g):
                a, b = la[g % 2], lg[g % 2]
                act.wait_ge(g_y, g + 1)
                own.step(act.activation(a[:], b[:], ACT.Abs))
                own.step(act.activation(a[:], a[:], ACT.Exp, scale=-1.0))
                act.activation(a[:], a[:], ACT.Ln, bias=ones[:, 0:1]).then_inc(g_ln, 1)

            def exps(g):
                a, b, fwd = la[g % 2], lg[g % 2], g < 2
                act.wait_ge(g_cum, g + 1)
                if g >= 1:
                    act.wait_ge(g_qk, g)
                act.activation(ex[0][:], a[:, 0:S], ACT.Exp, scale=LOG_SCALE)
                act.activation(ex[1][:], a[:, 0:S], ACT.Exp, scale=-LOG_SCALE).then_inc(g_ex, 1)
                if fwd:
                    act.activation(kendc[g][:], a[:, S:S + MEM], ACT.Exp, scale=-LOG_SCALE, bias=tot[:, g:g + 1])
                else:
                    act.activation(kendc[g][:], a[:, S:S + MEM], ACT.Exp, scale=LOG_SCALE)
                edge = CHUNK - 1 if fwd else 0
                act.activation(last[:, g, :], a[:, 0:S].rearrange("p (n c) -> p n c", c=CHUNK)[:, :, edge],
                               ACT.Exp, scale=LOG_SCALE)
                act.wait_ge(g_arg, g + 1)
                act.activation(b[:, 0:S], b[:, 0:S], ACT.Exp, scale=LOG_SCALE).then_inc(g_ex2, 1)

            def keep_kend(g):
                act.wait_ge(kend_mm, g + 1)
                act.activation(kendT[g][:], bank(7).rearrange("p (t c) -> p t c", c=P), ACT.Copy)
                act.activation(kendcT[g][:], bank(0, MEM).rearrange("p (t c) -> p t c", c=P), ACT.Copy).then_inc(kend_kept, 1)
            soft(0)
            soft(1)
            exps(0)
            soft(2)
            exps(1)
            keep_kend(0)
            soft(3)
            exps(2)
            keep_kend(1)
            exps(3)
            keep_kend(2)
            keep_kend(3)
            for s_ in range(1, G_HEADS + 2):
                h = s_ - 1
                if h < G_HEADS:
                    act.wait_ge(o_mm, h + 1)
                    own.step(act.activation(oG[h][:], bank(h % 2), ACT.Copy))
                    if h >= 2:
                        act.wait_ge(gh_y, h - 1)
                    act.activation(tmp[2 + h % 2][:], oG[h][:], ACT.Square).then_inc(o_sq, 1)
                h = s_ - 2
                if 0 <= h:
                    act.wait_ge(gh_v, h + 1)
                    act.activation(tmp[2 + h % 2][:], tmp[2 + h % 2][:], ACT.Sqrt).then_inc(gh_r, 1)

            for i in range(3):
                act.wait_ge(f_arg, i + 1)
                act.activation(fh[i % 2][:], ft[0][:], ACT.Sin).then_inc(f_sin, 1)
            for tt in range(HT):
                act.wait_ge(ab_done, tt + 1)
                act.activation(tmp[tt][:], ab[:, 0, tt, :], ACT.Square)
                act.activation(decay[:, tt, :], ab[:, 1, tt, :], ACT.Square).then_inc(ab_sq, 1)
                for j in range(2):
                    ins = act.activation(abH[:, j, tt, :], ab[:, j, tt, :], ACT.Copy)
                ins.then_inc(ab_h, 1)
            act.wait_ge(nrm_v, 1)
            act.activation(nrm[:], nrm[:], ACT.Sqrt).then_inc(nrm_r, 1)
            follow(st["sa"])
            follow(st["sb"])
            for tt in range(HT):
                act.wait_ge(wt_mm, tt + 1)
                act.activation(wtH[:, tt, :], bank(3 + tt), ACT.Copy).then_inc(wt_h, 1)
            for i in range(8):
                high_at(st["uu"].base + i + SLOTS)
                if i >= 4:
                    k = i - 4
                    act.wait_ge(y_t, k + 1)
                    act.activation(YH[:, k, :], tmp[2 * (k % 2)][:], ACT.Copy)
                    act.activation(YH[:, HT + k, :], tmp[2 * (k % 2) + 1][:], ACT.Copy).then_inc(y_h, 1)
            follow(st["inv"])
            follow(st["wo"])
            stat("mlp2", r)
            modulate(16, S, lambda k: mod[:, 24 + k, 0:1], hH)
            for name in ("m1_0", "m1_1", "m2_0", "m1_2", "m2_1", "m1_3", "m2_2", "m2_3"):
                follow(st[name])
            finish("fin2")

        @block.tensor
        def _(pe):
            pe.wait_ge(const_in, CONSTS_IN)
            pe.wait_ge(vec_in, 16 * len(VEC_ROWS))
            pe.transpose(ps[:, 3, 0:VEC_SPLIT], vecload[0:VEC_SPLIT, 0, :], ident[0:VEC_SPLIT, 0:VEC_SPLIT])
            n = VECS - VEC_SPLIT
            pe.transpose(ps[:, 4, 0:n], vecload[0:n, 1, :], ident[0:n, 0:n]).then_inc(vec_t, 1)

            def prep(src, tiles, n0):
                for k in range(DT):
                    if n0 == 0 and k == 0:
                        pe.wait_ge(vec_ok, 1)
                    if k >= 2:
                        pe.wait_ge(x_c, n0 + k - 1)
                    for i in range(tiles):
                        ins = pe.transpose(ps[:, 3 + k % 2, i * P:(i + 1) * P], src[:, i, k * P:(k + 1) * P], ident[:])
                    ins.then_inc(x_t, 1)

            def stat(name, ready, value, n=S):
                pe.wait_ge(ready, value)
                pe.matmul(bank(7, n), ones[:], acc[:, 0:n], start=True, stop=True).then_inc(stat_sum, 1)

            def unit(pos, stage, rh, rl, n=S, m=P, extra=None):
                pe.wait_ge(low_done, pos.u + 1)
                if not isinstance(pos.u, int) or pos.u >= SLOTS:
                    pe.wait_ge(bank_free, pos.u - (SLOTS - 1))
                for dst, rh_, rl_, n_ in [(bank(pos.slot, n, m), rh, rl, n)] + ([extra(pos)] if extra else []):
                    k = 0
                    for w, a in ((WH, rh_), (WH, rl_), (WL, rh_)):
                        for q in range(stage.kt):
                            ins = pe.matmul(dst, w[pos.slot][:, q, 0:m], a[:, q, :], start=(k == 0),
                                            stop=(k == 3 * stage.kt - 1))
                            k += 1
                ins.then_inc(unit_done, 1)

            def opening(name, rh, rl, order, ready, group):
                stage = st[name]
                first = [Pos(stage, 0, j, 0) for j in range(group)]
                pe.wait_ge(low_done, stage.base + group)
                pe.wait_ge(bank_free, stage.base - SLOTS + group)
                for c, (value, q) in enumerate(order):
                    if value:
                        pe.wait_ge(ready, value)
                    for pos in first:
                        for e, (w, a) in enumerate(((WH, rh), (WH, rl), (WL, rh))):
                            ins = pe.matmul(bank(pos.slot), w[pos.slot][:, q, :], a[:, q, :],
                                            start=(c == 0 and e == 0), stop=(c == stage.kt - 1 and e == 2))
                        if c == stage.kt - 1:
                            ins.then_inc(unit_done, 1)

            def after_opening(name, rh, rl, order, ready, group=1):
                opening(name, rh, rl, order, ready, group)
                units(name, rh, rl, S, group)

            def tiles(n0=0, n=DT):
                return [(n0 + k + 1, k) for k in range(n)]

            def units(name, rh, rl, n=S, lo=0, hi=None):
                stage = st[name]
                each_unit(pe, stage, lambda pos: unit(pos, stage, rh, rl, n), lo, hi)

            def finish(stat_name):
                for k in range(DT):
                    pe.wait_ge(fin_h, k + 1)
                    if k >= 2:
                        pe.wait_ge(fin_c, k - 1)
                    for i in range(ST):
                        ins = pe.transpose(ps[:, 3 + k % 2, i * P:(i + 1) * P], tmp[k % 2][:, i * P:(i + 1) * P], ident[:])
                    ins.then_inc(fin_t, 1)

            pe.wait_ge(tok_in, 16)
            prep(tok, ST, 0)
            stat("x", x_acc, DT)
            pe.wait_ge(rel_back, 16)
            for h in range(B_HEADS):
                if h >= 2:
                    pe.wait_ge(bias_ok, h - 1)
                for b in range(ST):
                    d = ST - 1 - b
                    ins = pe.matmul(ps[:, 5 + h % 2, b * P:(b + 1) * P], hankel[:, h, d * P:(d + 1) * P],
                                    anti[:], start=(b == 0), stop=True, skip_group_check=True)
                ins.then_inc(rel_mm, 1)
            stage = st["rope"]
            for i in range(stage.n + 1):
                if i < stage.n:
                    unit(Pos(stage, 0, i, 0), stage, hH, hL)
                if i >= 1:
                    pe.wait_ge(bank_free, stage.base + i)
                    if i >= 3:
                        pe.wait_ge(roped, i - 2)
                    pe.matmul(bank(3 + (i - 1) % 2), swap[:], tmp[(i - 1) % 2][:], start=True, stop=True).then_inc(rot_done, 1)

            def turn_v(n0, i, tt=ST, src=None):
                pe.wait_ge(bank_free, n0[0] + i + 1)
                c = n0[1] + i
                if c >= 2:
                    pe.wait_ge(v_kept, c - 1)
                for q in range(tt):
                    ins = pe.transpose(ps[:, 5 + c % 2, q * P:(q + 1) * P], tmp[i % 2][:, q * P:(q + 1) * P], ident[:])
                ins.then_inc(v_turned, 1)

            def values(name, rh, rl, c0, n=S):
                stage = st[name]
                for i in range(stage.n + 1):
                    if i < stage.n:
                        unit(Pos(stage, 0, i, 0), stage, rh, rl, n)
                    if i >= 1:
                        turn_v((stage.base, c0), i - 1, n // P)

            values("va", hH, hL, 0)
            units("qkb", hH, hL)
            values("vb", hH, hL, 4)
            units("gate", hH, hL)

            def ada(i):
                u = st["ada"].base + i
                pe.wait_ge(low_done, u + 1)
                if i % 4 == 0 and i:
                    pe.wait_ge(bank_free, u)
                for q in range(2):
                    for w in (WH, WL):
                        k = 2 * (i % 4) + q
                        ins = pe.matmul(bank(1, S, 4), cR[:, k, :], wide(w[u % SLOTS])[:, q, :],
                                        start=(k == 0 and w is WH), stop=(k == DT - 1 and w is WL))
                ins.then_inc(unit_done, 1)

            def attend(kind):
                items, lag, _ahead = ATT[kind]
                for s_ in range(items + lag + 1):
                    if s_ < items:
                        n, h, qt = s_, s_ // ST, s_ % ST
                        nk = keys_of(kind, qt) * P
                        q = slice(qt * P, (qt + 1) * P)
                        if kind == "a":
                            if n >= 2:
                                pe.wait_ge(exped["a"], n - 1)
                            for c in range(2):
                                rows = slice(64 * c, 64 * c + 64)
                                dst = ps[:, 3 + 2 * (n % 2) + c, 0:nk]
                                pe.matmul(dst, qA[rows, h, q], kA[rows, h, 0:nk], start=True, stop=True)
                                ins = pe.matmul(dst[:, nk - CHUNK:nk], mask_row[0:1, 0:P], mask_row[0:1, P:P + CHUNK],
                                                start=False, stop=True, skip_group_check=True)
                        elif kind == "b":
                            if n >= 4:
                                pe.wait_ge(maxed["b"], n - 3)
                            rows = slice(64 * (h % 2), 64 * (h % 2) + 64)
                            ins = pe.matmul(bank(3 + n % 4, nk), qB[rows, h // 2, q], kB[rows, h // 2, 0:nk],
                                            start=True, stop=True)
                        else:
                            if n >= 4:
                                pe.wait_ge(exped["c"], n - 3)
                            for j in range(2):
                                ins = pe.matmul(bank(3 + n % 4, nk), qc[:, 2 * h + j, q], kc[:, 2 * h + j, :],
                                                start=(j == 0), stop=(j == 1))
                        ins.then_inc(scored[kind], 1)
                        if kind != "c":
                            ada(s_ + (0 if kind == "a" else A_HEADS * ST))
                    m = s_ - lag
                    if 0 <= m < items:
                        pe.wait_ge(normed[kind], m + 1)
                        if m >= 2:
                            pe.wait_ge(kept[kind], m - 1)
                        src = {"a": lambda c: pA[m % 2][:, 0, c], "b": lambda c: pB[m % 4][:, c],
                               "c": lambda c: pC[m % 4][:, c]}[kind]
                        for b in range(keys_of(kind, m % ST)):
                            ins = pe.transpose(ps[:, (7, 2)[m % 2], b * P:(b + 1) * P], src(slice(b * P, (b + 1) * P)), ident[:])
                        ins.then_inc(turned[kind], 1)
                    if m >= 1 and m % ST == 0:
                        h = m // ST - 1
                        pe.wait_ge(kept[kind], ST * (h + 1))
                        if kind == "c":
                            if h >= 1:
                                pe.wait_ge(pv_out["c"], 2 * h)
                            for j in range(2):
                                c = slice((2 * h + j) * P, (2 * h + j + 1) * P)
                                for b in range(2):
                                    ins = pe.matmul(bank(j), vc[:, b, c], pcT[h % 2][:, b, :], start=(b == 0), stop=(b == 1))
                        else:
                            if kind == "a":
                                if h >= 1:
                                    pe.wait_ge(pv_out["a"], h)
                                v, c, rows = vA, slice(h * P, (h + 1) * P), slice(0, P)
                            else:
                                if h >= 2 and h % 2 == 0:
                                    pe.wait_ge(pv_out["b"], h // 2)
                                v, c, rows = vB, slice(h * B_DH, (h + 1) * B_DH), slice(64 * (h % 2), 64 * (h % 2) + 64)
                            for b in range(ST):
                                ins = pe.matmul(ps[rows, 0, b * P:S], v[:, b, c], attT[h % 2][:, b, b * P:S],
                                                start=(b == 0), stop=True, skip_group_check=True)
                        ins.then_inc(pv_done[kind], 1)

            pe.wait_ge(bank_free, st["ada"].base)
            pe.wait_ge(roped, 8)
            pe.wait_ge(v_kept, 8)
            pe.wait_ge(bias_ok, B_HEADS)
            pe.wait_ge(cond_ok, 1)
            attend("a")
            pe.wait_ge(pv_out["a"], A_HEADS)
            attend("b")
            for h in range(A_HEADS):
                pe.wait_ge(head_sq, h + 1)
                pe.matmul(bank(3 + h), ones[:], tmp[h][:], start=True, stop=True).then_inc(head_mm, 1)
            pe.wait_ge(mem_in, 16)
            pe.wait_ge(head_v, A_HEADS)
            prep(memtok, 2, 8)
            stat("mem", x_acc, 2 * DT, MEM)
            pe.wait_ge(y_ok, 2)
            stage = st["up"]
            each_unit(pe, stage, lambda pos: unit(pos, stage, *(
                (hH[:, 4:8], hL[:, 4:8]) if (pos.lo + pos.j) % 2 else (hH[:, 0:4], hL[:, 0:4]))))
            pe.wait_ge(mod_in, 16)
            for c in range(4):
                ins = pe.transpose(ps[:, 3, c * 48:(c + 1) * 48], mod_rows[:, c, :], ident[0:48, 0:48])
            ins.then_inc(mod_mm, 1)
            after_opening("out", mgH, mgL, tiles(), res["up"])
            units("mk", memH, memL, MEM, 0, 3)
            stat("cross", res["out"], DT)
            units("mk", memH, memL, MEM, 3)
            values("mv", memH, memL, 8, MEM)
            units("cq", hH, hL)
            pe.wait_ge(bank_free, st["co"].base)
            pe.wait_ge(v_kept, 16)
            attend("c")
            pe.wait_ge(ctx_in, 16)
            prep(ctxtok, 2, 16)
            stat("ctx", x_acc, 3 * DT, MEM)
            after_opening("co", oH, oL, tiles(), pv_out["c"])
            opening("gu", hH, hL, tiles(), res["co"], 1)
            stat("ffn", res["co"], DT)
            units("gu", hH, hL, S, 1)
            pe.wait_ge(res["gu"], 15)
            units("dn0", fH[:, 0:8], fL[:, 0:8])
            units("dn1", fH[:, 8:15], fL[:, 8:15])
            pe.wait_ge(res["gu"], FT)
            units("dn2", fH[:, 15:22], fL[:, 15:22])
            stat("fin1", res["dn2"], DT)
            pe.matmul(bank(6), ones[:], acc2[:], start=True, stop=True).then_inc(stat_sum, 1)
            after_opening("hyp", hH, hL, tiles(), md_ok, 2)
            units("qp", hH, hL)
            pe.wait_ge(md_ok, 2 * DT)

            def with_context(name):
                stage = st[name]
                return lambda pos: unit(pos, stage, hH, hL, S, width(stage),
                                        lambda pos: (bank(3 + pos.slot, MEM, width(stage)), cH, cL, MEM))
            each_unit(pe, st["kp"], with_context("kp"))
            stage = st["vp"]
            one = with_context("vp")
            for i in range(stage.n + 1):
                if i < stage.n:
                    one(Pos(stage, 0, i, 0))
                if i >= 1:
                    c = i - 1
                    pe.wait_ge(bank_free, stage.base + c + 1)
                    pe.wait_ge(v_kept, 16 + c)
                    for q in range(ST):
                        pe.transpose(ps[:, 6, q * P:(q + 1) * P], vfT[c % 2][:, q * P:(q + 1) * P], ident[:])
                    for q in range(2):
                        ins = pe.transpose(ps[:, 7, q * P:(q + 1) * P], vfTc[c % 2][:, q * P:(q + 1) * P], ident[:])
                    ins.then_inc(v_turned, 1)
            units("ogp", hH, hL)
            each_unit(pe, st["grp"], with_context("grp"))

            pe.wait_ge(bank_free, st["sa"].base)
            pe.wait_ge(v_kept, 20)
            pe.wait_ge(gate_in, 32)
            for g in range(4):
                if g >= 2:
                    pe.wait_ge(g_y, g - 1)
                w = gate_w[:, g // 2, (g % 2) * P:(g % 2 + 1) * P]
                pe.matmul(bank(3 + 2 * (g % 2)), w, gr[:, 0:S], start=True, stop=True)
                pe.matmul(bank(4 + 2 * (g % 2), MEM), w, gr[:, S:S + MEM], start=True, stop=True).then_inc(g_mm, 1)
            for g in range(4):
                pe.wait_ge(g_done, g + 1)
                if g >= 1:
                    pe.wait_ge(kend_kept, g)
                for q in range(ST):
                    pe.transpose(ps[:, 7, q * P:(q + 1) * P], kend[g][:, q * P:(q + 1) * P], ident[:])
                for q in range(2):
                    ins = pe.transpose(ps[:, 0, q * P:(q + 1) * P], kendc[g][:, q * P:(q + 1) * P], ident[:])
                ins.then_inc(kend_mm, 1)
            pe.wait_ge(g_y, 4)
            for g in range(4):
                pe.wait_ge(kend_kept, g + 1)
                if g >= 2:
                    pe.wait_ge(state_ok, g - 1)
                for half in range(2):
                    h = 2 * (g % 2) + half
                    rows = slice(64 * half, 64 * half + 64)
                    dv = slice(h * P, (h + 1) * P)
                    for b in range(2):
                        pe.matmul(ps[rows, 1 + g % 2, 0:P], kendcT[g][:, b, rows], vGc[:, b, dv],
                                  start=(b == 0), stop=(b == 1), skip_group_check=True)
                    for n in range(NCH):
                        tok_rows = slice(64 * (n % 2), 64 * (n % 2) + 64)
                        c = n // 2
                        ins = pe.matmul(ps[rows, 3 + 2 * (g % 2) + n % 2, c * P:(c + 1) * P],
                                        kendT[g][tok_rows, n // 2, rows], vG[tok_rows, n // 2, dv],
                                        start=True, stop=True, skip_group_check=True)
                ins.then_inc(state_mm, 1)
            pe.wait_ge(state_ok, 4)
            for s_ in range(G_HEADS + 2):
                if s_ < G_HEADS:
                    h = s_
                    rows = slice(64 * (h % 2), 64 * (h % 2) + 64)
                    if h >= 2:
                        pe.wait_ge(att_ok, h - 1)
                    for d in range(2):
                        g = 2 * d + h // 2
                        for b in range(ST):
                            c = slice(b * P, (b + 1) * P)
                            ins = pe.matmul(ps[:, 3 + 2 * (h % 2) + d, c], kin[g][rows, c], qin[g][rows, c],
                                            start=True, stop=True, skip_group_check=True)
                    ins.then_inc(fb_mm, 1)
                h = s_ - 1
                if 0 <= h < G_HEADS:
                    rows = slice(64 * (h % 2), 64 * (h % 2) + 64)
                    pe.wait_ge(att_ok, h + 1)
                    if h >= 2:
                        pe.wait_ge(o_sq, h - 1)
                    for b in range(ST):
                        pe.matmul(ps[:, h % 2, b * P:(b + 1) * P], vG[:, b, h * P:(h + 1) * P],
                                  att[h % 2][:, b * P:(b + 1) * P], start=True, stop=True, skip_group_check=True)
                        for n in (2 * b, 2 * b + 1):
                            c = slice(n * CHUNK, (n + 1) * CHUNK)
                            for d in range(2):
                                g = 2 * d + h // 2
                                ins = pe.matmul(ps[:, h % 2, c], state[g][rows, n, :], qin[g][rows, c],
                                                start=False, stop=True, skip_group_check=True)
                    ins.then_inc(o_mm, 1)
                h = s_ - 2
                if 0 <= h < G_HEADS:
                    pe.wait_ge(o_sq, h + 1)
                    if h >= 1:
                        pe.wait_ge(gh_v, h)
                    pe.matmul(bank(7), ones[:], tmp[2 + h % 2][:], start=True, stop=True).then_inc(gh_mm, 1)

            pe.wait_ge(filt_in, 16 * 10)
            pe.matmul(bank(3, S, HID), fw[0:EMB, 0, :], zT[:], start=True, stop=True).then_inc(f_mm, 1)
            for i in (1, 2):
                pe.wait_ge(f_sin, i)
                pe.matmul(bank(3, S, HID), fw[:, i, :], fh[(i - 1) % 2][:], start=True, stop=True).then_inc(f_mm, 1)
            pe.wait_ge(f_sin, 3)
            for tt in range(HT):
                if tt >= 2:
                    pe.wait_ge(ab_done, tt - 1)
                for j in range(2):
                    ins = pe.matmul(bank(3 + 2 * (tt % 2) + j), fh[0][:, tt * P:(tt + 1) * P],
                                    fout[:, j * D_HY:(j + 1) * D_HY], start=True, stop=True)
                ins.then_inc(f_out, 1)
            pe.wait_ge(gh_v, G_HEADS)
            pe.wait_ge(ab_sq, HT)
            for c in range(HT):
                for tt in range(HT):
                    for j in range(2):
                        src = (tmp[tt][:] if j == 0 else decay[:, tt, :])[:, c * P:(c + 1) * P]
                        ins = pe.matmul(ps[:, 7, c:c + 1], src, ones[:, 0:1], start=(tt == 0 and j == 0),
                                        stop=(tt == HT - 1 and j == 1), skip_group_check=True)
            ins.then_inc(nrm_mm, 1)
            pe.wait_ge(ab_l, HT)
            units("sa", abH[:, 0], abL[:, 0])
            units("sb", abH[:, 1], abL[:, 1])
            pe.wait_ge(w_ok, HT)
            for tt in range(HT):
                for i in range(HT):
                    ins = pe.transpose(ps[:, 3 + tt, i * P:(i + 1) * P], wk[:, i, tt * P:(tt + 1) * P], ident[:])
                ins.then_inc(wt_mm, 1)
            pe.wait_ge(wt_l, HT)
            units("uu", wtH, wtL)
            after_opening("inv", YH, YL, [(k + 1 if not j else 0, HT * j + k) for k in range(HT) for j in range(2)], y_l, 2)
            pe.wait_ge(bank_free, st["wo"].base)
            for c in range(HT):
                for tt in range(HT):
                    ins = pe.transpose(ps[:, 3 + c, tt * P:(tt + 1) * P], yt[:, tt, c * P:(c + 1) * P], ident[:])
                ins.then_inc(yt_mm, 1)
            after_opening("wo", yH, yL, [(k + 1, (k + HT) % DT) for k in range(DT)], y2_ok, 2)
            stat("mlp2", res["wo"], DT)
            for name, q in (("m1_0", 0), ("m1_1", 1), ("m2_0", 0), ("m1_2", 2), ("m2_1", 1), ("m1_3", 3),
                            ("m2_2", 2), ("m2_3", 3)):
                if name == "m1_0":
                    after_opening(name, hH, hL, tiles(2 * DT), md_ok, 2)
                elif name[1] == "1":
                    units(name, hH, hL)
                else:
                    after_opening(name, mH[q % 2], mL[q % 2], tiles(DT * q), res["m1"])
            stat("fin2", res["m2_3"], DT)
            finish("fin2")

        @block.vector
        def _(dve):
            own = Own(dve, own_v)

            def taken(u):
                dve.wait_ge(bank_free, u + 1)

            def stat(name, n=S):
                dve.wait_ge(stat_sum, stat_no[name] + 1)
                own.step(dve.tensor_scalar(tmp[3][:, 0:n], bank(7, n), 1.0 / D, EPS, ALU.mult, ALU.add))
                dve.reciprocal(tmp[3][:, 0:n], tmp[3][:, 0:n]).then_inc(stat_v, 1)

            def split(src, dh, dl):
                own.step(dve.tensor_scalar(dh, src, 1.0, None, ALU.mult))
                return dve.tensor_tensor(dl, src, dh.bitcast(F32), ALU.subtract)

            def prep(tiles, n0, kept_, g, dh, dl):
                n = tiles * P
                own.step(dve.memset(acc[:], 0.0))
                for k in range(DT):
                    dve.wait_ge(x_sq, n0 + k + 1)
                    if g is not None:
                        src = kept_[:, k, :] if kept_ is not None else tmp[k % 2][:, 0:n]
                        own.step(dve.tensor_scalar(tmp[k % 2][:, 0:n], src, vcol(g, k), None, ALU.mult))
                        own.step(split(tmp[k % 2][:, 0:n], dh[:, k, :], dl[:, k, :]))
                    dve.tensor_tensor(acc[:, 0:n], acc[:, 0:n], tmp[2 + k % 2][:, 0:n], ALU.add).then_inc(x_acc, 1)
                    dve.wait_ge(x_acc, n0 + k + 1)

            def finish(stat_name, g):
                stat(stat_name)
                dve.wait_ge(stat_r, stat_no[stat_name] + 1)
                for k in range(DT):
                    if k >= 2:
                        dve.wait_ge(fin_t, k - 1)
                    dve.scalar_tensor_tensor(tmp[k % 2][:], x[:, k, :], vcol(g, k), r[:], ALU.mult, ALU.mult).then_inc(fin_h, 1)

            dve.wait_ge(rel_in, 16)
            dve.tensor_copy(rel_ext[:, REL:768], rel_ext[:, REL - 1:REL].to_broadcast([B_HEADS, 768 - REL])).then_inc(rel_ok, 1)
            dve.wait_ge(vec_t, 1)
            own.step(dve.tensor_copy(vec[:, 0:VEC_SPLIT], ps[:, 3, 0:VEC_SPLIT]))
            own.step(dve.tensor_copy(vec[:, VEC_SPLIT:VECS], ps[:, 4, 0:VECS - VEC_SPLIT]))
            dve.tensor_scalar(vcol("subln_g"), vcol("subln_g"), 1.0 - LAM_INIT, None, ALU.mult).then_inc(vec_ok, 1)
            dve.wait_ge(vec_ok, 1)
            dve.wait_ge(lam_in, 64)
            for c in range(2):
                own.step(dve.tensor_tensor(lam_parts[:, 2 * c, :], lam_parts[:, 2 * c, :], lam_parts[:, 2 * c + 1, :], ALU.mult))
                dve.reduce_sum(lam_s[:, c:c + 1], lam_parts[:, 2 * c, :], AX.X).then_inc(lam_ok, 1)
            prep(ST, 0, x, "norm_mix_g", hH, hL)
            dve.wait_ge(lam_exp, 1)
            own.step(dve.tensor_tensor(lam_s[:, 6:7], lam_s[:, 3:4], lam_s[:, 2:3], ALU.subtract))
            own.step(dve.tensor_scalar(lam_s[:, 7:8], lam_s[:, 6:7], -LAM_INIT, None, ALU.add))
            stat("x")
            for h in range(B_HEADS):
                dve.wait_ge(rel_mm, h + 1)
                ins = dve.tensor_scalar(bias_t[:, h, :], bank(5 + h % 2), float(B_DH) ** 0.5, None, ALU.mult)
                if h < B_HEADS - 1:
                    ins.then_inc(bias_ok, 1)
            own.step(ins)
            dve.memset(bias_t[0:CHUNK, :, S - CHUNK:S], NEG * float(B_DH) ** 0.5).then_inc(bias_ok, 1)
            dve.wait_ge(stat_r, 1)
            dve.wait_ge(rope_in, 16)
            stage = st["rope"]
            for i in range(stage.n + 1):
                if i < stage.n:
                    u = stage.base + i
                    dve.wait_ge(unit_done, u + 1)
                    dve.tensor_tensor(tmp[i % 2][:], bank(u % SLOTS), r[:], ALU.mult).then_inc(bank_free, 1)
                    taken(u)
                if i >= 1:
                    k = i - 1
                    dve.wait_ge(rot_done, k + 1)
                    own.mark(dve.tensor_tensor(tmp[2][:], bank(3 + k % 2), rope[:, 1, :], ALU.mult))
                    own.step(dve.tensor_tensor(tmp[3][:], tmp[k % 2][:], rope[:, 0, :], ALU.mult))
                    dve.tensor_tensor((qA if k < 4 else kA)[:, k % 4, :], tmp[2][:], tmp[3][:], ALU.add).then_inc(roped, 1)
                    dve.wait_ge(roped, k + 1)

            def times_r(stage, dst, rr=r, n=S, buffers=None):
                def one(pos):
                    dve.wait_ge(unit_done, pos.u + 1)
                    if buffers:
                        buffers(pos)
                    dve.tensor_tensor(dst(pos), bank(pos.slot, n), rr[:, 0:n], ALU.mult).then_inc(bank_free, 1)
                return one

            def values(name, c0, rr=r, n=S):
                stage = st[name]
                for i in range(stage.n):
                    u = stage.base + i
                    dve.wait_ge(unit_done, u + 1)
                    if i >= 2:
                        dve.wait_ge(v_turned, c0 + i - 1)
                    dve.tensor_tensor(tmp[i % 2][:, 0:n], bank(u % SLOTS, n), rr[:, 0:n], ALU.mult).then_inc(bank_free, 1)
                dve.wait_ge(v_turned, c0 + stage.n)

            dve.wait_ge(silu_c, 2)
            own.step(dve.tensor_scalar(cR[:, :, 0:2], cS[:], 1.0, None, ALU.mult))
            dve.tensor_tensor(cR[:, :, 2:4], cS[:], cR[:, :, 0:2].bitcast(F32), ALU.subtract).then_inc(cond_ok, 1)
            values("va", 0)
            for half, dst in ((0, qB), (4, kB)):
                for i in range(4):
                    u = st["qkb"].base + half + i
                    dve.wait_ge(unit_done, u + 1)
                    dve.tensor_tensor(dst[:, i, :], bank(u % SLOTS), r[:], ALU.mult).then_inc(bank_free, 1)
            values("vb", 4)

            stage = st["gate"]

            def gate_buffer(pos):
                if not isinstance(pos.i, int) or pos.i >= SLOTS:
                    dve.wait_ge(sig_done, pos.i - (SLOTS - 1))
            each_unit(dve, stage, times_r(stage, lambda pos: tmp[pos.slot][:], buffers=gate_buffer), 0, 3)
            each_unit(dve, stage, times_r(stage, lambda pos: tmp[pos.slot][:], buffers=gate_buffer), 3)

            def attend(kind):
                items, lag, _ahead = ATT[kind]
                for s_ in range(items + 1 + (lag + ST + 3)):
                    if s_ < items:
                        n, h, qt = s_, s_ // ST, s_ % ST
                        nk = keys_of(kind, qt) * P
                        k = 2 * (n % 4)
                        dve.wait_ge(scored[kind], n + 1)
                        if kind == "a":
                            own.step(dve.tensor_reduce(tiny[:, k:k + 2], ps[:, 3 + 2 * (n % 2):5 + 2 * (n % 2), 0:nk], AX.X, ALU.max))
                            dve.tensor_scalar(tiny[:, k:k + 2], tiny[:, k:k + 2], -(A_DK ** -0.5), None, ALU.mult).then_inc(maxed[kind], 1)
                        elif kind == "b":
                            if n >= 4:
                                dve.wait_ge(turned["b"], n - 3)
                            own.step(dve.tensor_tensor_reduce(
                                out=pB[n % 4][:, 0:nk], in0=bank(3 + n % 4, nk), in1=bias_t[:, h, S - nk:S],
                                scale=float(B_DH) ** -0.5, scalar=-3.0e38, op0=ALU.add, op1=ALU.max,
                                accum_out=tiny[:, k:k + 1]))
                            dve.tensor_scalar(tiny[:, k:k + 1], tiny[:, k:k + 1], -1.0, None, ALU.mult).then_inc(maxed[kind], 1)
                        else:
                            own.step(dve.tensor_reduce(tiny[:, k:k + 1], bank(3 + n % 4, nk), AX.X, ALU.max))
                            dve.tensor_scalar(tiny[:, k:k + 1], tiny[:, k:k + 1], -1.0 / 16, None, ALU.mult).then_inc(maxed[kind], 1)
                    n = s_ - 1
                    if 0 <= n < items:
                        nk = keys_of(kind, n % ST) * P
                        k = 2 * (n % 4)
                        dve.wait_ge(exped[kind], n + 1)
                        if kind == "a":
                            own.step(dve.reciprocal(tiny[:, 8 + k:10 + k], tiny[:, 8 + k:10 + k]))
                            own.step(dve.tensor_scalar(pA[n % 2][:, 1, 0:nk], pA[n % 2][:, 1, 0:nk], tiny[:, 9 + k:10 + k],
                                                       lam_s[:, 7:8], ALU.mult, ALU.mult))
                            dve.scalar_tensor_tensor(pA[n % 2][:, 0, 0:nk], pA[n % 2][:, 0, 0:nk], tiny[:, 8 + k:9 + k],
                                                     pA[n % 2][:, 1, 0:nk], ALU.mult, ALU.add).then_inc(normed[kind], 1)
                        else:
                            own.step(dve.reciprocal(tiny[:, 8 + k:9 + k], tiny[:, 8 + k:9 + k]))
                            p = (pB if kind == "b" else pC)[n % 4][:, 0:nk]
                            dve.tensor_scalar(p, p, tiny[:, 8 + k:9 + k], None, ALU.mult).then_inc(normed[kind], 1)
                    m = s_ - lag - 2
                    if m >= 1 and m % ST == 0 and m // ST <= items // ST:
                        h = m // ST - 1
                        if kind == "a":
                            dve.wait_ge(pv_done["a"], h + 1)
                            dve.tensor_copy(qA[:, h, :], bank(0)).then_inc(pv_out["a"], 1)
                        elif kind == "b" and h % 2 == 1:
                            dve.wait_ge(pv_done["b"], h + 1)
                            dve.tensor_copy(qB[:, h // 2, :], bank(0)).then_inc(pv_out["b"], 1)
                        elif kind == "c":
                            dve.wait_ge(pv_done["c"], h + 1)
                            for j in range(2):
                                own.step(dve.tensor_copy(tmp[j][:], bank(j)))
                                own.step(dve.tensor_scalar(oH[:, 2 * h + j, :], tmp[j][:], 1.0, None, ALU.mult))
                                dve.tensor_tensor(oL[:, 2 * h + j, :], tmp[j][:], oH[:, 2 * h + j, :].bitcast(F32),
                                                  ALU.subtract).then_inc(pv_out["c"], 1)
            attend("a")
            attend("b")
            dve.wait_ge(pv_out["a"], A_HEADS)
            for h in range(A_HEADS):
                dve.tensor_tensor(tmp[h][:], qA[:, h, :], qA[:, h, :], ALU.mult).then_inc(head_sq, 1)
            dve.wait_ge(pv_out["b"], B_HEADS // 2)
            for k in range(4):
                ins = split(qB[:, k, :], hH[:, 4 + k, :], hL[:, 4 + k, :])
            ins.then_inc(y_ok, 1)
            for h in range(A_HEADS):
                dve.wait_ge(head_mm, h + 1)
                own.step(dve.tensor_scalar(tmp[h][:], bank(3 + h), 1.0 / P, EPS, ALU.mult, ALU.add))
                dve.reciprocal(tmp[h][:], tmp[h][:]).then_inc(head_v, 1)
            for h in range(A_HEADS):
                dve.wait_ge(head_r, h + 1)
                own.step(dve.scalar_tensor_tensor(qA[:, h, :], qA[:, h, :], vcol("subln_g"), tmp[h][:], ALU.mult, ALU.mult))
                ins = split(qA[:, h, :], hH[:, h, :], hL[:, h, :])
            ins.then_inc(y_ok, 1)
            dve.wait_ge(y_ok, 2)
            prep(2, 8, None, "norm_mem_g", memH, memL)
            stat("mem", MEM)
            dve.wait_ge(stat_r, 2)

            stage = st["up"]
            n0 = own.n

            def merge(pos):
                dve.wait_ge(unit_done, pos.u + 1)
                if (pos.lo + pos.j) % 2 == 0:
                    dve.tensor_tensor(tmp[pos.slot][:], bank(pos.slot), gates[:, 0:DT][:, bass.ds(pos.pair, 1), :][:, 0],
                                      ALU.mult).then_inc(bank_free, 1)
                else:
                    own.group(n0, pos.pair, 2)
                    dve.tensor_tensor(tmp[3][:], bank(pos.slot), gates[:, DT:2 * DT][:, bass.ds(pos.pair, 1), :][:, 0],
                                      ALU.mult).then_inc(bank_free, 1)
                    taken(pos.u)
                    own.step(dve.tensor_tensor(tmp[3][:], tmp[3][:], tmp[(pos.slot - 1) % SLOTS][:], ALU.add))
                    h_, l_ = (y_[:, bass.ds(pos.pair, 1), :][:, 0] for y_ in (mgH, mgL))
                    split(tmp[3][:], h_, l_).then_inc(res["up"], 1)
                    dve.wait_ge(res["up"], pos.pair + 1)
            each_unit(dve, stage, merge)
            own.leave(n0 + 2 * DT)

            def residual(stage, scale=None, g=None, squares=True, done=None, second=None):
                per = (4 if g else 4 if second else 1) if squares else 0
                if squares:
                    own.step(dve.memset(acc[:], 0.0))
                n0 = own.n

                def one(pos):
                    own.group(n0, pos.i, per)
                    xm = x[:, bass.ds(pos.i, 1), :][:, 0]
                    dve.wait_ge(unit_done, pos.u + 1)
                    if scale is None:
                        dve.tensor_tensor(xm, bank(pos.slot), xm, ALU.add).then_inc(bank_free, 1)
                    else:
                        dve.scalar_tensor_tensor(xm, bank(pos.slot), scale(pos.i), xm, ALU.mult, ALU.add).then_inc(bank_free, 1)
                    taken(pos.u)
                    if not squares:
                        return
                    own.mark(dve.tensor_tensor(tmp[0][:], xm, xm, ALU.mult))
                    if second:
                        own.step(dve.tensor_scalar(tmp[1][:], xm, vcol(second, pos.i), None, ALU.mult))
                        own.step(dve.tensor_tensor(tmp[1][:], tmp[1][:], tmp[1][:], ALU.mult))
                        own.mark(dve.tensor_tensor(acc2[:], acc2[:], tmp[1][:], ALU.add))
                    if g is None:
                        own.settle()
                        dve.tensor_tensor(acc[:], acc[:], tmp[0][:], ALU.add).then_inc(res[done], 1)
                        dve.wait_ge(res[done], pos.i + 1)
                        return
                    own.step(dve.tensor_scalar(tmp[1][:], xm, vcol(g, pos.i), None, ALU.mult))
                    own.mark(dve.tensor_tensor(acc[:], acc[:], tmp[0][:], ALU.add))
                    h_, l_ = (y_[:, bass.ds(pos.i, 1), :][:, 0] for y_ in (hH, hL))
                    split(tmp[1][:], h_, l_).then_inc(res[done], 1)
                    dve.wait_ge(res[done], pos.i + 1)
                each_unit(dve, stage, one)
                own.leave(n0 + per * stage.n)

            dve.wait_ge(mod_mm, 1)
            for c in range(2):
                own.step(dve.tensor_tensor(mod[:, :, c], ps[:, 3, c * 48:(c + 1) * 48],
                                           vec[:, VEC_AT["b_ada_2"]:VEC_AT["b_ada_2"] + 48], ALU.add))
                ins = dve.tensor_tensor(mod[:, :, c], ps[:, 3, (2 + c) * 48:(3 + c) * 48], mod[:, :, c], ALU.add)
                if c == 0:
                    own.step(ins)
            ins.then_inc(mod_ok, 1)
            residual(st["out"], g="norm_cross_g", done="out")
            dve.wait_ge(stat_r, 2)
            stage = st["mk"]
            one = times_r(stage, lambda pos: kc[:, bass.ds(pos.i, 1), :][:, 0], rm, MEM)
            each_unit(dve, stage, one, 0, 3)
            stat("cross")
            each_unit(dve, stage, one, 3)
            values("mv", 8, rm, MEM)
            dve.wait_ge(stat_r, 3)
            stage = st["cq"]
            each_unit(dve, stage, times_r(stage, lambda pos: qc[:, bass.ds(pos.i, 1), :][:, 0]))
            attend("c")
            prep(2, 16, ctxT, None, None, None)
            stat("ctx", MEM)
            for c, (name, m, col) in enumerate((("norm_mix_2", 8, 0), ("norm_mix_2", 8, 1), ("norm_mlp_2", 32, 0))):
                own.mark(dve.scalar_tensor_tensor(gain[:, c, :], mod[:, m:m + DT, col], 1.0,
                                                  vec[:, VEC_AT[name]:VEC_AT[name] + DT], ALU.add, ALU.mult))
            own.settle()
            c = VEC_AT["norm_final_g"]
            own.step(dve.tensor_tensor(gain[:, 3, :], gain[:, 0, :], vec[:, c:c + DT], ALU.mult))
            dve.wait_ge(stat_r, stat_no["ctx"] + 1)
            residual(st["co"], g="norm_ffn_g", done="co")
            stat("ffn")
            dve.wait_ge(stat_r, stat_no["ffn"] + 1)
            n0 = own.n

            def swiglu(pos):
                dve.wait_ge(unit_done, pos.u + 1)
                if (pos.lo + pos.j) % 2 == 0:
                    dve.tensor_tensor(tmp[pos.slot][:], bank(pos.slot), r[:], ALU.mult).then_inc(bank_free, 1)
                else:
                    own.group(n0, pos.pair, 2)
                    dve.tensor_tensor(tmp[3][:], bank(pos.slot), r[:], ALU.mult).then_inc(bank_free, 1)
                    taken(pos.u)
                    dve.wait_ge(silu_done, pos.pair + 1)
                    own.step(dve.tensor_tensor(tmp[3][:], tmp[3][:], tmp[(pos.slot - 1) % SLOTS][:], ALU.mult))
                    h_, l_ = (y_[:, bass.ds(pos.pair, 1), :][:, 0] for y_ in (fH, fL))
                    split(tmp[3][:], h_, l_).then_inc(res["gu"], 1)
                    dve.wait_ge(res["gu"], pos.pair + 1)
            each_unit(dve, st["gu"], swiglu)
            own.leave(n0 + 2 * FT)
            residual(st["dn0"], squares=False)
            residual(st["dn1"], squares=False)
            own.step(dve.memset(acc2[:], 0.0))
            residual(st["dn2"], done="dn2", second="norm_final_g")
            dve.wait_ge(stat_sum, stat_no["mix2"] + 1)
            own.step(dve.tensor_scalar(tmp[2][:], bank(7), 1.0 / D, EPS, ALU.mult, ALU.add))
            dve.reciprocal(tmp[2][:], tmp[2][:]).then_inc(stat_v, 1)
            dve.wait_ge(stat_v, stat_no["fin1"] + 1)
            own.step(dve.scalar_tensor_tensor(tmp[3][:], bank(6), 1.0 / D, tmp[2][:], ALU.mult, ALU.mult))
            own.step(dve.tensor_scalar(tmp[3][:], tmp[3][:], EPS, None, ALU.add))
            dve.reciprocal(tmp[3][:], tmp[3][:]).then_inc(stat_v, 1)
            dve.wait_ge(stat_r, stat_no["mix2"] + 1)
            own.step(dve.tensor_tensor(acc[:], r[:], r2[:], ALU.mult))

            def modulate(n0, src, rr, n, which, shift, dh, dl):
                for k in range(DT + 1):
                    if k < DT:
                        if n0 + k >= 3:
                            dve.wait_ge(md_ok, n0 + k - 2)
                        dve.scalar_tensor_tensor(tmp[k % 3][:, 0:n], src[:, k, :], gain[:, which, k:k + 1], rr[:, 0:n],
                                                 ALU.mult, ALU.mult).then_inc(md_t, 1)
                    if k >= 1:
                        q = k - 1
                        dve.wait_ge(md_h, n0 + k)
                        dve.scalar_tensor_tensor(dl[:, q, :], tmp[q % 3][:, 0:n], shift(q), dh[:, q, :].bitcast(F32),
                                                 ALU.add, ALU.subtract).then_inc(md_ok, 1)
                dve.wait_ge(md_ok, n0 + DT)
            modulate(0, x, acc, S, 3, lambda k: mod[:, k, 0:1], hH, hL)
            for k in range(DT):
                own.mark(dve.scalar_tensor_tensor(x[:, k, :], x[:, k, :], vcol("norm_final_g", k), r[:], ALU.mult, ALU.mult))
            modulate(8, ctxT, rc, MEM, 1, lambda k: mod[:, k, 1:2], cH, cL)

            def copies(name, dst, scale=1.0, also=None):
                def one(pos):
                    dve.wait_ge(unit_done, pos.u + 1)
                    ins = dve.tensor_scalar(dst(pos), bank(pos.slot, S, width(st[name])), scale, None, ALU.mult)
                    if also:
                        ins = dve.tensor_scalar(also(pos), bank(3 + pos.slot, MEM, width(st[name])), scale, None, ALU.mult)
                    ins.then_inc(bank_free, 1)
                each_unit(dve, st[name], one)
            copies("hyp", lambda pos: hy[:, bass.ds(pos.i, 1), :][:, 0])
            copies("qp", lambda pos: qG[:, pos.i, :], 64 ** -0.5)
            copies("kp", lambda pos: kG[:, pos.i, :], 1.0, lambda pos: kGc[:, pos.i, :])
            stage = st["vp"]
            for i in range(stage.n):
                u = stage.base + i
                dve.wait_ge(unit_done, u + 1)
                if i >= 2:
                    dve.wait_ge(v_turned, 16 + i - 1)
                dve.tensor_copy(vfT[i % 2][:], bank(u % SLOTS))
                dve.tensor_copy(vfTc[i % 2][:], bank(3 + u % SLOTS, MEM)).then_inc(bank_free, 1)
            copies("ogp", lambda pos: og[:, pos.i, :])
            copies("grp", lambda pos: gr[:, 0:S], 1.0, lambda pos: gr[:, S:S + MEM])

            dve.wait_ge(gla_in, 32)

            def gate_in_(g):
                dve.wait_ge(g_mm, g + 1)
                b0 = 3 + 2 * (g % 2)
                bias = vcol("gk_b_fwd_2" if g < 2 else "gk_b_bwd_2", g % 2)
                dve.tensor_scalar(lg[g % 2][:], ps[:, b0:b0 + 2, :].rearrange("p a b -> p (a b)")[:, 0:S + MEM],
                                  bias, None, ALU.add).then_inc(g_y, 1)

            def sums(g):
                a, b, i = la[g % 2], lg[g % 2], g % 2
                dve.wait_ge(g_ln, g + 1)
                own.step(dve.scalar_tensor_tensor(b[:], b[:], 0.0, a[:], ALU.min, ALU.subtract))
                if g < 2:
                    own.mark(dve.tensor_tensor_scan(a[:, 0:S], reset[:], b[:, 0:S], 0.0, ALU.mult, ALU.add))
                else:
                    own.mark(dve.tensor_tensor_scan(a[:, 0:S][:, ::-1], reset[:], b[:, 0:S][:, ::-1], 0.0, ALU.mult, ALU.add))
                own.step(dve.tensor_tensor_scan(a[:, S:S + MEM], ones[:, 0:1].to_broadcast([P, MEM]), b[:, S:S + MEM],
                                                0.0, ALU.mult, ALU.add))
                if g < 2:
                    dve.tensor_scalar(tot[:, g:g + 1], a[:, S + MEM - 1:S + MEM], LOG_SCALE, None, ALU.mult).then_inc(g_cum, 1)
                else:
                    dve.tensor_tensor(a[:, S:S + MEM], a[:, S:S + MEM], b[:, S:S + MEM], ALU.subtract).then_inc(g_cum, 1)
                edge = CHUNK - 1 if g < 2 else 0
                ac = a[:, 0:S].rearrange("p (n c) -> p n c", c=CHUNK)
                dve.tensor_tensor(b[:, 0:S].rearrange("p (n c) -> p n c", c=CHUNK),
                                  ac[:, :, edge:edge + 1].to_broadcast([P, NCH, CHUNK]), ac, ALU.subtract).then_inc(g_arg, 1)

            def gated(g):
                i = g % 2
                dve.wait_ge(g_ex, g + 1)
                dve.tensor_tensor(qin[g][:], qG[:, i, :], ex[0][:], ALU.mult)
                dve.tensor_tensor(kin[g][:], kG[:, i, :], ex[1][:], ALU.mult).then_inc(g_qk, 1)
                dve.wait_ge(g_ex2, g + 1)
                dve.tensor_tensor(kendc[g][:], kGc[:, i, :], kendc[g][:], ALU.mult)
                dve.tensor_tensor(kend[g][:], kG[:, i, :], lg[g % 2][:, 0:S], ALU.mult).then_inc(g_done, 1)
                dve.wait_ge(g_done, g + 1)
            gate_in_(0)
            gate_in_(1)
            sums(0)
            gated(0)
            gate_in_(2)
            sums(1)
            gated(1)
            gate_in_(3)
            sums(2)
            gated(2)
            sums(3)
            gated(3)
            for g in range(4):
                dve.wait_ge(state_mm, g + 1)
                order = range(NCH) if g < 2 else range(NCH - 1, -1, -1)
                own.step(dve.tensor_copy(state[g][:, order[0], :], ps[:, 1 + g % 2, 0:P]))
                for n, nxt in zip(order, order[1:]):
                    ins = dve.scalar_tensor_tensor(state[g][:, nxt, :], state[g][:, n, :], last[:, g, n:n + 1],
                                                   ps[:, 3 + 2 * (g % 2) + n % 2, (n // 2) * P:(n // 2 + 1) * P],
                                                   ALU.mult, ALU.add)
                    if nxt != order[-1]:
                        own.step(ins)
                ins.then_inc(state_ok, 1)
            for s_ in range(G_HEADS + 3):
                h = s_
                if h < G_HEADS:
                    dve.wait_ge(fb_mm, h + 1)
                    if h >= 2:
                        dve.wait_ge(o_mm, h - 1)
                    if h >= 1:
                        dve.wait_ge(att_ok, h)
                    for d in range(2):
                        ins = dve.tensor_tensor(tmp[d][:].rearrange("p (b c) -> p b c", c=P),
                                                bank(3 + 2 * (h % 2) + d).rearrange("p (b c) -> p b c", c=P),
                                                masks[:, d:d + 1, :].to_broadcast([P, ST, P]), ALU.mult)
                    own.step(ins)
                    dve.tensor_tensor(att[h % 2][:], tmp[0][:], tmp[1][:], ALU.add).then_inc(att_ok, 1)
                h = s_ - 2
                if 0 <= h < G_HEADS:
                    dve.wait_ge(gh_mm, h + 1)
                    own.step(dve.tensor_scalar(tmp[2 + h % 2][:], bank(7), 1.0 / P, EPS, ALU.mult, ALU.add))
                    dve.reciprocal(tmp[2 + h % 2][:], tmp[2 + h % 2][:]).then_inc(gh_v, 1)
                    dve.wait_ge(gh_r, h + 1)
                    own.step(dve.scalar_tensor_tensor(oG[h][:], oG[h][:], vcol("gla_norm_2"), tmp[2 + h % 2][:], ALU.mult, ALU.mult))
                    dve.tensor_tensor(og[:, h, :], og[:, h, :], oG[h][:], ALU.mult).then_inc(gh_y, 1)

            for i in range(3):
                dve.wait_ge(f_mm, i + 1)
                own.step(dve.tensor_scalar(ft[0][:], bank(3, S, HID), fvec[:, i:i + 1], fvec[:, 3:4], ALU.add, ALU.mult))
                own.step(dve.tensor_scalar(ft[1][:], ft[0][:], 1.0 / (2 * np.pi), ROUND, ALU.mult, ALU.add))
                own.step(dve.tensor_scalar(ft[1][:], ft[1][:], -ROUND, None, ALU.add))
                own.step(dve.scalar_tensor_tensor(ft[0][:], ft[1][:], -TWO_PI_HI, ft[0][:], ALU.mult, ALU.add))
                own.step(dve.scalar_tensor_tensor(ft[0][:], ft[1][:], -TWO_PI_LO, ft[0][:], ALU.mult, ALU.add))
                dve.tensor_scalar(ft[0][:], ft[0][:], PI_SAFE, -PI_SAFE, ALU.min, ALU.max).then_inc(f_arg, 1)
            for tt in range(HT):
                dve.wait_ge(f_out, tt + 1)
                for j in range(2):
                    own.mark(dve.tensor_tensor(hb[j][:], bank(3 + 2 * (tt % 2) + j), decay[:, tt, :], ALU.mult))
                own.settle()
                if tt == 0:
                    own.step(dve.memset(hb[1][0:1, :], 0.0))
                dve.tensor_tensor(ab[:, 0, tt, :], hb[0][:], hb[1][:], ALU.add)
                dve.tensor_tensor(ab[:, 1, tt, :], hb[0][:], hb[1][:], ALU.subtract).then_inc(ab_done, 1)
                dve.wait_ge(ab_done, tt + 1)
            for tt in range(HT):
                dve.wait_ge(ab_h, tt + 1)
                for j in range(2):
                    ins = dve.tensor_tensor(abL[:, j, tt, :], ab[:, j, tt, :], abH[:, j, tt, :].bitcast(F32), ALU.subtract)
                ins.then_inc(ab_l, 1)
            dve.wait_ge(nrm_mm, 1)
            own.step(dve.tensor_scalar(nrm[:], ps[:, 7, 0:HT], 0.5, EPS, ALU.mult, ALU.add))
            dve.reciprocal(nrm[:], nrm[:]).then_inc(nrm_v, 1)

            def conv(tile, dst):
                src = hy[:, tile, :]
                d3, s3 = (a.rearrange("p (r c) -> p r c", c=CHUNK) for a in (dst, src))
                w = [vcol("conv_w_2", 12 * j + tile) for j in range(3)]
                own.step(dve.tensor_scalar(dst, src, w[1], vcol("conv_b_2", tile), ALU.mult, ALU.add))
                own.step(dve.scalar_tensor_tensor(d3[:, :, 1:CHUNK], s3[:, :, 0:CHUNK - 1], w[0], d3[:, :, 1:CHUNK], ALU.mult, ALU.add))
                own.step(dve.scalar_tensor_tensor(d3[:, :, 0:CHUNK - 1], s3[:, :, 1:CHUNK], w[2], d3[:, :, 0:CHUNK - 1], ALU.mult, ALU.add))

            def conv_pair(i):
                conv(4 + i, tmp[0][:])
                conv(8 + i, tmp[1][:])
                dve.tensor_tensor(wk[:, i, :], tmp[0][:], tmp[1][:], ALU.mult).then_inc(w_ok, 1)
                dve.wait_ge(w_ok, i + 1)

            def take(u, dst, m=P):
                dve.wait_ge(unit_done, u + 1)
                dve.tensor_copy(dst, bank(u % SLOTS, S, m)).then_inc(bank_free, 1)
            base = st["sa"].base
            for i in range(9):
                take(base + i, nyq[:] if i == 4 else spec[:, i - (i > 4), :], 1 if i == 4 else P)
                if i % 2 == 0 and i < 8:
                    conv_pair(i // 2)
            taken(base + 5)
            own.step(dve.memset(spec[0:1, HT, :], 0.0))
            for tt in range(HT):
                dve.wait_ge(wt_h, tt + 1)
                dve.tensor_tensor(wtL[:, tt, :], bank(3 + tt), wtH[:, tt, :].bitcast(F32), ALU.subtract).then_inc(wt_l, 1)

            def low_y(k):
                dve.wait_ge(y_h, k + 1)
                for j in range(2):
                    ins = dve.tensor_tensor(YL[:, HT * j + k, :], tmp[2 * (k % 2) + j][:], YH[:, HT * j + k, :].bitcast(F32), ALU.subtract)
                ins.then_inc(y_l, 1)
            base = st["uu"].base
            for i in range(8):
                take(base + i, U[:, i, :])
                k = i - 4
                if k >= 0:
                    taken(base + i)
                    if k >= 2:
                        dve.wait_ge(y_l, k - 1)
                    re, im = tmp[2 * (k % 2)], tmp[2 * (k % 2) + 1]
                    ur, us, kr, ks = U[:, k, :], U[:, HT + k, :], spec[:, k, :], spec[:, HT + k, :]
                    own.mark(dve.tensor_tensor(re[:], ur, kr, ALU.mult))
                    own.mark(dve.tensor_tensor(hb[0][:], us, ks, ALU.mult))
                    own.mark(dve.tensor_tensor(im[:], ur, ks, ALU.mult))
                    own.step(dve.tensor_tensor(hb[1][:], us, kr, ALU.mult))
                    own.mark(dve.tensor_tensor(re[:], re[:], hb[0][:], ALU.subtract))
                    ins = dve.tensor_tensor(im[:], im[:], hb[1][:], ALU.add)
                    if k == 0:
                        own.step(ins)
                        ins = dve.tensor_tensor(im[0:1, :], U[0:1, HT, :], nyq[:], ALU.mult)
                    ins.then_inc(y_t, 1)
                    if k >= 1:
                        low_y(k - 1)
            low_y(3)
            for i in range(HT):
                conv(i, x0c[:, i, :])
            dve.wait_ge(y_l, HT)
            for k in range(HT):
                split(og[:, k, :], yH[:, HT + k, :], yL[:, HT + k, :]).then_inc(y2_ok, 1)
            base = st["inv"].base
            for i in range(4):
                take(base + i, yt[:, i, :])
            dve.wait_ge(nrm_r, 1)
            for c in range(HT):
                own.step(dve.tensor_scalar(tmp[0][:], wk[:, c, :], vcol("hyena_bias_2", c), None, ALU.mult))
                dve.wait_ge(yt_mm, c + 1)
                own.step(dve.scalar_tensor_tensor(tmp[1][:], bank(3 + c), nrm[:, c:c + 1], tmp[0][:], ALU.mult, ALU.add))
                own.step(dve.tensor_tensor(tmp[2][:], tmp[1][:], x0c[:, c, :], ALU.mult))
                split(tmp[2][:], yH[:, c, :], yL[:, c, :]).then_inc(y2_ok, 1)
                dve.wait_ge(y2_ok, HT + c + 1)
            residual(st["wo"], lambda i: mod[:, 16:24, 0][:, bass.ds(i, 1)], done="wo")
            stat("mlp2")
            dve.wait_ge(stat_r, stat_no["mlp2"] + 1)
            modulate(16, x, r, S, 2, lambda k: mod[:, 24 + k, 0:1], hH, hL)

            def hidden(q, n0):
                def one(pos):
                    dve.wait_ge(unit_done, pos.u + 1)
                    dve.tensor_scalar(tmp[pos.slot][:], bank(pos.slot), 0.0, None, ALU.max).then_inc(bank_free, 1)
                    taken(pos.u)
                    own.group(n0, pos.i, 2)
                    own.step(dve.tensor_tensor(tmp[3][:], tmp[pos.slot][:], tmp[pos.slot][:], ALU.mult))
                    h_, l_ = (y_[:, bass.ds(pos.i, 1), :][:, 0] for y_ in (mH[q % 2], mL[q % 2]))
                    split(tmp[3][:], h_, l_).then_inc(res["m1"], 1)
                    dve.wait_ge(res["m1"], pos.i + DT * q + 1)
                each_unit(dve, st[f"m1_{q}"], one)
                own.leave(n0 + 2 * DT)
            for name, q in (("m1_0", 0), ("m1_1", 1), ("m2_0", 0), ("m1_2", 2), ("m2_1", 1), ("m1_3", 3),
                            ("m2_2", 2), ("m2_3", 3)):
                if name[1] == "1":
                    hidden(q, own.n)
                else:
                    residual(st[name], lambda i: mod[:, 40:48, 0][:, bass.ds(i, 1)], squares=(q == 3),
                             done="m2_3" if q == 3 else None)
            finish("fin2", "norm_final_2")


def tables():
    i = np.arange(P)
    swap_m = np.zeros((P, P))
    swap_m[i ^ 32, i] = 1
    tri = (i[:, None] // CHUNK == i[None, :] // CHUNK) & (i[:, None] <= i[None, :])
    square = np.stack([np.eye(P), swap_m, np.eye(P)[::-1], tri, tri.T])
    inv_freq = 1.0 / (10000.0 ** (np.arange(0, A_DK, 2) / A_DK))
    angle = (np.arange(S)[:, None] * inv_freq[None, :]).T[i % 32]
    sign = np.where(i % 64 < 32, -1.0, 1.0)[:, None]
    rope_m = np.stack([np.cos(angle), sign * np.sin(angle)])
    tt, ff = np.arange(S), np.arange(S)
    turn = 2 * np.pi * ((tt[:, None] * ff[None, :]) % (2 * S)) / (2 * S)
    cos_m, sin_m = np.cos(turn), np.sin(turn)
    alt = (-1.0) ** tt
    sin_f = sin_m.copy()
    sin_f[:, 0] = alt
    dft = np.concatenate([cos_m, sin_f], axis=1)
    cos_i, sin_i = cos_m / S, sin_m / S
    cos_i[0] = 1 / (2 * S)
    sin_i[0] = alt / (2 * S)
    inverse = np.concatenate([cos_i, sin_i], axis=0)
    length = np.linspace(0.0, 1.0, S)[:, None]
    w = 2.0 * np.pi * np.arange(S) / S
    bands = (EMB - 1) // 2
    ang = w[:, None] * np.linspace(1e-4, bands - 1, bands)[None, :]
    z_m = np.concatenate([length, np.cos(ang), -np.sin(ang)], axis=1).T
    rates = np.abs(np.linspace(np.log(1e-2) / 1.5, np.log(1e-2) / 0.3, D_HY))
    decay_m = np.exp(-length * rates[None, :])
    reset_m = np.broadcast_to((np.arange(S) % CHUNK != 0), (P, S))
    f = lambda a: np.ascontiguousarray(a, dtype=np.float32)
    return {"k_square": f(square), "k_rope": f(rope_m), "k_dft": f(dft), "k_inv": f(inverse),
            "k_z": f(z_m), "k_decay": f(decay_m), "k_reset": f(reset_m)}


_INS = ["x", "mem", "norm_mix_g", "w_in", "lam_q1", "lam_k1", "lam_q2", "lam_k2", "subln_g",
        "rel_bias", "w_up_a", "w_up_b", "w_out", "norm_cross_g", "norm_mem_g", "w_cq", "w_ckv",
        "w_co", "norm_ffn_g", "w_gate_up", "w_down", "norm_final_g", "c_2", "ctx_2", "c_ctx_2",
        "w_ada_2", "b_ada_2", "norm_mix_2", "norm_mlp_2", "w_in_2", "conv_w_2", "conv_b_2",
        "filt_w1_2", "filt_b1_2", "filt_w2_2", "filt_b2_2", "filt_w3_2", "filt_b3_2",
        "filt_freq_2", "filt_wout_2", "hyena_bias_2", "gk_w_fwd_2", "gk_b_fwd_2", "gk_w_bwd_2",
        "gk_b_bwd_2", "gla_norm_2", "w_out_2", "w_mlp1_2", "w_mlp2_2", "norm_final_2"]
_OUTS = [((1, S, D), "float32")]


def kernel(**inputs):
    import numpy as _np
    import concourse.bacc as _bacc
    from concourse import mybir as _mybir
    from concourse.bass_utils import run_bass_kernel_spmd as _run

    nc = _bacc.Bacc("TRN2", target_bir_lowering=False, num_devices=1)
    given = {name: inputs[name] for name in _INS}
    given.update(tables())
    arrays, args = {}, {}
    for name, value in given.items():
        a = _np.ascontiguousarray(value)
        arrays[f"in_{name}_dram"] = a
        args[name] = nc.dram_tensor(f"in_{name}_dram", a.shape, _mybir.dt.from_np(a.dtype), kind="ExternalInput").ap()
    outs = []
    for i, (shape, dtype) in enumerate(_OUTS):
        dt = _mybir.dt.from_np(_np.dtype(dtype))
        outs.append(nc.dram_tensor(f"out_{i}_dram", shape, dt, kind="ExternalOutput").ap())
    build(nc, args, outs[0])
    r = _run(nc, [arrays], core_ids=[0])
    got = tuple(r.results[0][f"out_{i}_dram"] for i in range(len(_OUTS)))
    return got[0]
```

```python
from contextlib import ExitStack

import concourse.bass as bass
import numpy as np
from concourse import mybir

ALU = mybir.AluOpType
ACT = mybir.ActivationFunctionType
AX = mybir.AxisListType
F32 = mybir.dt.float32
F32R = mybir.dt.float32r

P = 128
D = 1024
DT = D // P
S = 512
ST = S // P
MEM = 256
EPS = 1e-6
NEG = -1e30
CHUNK = 64
NCH = S // CHUNK
A_HEADS, A_DK = 4, 64
B_HEADS, B_DH = 8, 64
X_HEADS = 4
D_FF = 2816
FT = D_FF // P
HALF = FT // 2
LAM_INIT = 0.8 - 0.6
MAX_REL = 256
REL = 2 * MAX_REL + 1
D_HY = 512
HT = D_HY // P
G_HEADS = 4
RANK = 16
LOG_SCALE = 1.0 / 16.0
D_MLP = 4 * D
N_IN_2 = 3104
EMB, HID = 33, 64
TWO_PI_HI = 6.28125
TWO_PI_LO = 2 * np.pi - 6.28125
ROUND = 1.5 * 2.0 ** 23
PI_SAFE = 3.1415925

SLOTS = 3
SLAB_KT = 8

VEC_ROWS = [("norm_mix_g", 8), ("norm_cross_g", 8), ("norm_mem_g", 8), ("norm_ffn_g", 8),
            ("norm_final_g", 8), ("norm_mix_2", 8), ("norm_mlp_2", 8), ("norm_final_2", 8),
            ("subln_g", 1), ("gla_norm_2", 1), ("hyena_bias_2", 4), ("gk_b_fwd_2", 2),
            ("gk_b_bwd_2", 2), ("c_2", 8), ("c_ctx_2", 8), ("b_ada_2", 48), ("conv_w_2", 36),
            ("conv_b_2", 12)]
VEC_AT, _at = {}, 0
for _name, _n in VEC_ROWS:
    VEC_AT[_name] = _at
    _at += _n
VECS = _at
VEC_SPLIT = VEC_AT["b_ada_2"]


class Stage:

    def __init__(self, name, n, kt, source, unroll=3):
        self.name, self.n, self.kt, self.source, self.unroll, self.base = name, n, kt, source, unroll, 0


class Pos:

    def __init__(self, stage, it, j, lo):
        self.it, self.j, self.lo = it, j, lo
        self.pair = it * (stage.unroll // 2) + (lo + j) // 2
        self.i = it * stage.unroll + (lo + j)
        b = stage.base + lo + j
        self.slot = b % SLOTS
        self.turn = it * (stage.unroll // SLOTS) + b // SLOTS
        self.u = self.i + stage.base


def each_unit(eng, stage, body, lo=0, hi=None):
    hi = stage.n if hi is None else hi
    k = stage.unroll
    start = lo
    if stage.base + lo < SLOTS:
        for j in range(k):
            body(Pos(stage, 0, j, lo))
        start = lo + k
    n = (hi - start) // k
    if n >= 2:
        with eng.Fori(0, n, 1) as it:
            for j in range(k):
                body(Pos(stage, it, j, start))
        start += n * k
    for j in range(hi - start):
        body(Pos(stage, j // k, j % k, start))


class Own:

    def __init__(self, eng, sem):
        self.eng, self.sem, self.n, self.at = eng, sem, 0, 0

    def mark(self, ins):
        ins.then_inc(self.sem, 1)
        self.n += 1

    def settle(self):
        self.eng.wait_ge(self.sem, self.at + self.n)

    def step(self, ins):
        self.mark(ins)
        self.settle()

    def group(self, first, index, per):
        self.at, self.n = index * per + first, 0

    def leave(self, total):
        self.at, self.n = 0, total


def build(nc, t, out):
    ctx = ExitStack()
    with ctx:
        top = [16512]

        def place(name, shape, dt=F32, at=None):
            size = int(np.prod(shape[1:])) * 4
            if at is None:
                at = top[0]
                top[0] += (size + 31) // 32 * 32
            assert at + size <= 229344, (name, at + size)
            return nc.alloc_sbuf_tensor_at(name, shape, dt, offset=at)

        def sem(name):
            return ctx.enter_context(nc.semaphore(name))

        raw = [place(f"raw{i}", [P, SLAB_KT, P]) for i in range(SLOTS)]
        WH = [place(f"WH{i}", [P, SLAB_KT, P], F32R) for i in range(SLOTS)]
        WL = [place(f"WL{i}", [P, SLAB_KT, P], F32R) for i in range(SLOTS)]
        x = place("x", [P, DT, S])
        h_at = top[0]
        hH = place("hH", [P, DT, S], F32R)
        hL = place("hL", [P, DT, S], F32R)
        r_at = top[0]
        r = place("r", [P, S])
        acc = place("acc", [P, S])
        tmp = [place(f"tmp{i}", [P, S]) for i in range(4)]
        ident = place("ident", [P, P])
        ones = place("ones", [P, P])
        swap = place("swap", [P, P])
        anti = place("anti", [P, P])
        vec = place("vec", [P, VECS])
        cS = place("cS", [P, DT, 2])
        cR = place("cR", [P, DT, 4], F32R)
        mod = place("mod", [P, 48, 2])
        gain = place("gain", [P, 4, DT])
        lam_parts = place("lam_parts", [P, 4, A_DK])
        lam_s = place("lam_s", [P, 8])
        tiny = place("tiny", [P, 16])
        warm = place("warm", [P, 1])
        mask_row = place("mask_row", [1, P + CHUNK])
        nrm = place("nrm", [P, HT])
        gate_w = place("gate_w", [2 * RANK, 2, 256])
        Z = top[0]

        def z(name, kb, shape, dt=F32):
            return place(name, shape, dt, at=Z + int(kb * 1024))

        def hz(name, kb, shape, dt=F32):
            return place(name, shape, dt, at=h_at + int(kb * 1024))

        qA = z("qA", 0, [P, 4, S])
        kA = z("kA", 8, [P, 4, S])
        qB = z("qB", 16, [P, 4, S])
        kB = z("kB", 24, [P, 4, S])
        vA = z("vA", 32, [P, ST, S])
        vB = z("vB", 40, [P, ST, S])
        gates = z("gates", 48, [P, 2 * DT, S])
        tok = z("tok", 48, [P, ST, D])
        rope = z("rope", 64, [P, 2, S])
        vecload = z("vecload", 68, [P, 2, P])
        bias_t = z("bias_t", 80, [P, B_HEADS, S])
        rows = [z(f"rows{i}", 96 + 2 * i, [4, S]) for i in range(4)]
        mod_rows = z("mod_rows", 96, [48, 4, P])
        hankel = z("hankel", 0, [P, B_HEADS, S])
        rel_ext = z("rel_ext", 16, [B_HEADS, 768])
        attT = [hz(f"attT{i}", 8 * i, [P, ST, S]) for i in range(2)]
        pA = [hz(f"pA{i}", 16 + 4 * i, [P, 2, S]) for i in range(2)]
        pB = [hz(f"pB{i}", 16 + 2 * i, [P, S]) for i in range(4)]
        mgH = z("mgH", 0, [P, DT, S], F32R)
        mgL = z("mgL", 16, [P, DT, S], F32R)
        memtok = z("memtok", 32, [P, 2, D])
        mem_t = [z(f"mem_t{i}", 89 + i, [P, MEM]) for i in range(2)]
        mem_sq = [z(f"mem_sq{i}", 91 + i, [P, MEM]) for i in range(2)]
        mem_acc = z("mem_acc", 93, [P, MEM])
        memH = z("memH", 40, [P, DT, MEM], F32R)
        memL = z("memL", 80, [P, DT, MEM], F32R)
        rm = z("rm", 88, [P, MEM])
        kc = z("kc", 48, [P, DT, MEM])
        vc = z("vc", 56, [P, 2, D])
        qc = z("qc", 64, [P, DT, S])
        oH = z("oH", 0, [P, DT, S], F32R)
        oL = z("oL", 16, [P, DT, S], F32R)
        pC = [z(f"pC{i}", 32 + i, [P, MEM]) for i in range(4)]
        pcT = [z(f"pcT{i}", 36 + 4 * i, [P, 2, S]) for i in range(2)]
        fH = z("fH", 0, [P, FT, S], F32R)
        fL = z("fL", 44, [P, FT, S], F32R)
        ctxtok = z("ctxtok", 88, [P, 2, D])
        ctxT = z("ctxT", 96, [P, DT, MEM])
        rc = z("rc", 88, [P, MEM])
        acc2 = z("acc2", 89, [P, S])
        r2 = z("r2", 91, [P, S])
        hy = z("hy", 0, [P, 12, S])
        qG = z("qG", 24, [P, 2, S])
        kG = z("kG", 28, [P, 2, S])
        masks = z("masks", 32, [P, 2, P])
        reset = z("reset", 34, [P, S])
        vG = z("vG", 40, [P, ST, S])
        kGc = z("kGc", 48, [P, 2, MEM])
        vGc = z("vGc", 50, [P, 2, S])
        gr = z("gr", 54, [2 * RANK, S + MEM])
        cH = z("cH", 65, [P, DT, MEM], F32R)
        cL = z("cL", 73, [P, DT, MEM], F32R)
        vfT = [z(f"vfT{i}", 81 + 2 * i, [P, S]) for i in range(2)]
        vfTc = [z(f"vfTc{i}", 85 + i, [P, MEM]) for i in range(2)]
        og = z("og", 96, [P, 4, S])
        kin = [hz(f"kin{i}", 2 * i, [P, S]) for i in range(4)]
        qin = [hz(f"qin{i}", 8 + 2 * i, [P, S]) for i in range(4)]
        kend = [hz(f"kend{i}", 16 + 2 * i, [P, S]) for i in range(4)]
        oG = kend
        kendT = [hz(f"kendT{i}", 24 + 2 * i, [P, ST, P]) for i in range(4)]
        att = [z(f"att{i}", 36 + 2 * i, [P, S]) for i in range(2)]
        state = [z(f"state{i}", 57 + 4 * i, [P, NCH, P]) for i in range(4)]
        cum = [z(f"cum{i}", kb, [P, S + MEM]) for i, kb in enumerate((57, 60, 36))]
        cum.append(place("cum3", [P, S + MEM], at=r_at))
        lg = [z(f"lg{i}", 87 + 3 * i, [P, S + MEM]) for i in range(2)]
        arg = [z(f"arg{i}", 73 + 2 * i, [P, S]) for i in range(2)]
        ex = [z(f"ex{i}", 79 + 2 * i, [P, S]) for i in range(4)]
        kendc = [z(f"kendc{i}", 89 + i, [P, MEM]) for i in range(4)]
        last = z("last", 93, [P, 4, NCH])
        tot = z("tot", 93.25, [P, 4])
        kendcT = [z(f"kendcT{i}", at_, [P, 2, P]) for i, at_ in enumerate((33, 94, 95, 54))]
        zT = z("zT", 24, [EMB, S])
        fw = z("fw", 26, [HID, 3, HID])
        fvec = z("fvec", 26.75, [HID, 4])
        fout = z("fout", 27, [HID, 2 * D_HY])
        decay = z("decay", 73, [P, HT, S])
        fh = [z(f"fh{i}", 81 + 2 * i, [HID, S]) for i in range(2)]
        ft = [z(f"ft{i}", 85 + 2 * i, [HID, S]) for i in range(2)]
        hb = [z(f"hb{i}", 83 + 2 * i, [P, S]) for i in range(2)]
        nyq = z("nyq", 89, [1, S])
        ab = hz("ab", 0, [P, 2, HT, S])
        spec = hz("spec", 16, [P, 2 * HT, S])
        abH = z("abH", 57, [P, 2, HT, S], F32R)
        abL = z("abL", 40, [P, 2, HT, S], F32R)
        x0c, wk = hy[:, 0:HT], hy[:, HT:2 * HT]
        wtH = z("wtH", 16, [P, HT, S], F32R)
        wtL = z("wtL", 24, [P, HT, S], F32R)
        U = hz("U", 0, [P, 2 * HT, S])
        YH = z("YH", 57, [P, 2 * HT, S], F32R)
        YL = z("YL", 40, [P, 2 * HT, S], F32R)
        yt = z("yt", 32, [P, HT, S])
        yH = z("yH", 16, [P, DT, S], F32R)
        yL = z("yL", 73, [P, DT, S], F32R)
        mH = [z(f"mH{i}", 32 * i, [P, DT, S], F32R) for i in range(2)]
        mL = [z(f"mL{i}", 32 * i + 16, [P, DT, S], F32R) for i in range(2)]
        final = z("final", 64, [P, ST, D])

        ps = ctx.enter_context(nc.psum_tensor("ps", [P, 8, S], F32))

        def bank(i, n=S, m=P):
            return ps[0:m, i, 0:n]

        mod_dram = nc.dram_tensor("mod_rows_dram", (4, 6 * D), F32, kind="Internal")
        bias_dram = nc.dram_tensor("bias_ext", (B_HEADS, 768), F32, kind="Internal")

        def columns(w, k0=0, kt=DT, c0=0):
            v = w.rearrange("(k p) n -> p k n", p=P)[:, k0:k0 + kt, :]
            return lambda pos: v[:, :, bass.ds(pos.i * P + c0 * P, P)]

        def pairs(even, odd):
            return lambda pos: (odd if (pos.lo + pos.j) % 2 else even)[:, :, bass.ds(pos.pair * P, P)]

        w_in = t["w_in"][0]
        w_ada = t["w_ada_2"][0].rearrange("(k p) n -> p k n", p=P)
        w_ckv = t["w_ckv"][0]
        gu = t["w_gate_up"][0].rearrange("(k p) n -> p k n", p=P)
        up_a = t["w_up_a"][0].rearrange("(k p) n -> p k n", p=P)
        up_b = t["w_up_b"][0].rearrange("(k p) n -> p k n", p=P)
        w_in2 = t["w_in_2"][0]
        w_m1, w_m2 = t["w_mlp1_2"][0], t["w_mlp2_2"][0]
        gates_slab = w_in2.rearrange("(k p) n -> p k n", p=P)[:, :, N_IN_2 - 2 * RANK:N_IN_2]
        stages = [
            Stage("rope", 8, DT, columns(w_in)),
            Stage("va", 4, DT, columns(w_in, c0=8)),
            Stage("qkb", 8, DT, columns(w_in, c0=12)),
            Stage("vb", 4, DT, columns(w_in, c0=20)),
            Stage("gate", 16, DT, columns(w_in, c0=24)),
            Stage("ada", 48, DT, lambda pos: w_ada[:, 2 * (pos.j % 4):2 * (pos.j % 4) + 2,
                                                   bass.ds((pos.it * 3 + pos.j // 4) * S, S)], 12),
            Stage("up", 16, 4, pairs(up_a, up_b), 6),
            Stage("out", 8, DT, columns(t["w_out"][0])),
            Stage("mk", 8, DT, columns(w_ckv)),
            Stage("mv", 8, DT, columns(w_ckv, c0=8)),
            Stage("cq", 8, DT, columns(t["w_cq"][0])),
            Stage("co", 8, DT, columns(t["w_co"][0])),
            Stage("gu", 44, DT, pairs(gu[:, :, 0:D_FF], gu[:, :, D_FF:2 * D_FF]), 6),
            Stage("dn0", 8, 8, columns(t["w_down"][0], 0, 8)),
            Stage("dn1", 8, 7, columns(t["w_down"][0], 8, 7)),
            Stage("dn2", 8, 7, columns(t["w_down"][0], 15, 7)),
            Stage("hyp", 12, DT, columns(w_in2)),
            Stage("grp", 1, DT, lambda pos: gates_slab),
            Stage("qp", 2, DT, columns(w_in2, c0=12)),
            Stage("kp", 2, DT, columns(w_in2, c0=14)),
            Stage("vp", 4, DT, columns(w_in2, c0=16)),
            Stage("ogp", 4, DT, columns(w_in2, c0=20)),
            Stage("sa", 5, 4, columns(t["k_dft"], kt=4)),
            Stage("sb", 4, 4, columns(t["k_dft"], kt=4, c0=4)),
            Stage("uu", 8, 4, columns(t["k_dft"], kt=4)),
            Stage("inv", 4, 8, columns(t["k_inv"])),
            Stage("wo", 8, DT, columns(t["w_out_2"][0])),
        ] + [Stage(f"m1_{q}", 8, DT, columns(w_m1, c0=8 * q)) for q in (0, 1)] + [
            Stage("m2_0", 8, DT, columns(w_m2, 0)),
            Stage("m1_2", 8, DT, columns(w_m1, c0=16)),
            Stage("m2_1", 8, DT, columns(w_m2, 8)),
            Stage("m1_3", 8, DT, columns(w_m1, c0=24)),
            Stage("m2_2", 8, DT, columns(w_m2, 16)),
            Stage("m2_3", 8, DT, columns(w_m2, 24)),
        ]
        total = 0
        for s_ in stages:
            s_.base = total
            total += s_.n
        st = {s_.name: s_ for s_ in stages}
        all_units = [(s_, i) for s_ in stages for i in range(s_.n)]
        width = lambda s_: 2 * RANK if s_.name == "grp" else P

        slab_in = [sem(f"slab_in{i}") for i in range(SLOTS)]
        high_done = sem("high_done")
        low_done = sem("low_done")
        unit_done = sem("unit_done")
        bank_free = sem("bank_free")
        res = {n: sem("res_" + n) for n in
               ("rope", "up", "out", "co", "gu", "dn2", "wo", "m1", "m2_3")}
        tok_in, const_in, vec_in, lam_in, rope_in, rel_in = (
            sem(n) for n in ("tok_in", "const_in", "vec_in", "lam_in", "rope_in", "rel_in"))
        vec_t, vec_ok, x_t, x_sq, x_c, x_acc, stat_sum, stat_v, stat_r = (
            sem(n) for n in ("vec_t", "vec_ok", "x_t", "x_sq", "x_c", "x_acc", "stat_sum",
                             "stat_v", "stat_r"))
        silu_c, rel_ok, rel_out, rel_back, rel_mm, bias_ok = (
            sem(n) for n in ("silu_c", "rel_ok", "rel_out", "rel_back", "rel_mm", "bias_ok"))
        rot_done, roped, v_turned, v_kept, sig_done = (
            sem(n) for n in ("rot_done", "roped", "v_turned", "v_kept", "sig_done"))
        cond_ok, mod_in, mod_mm, lam_exp, lam_ok = (
            sem(n) for n in ("cond_ok", "mod_in", "mod_mm", "lam_exp", "lam_ok"))
        row_out = [sem(f"row_out{i}") for i in range(4)]
        scored, maxed, exped, normed, turned, kept, pv_done, pv_out = (
            {k: sem(f"{k}_{n}") for k in "abc"} for n in
            ("scored", "maxed", "exped", "normed", "turned", "kept", "pv_done", "pv_out"))
        head_sq, head_mm, head_v, head_r = (sem(n) for n in ("head_sq", "head_mm", "head_v", "head_r"))
        y_ok, silu_done, mem_in, own_v, own_a, mod_ok = (
            sem(n) for n in ("y_ok", "silu_done", "mem_in", "own_v", "own_a", "mod_ok"))
        ctx_in, gate_in, gla_in, filt_in = (sem(n) for n in ("ctx_in", "gate_in", "gla_in", "filt_in"))
        og_h, yc_ok, yc_h = (sem(n) for n in ("og_h", "yc_ok", "yc_h"))
        h_ok, y_high, head_n = sem("h_ok"), sem("y_high"), sem("head_n")
        md_t, md_h, md_ok = (sem(n) for n in ("md_t", "md_h", "md_ok"))
        g_mm, g_y, g_ln, g_cum, g_ex, g_arg, g_ex2, g_qk, g_done = (
            sem("gla_" + n) for n in ("mm", "y", "ln", "cum", "ex", "arg", "ex2", "qk", "done"))
        kend_mm, kend_kept, state_mm, state_ok, fb_mm, att_ok, o_mm, o_sq = (
            sem(n) for n in ("kend_mm", "kend_kept", "state_mm", "state_ok", "fb_mm", "att_ok", "o_mm", "o_sq"))
        gh_mm, gh_v, gh_r, gh_y = (sem("gla_head_" + n) for n in ("mm", "v", "r", "y"))
        f_mm, f_arg, f_sin, f_out = (sem("filt_" + n) for n in ("mm", "arg", "sin", "out"))
        ab_done, ab_sq, ab_h, ab_l, nrm_mm, nrm_v, nrm_r = (
            sem(n) for n in ("ab_done", "ab_sq", "ab_h", "ab_l", "nrm_mm", "nrm_v", "nrm_r"))
        w_ok, wt_mm, wt_h, wt_l, y_t, y_h, y_l, yt_mm, y2_ok = (
            sem(n) for n in ("w_ok", "wt_mm", "wt_h", "wt_l", "y_t", "y_h", "y_l", "yt_mm", "y2_ok"))
        fin_h, fin_t, fin_c, fin_out = (sem(n) for n in ("fin_h", "fin_t", "fin_c", "fin_out"))
        STATS = ["x", "mem", "cross", "ctx", "ffn", "fin1", "mix2", "mlp2", "fin2"]
        stat_no = {n: i for i, n in enumerate(STATS)}

        def wide(a):
            return a[:].rearrange("p (a b) c -> p a (b c)", a=2)

        def vcol(name, i=0):
            c = VEC_AT[name]
            if isinstance(i, int):
                return vec[:, c + i:c + i + 1]
            return vec[:, c:c + 8][:, bass.ds(i, 1)]

        ATT = {"a": (A_HEADS * ST, 2, 3), "b": (B_HEADS * ST, 3, 4), "c": (X_HEADS * ST, 3, 4)}

        def keys_of(kind, qt):
            return 2 if kind == "c" else qt + 1

        block = ctx.enter_context(nc.Block())

        CONSTS_IN = 16 * 2 + 5

        @block.sync
        def _(sp):
            sp.dma_start(ident[:], t["k_square"][0]).then_inc(tok_in, 16)
            sp.dma_start(tok[:], t["x"][0].rearrange("(t p) d -> p t d", p=P)).then_inc(tok_in, 16)
            for k, dst in enumerate((swap, anti)):
                sp.dma_start(dst[:], t["k_square"][1 + k]).then_inc(const_in, 16)
            sp.dma_start(rel_ext[:, 0:REL], t["rel_bias"][0]).then_inc(rel_in, 16)
            for name, n in VEC_ROWS:
                c = VEC_AT[name]
                side, c = (0, c) if c < VEC_SPLIT else (1, c - VEC_SPLIT)
                src = t[name]
                while len(src.shape) > 1:
                    src = src.rearrange("a b -> (a b)") if len(src.shape) == 2 else src.rearrange("a b c -> (a b c)")
                sp.dma_start(vecload[c:c + n, side, :], src.rearrange("(n p) -> n p", p=P)).then_inc(vec_in, 16)
            sp.dma_start(rope[:], t["k_rope"].rearrange("a p s -> p a s")).then_inc(rope_in, 16)
            for k, name in enumerate(("lam_q1", "lam_k1", "lam_q2", "lam_k2")):
                sp.dma_start(lam_parts[:, k, :], t[name][0].partition_broadcast(P)).then_inc(lam_in, 16)

            def stream(stage, lo=0, hi=None):
                def load(pos):
                    if not isinstance(pos.u, int) or pos.u >= SLOTS:
                        sp.wait_ge(low_done, pos.u - (SLOTS - 1))
                    dst = wide(raw[pos.slot]) if stage.name == "ada" else raw[pos.slot][:, 0:stage.kt, 0:width(stage)]
                    sp.dma_start(dst, stage.source(pos)).then_inc(slab_in[pos.slot], 16)
                each_unit(sp, stage, load, lo, hi)

            for name in ("rope", "va", "qkb", "vb", "gate"):
                stream(st[name])
            sp.wait_ge(const_in, CONSTS_IN)
            for d, name in enumerate(("gk_w_fwd_2", "gk_w_bwd_2")):
                sp.dma_start(gate_w[d * RANK:(d + 1) * RANK, d, :], t[name][0]).then_inc(gate_in, 16)
            stream(st["ada"])
            stream(st["up"], 0, 3)
            sp.wait_ge(pv_out["b"], B_HEADS // 2)
            sp.dma_start(memtok[:], t["mem"][0].rearrange("(t p) d -> p t d", p=P)).then_inc(mem_in, 16)
            stream(st["up"], 3)
            for name in ("out", "mk", "mv"):
                stream(st[name])
            stream(st["cq"], 0, 3)
            sp.wait_ge(bank_free, st["cq"].base)
            sp.dma_start(ctxtok[:], t["ctx_2"][0].rearrange("(t p) d -> p t d", p=P)).then_inc(ctx_in, 16)
            stream(st["cq"], 3)
            for name in ("co", "gu", "dn0", "dn1", "dn2"):
                stream(st[name])
            stream(st["hyp"])
            sp.wait_ge(unit_done, st["hyp"].base)
            sp.dma_start(masks[:], t["k_square"][3:5].rearrange("k p c -> p k c")).then_inc(gla_in, 16)
            sp.dma_start(reset[:], t["k_reset"]).then_inc(gla_in, 16)
            for name in ("grp", "qp", "kp", "vp", "ogp"):
                stream(st[name])
            stream(st["sa"], 0, 3)
            sp.wait_ge(g_done, 4)
            sp.dma_start(zT[:], t["k_z"]).then_inc(filt_in, 16)
            sp.dma_start(fw[0:EMB, 0, :], t["filt_w1_2"][0]).then_inc(filt_in, 16)
            sp.dma_start(fw[:, 1, :], t["filt_w2_2"][0]).then_inc(filt_in, 16)
            sp.dma_start(fw[:, 2, :], t["filt_w3_2"][0]).then_inc(filt_in, 16)
            sp.dma_start(fout[:], t["filt_wout_2"][0]).then_inc(filt_in, 16)
            for k, name in enumerate(("filt_b1_2", "filt_b2_2", "filt_b3_2", "filt_freq_2")):
                sp.dma_start(fvec[:, k:k + 1], t[name].rearrange("a p -> p a")).then_inc(filt_in, 16)
            sp.dma_start(decay[:], t["k_decay"].rearrange("(t p) c -> p t c", p=P)).then_inc(filt_in, 16)
            stream(st["sa"], 3)
            for name in ("sb", "uu", "inv", "wo", "m1_0", "m1_1", "m2_0", "m1_2", "m2_1", "m1_3", "m2_2", "m2_3"):
                stream(st[name])
            for k in range(2):
                c = slice(k * D // 2, (k + 1) * D // 2)
                sp.wait_ge(fin_c, (k + 1) * DT // 2)
                sp.dma_start(out[0].rearrange("(t p) d -> p t d", p=P)[:, :, c], final[:, :, c]).then_inc(fin_out, 16)
            sp.wait_ge(fin_out, 32)

        @block.gpsimd
        def _(pool):
            pool.memset(ones[:], 1.0).then_inc(const_in, 1)
            pool.memset(gate_w[:], 0.0).then_inc(const_in, 1)
            pool.memset(mask_row[0:1, 0:CHUNK], NEG).then_inc(const_in, 1)
            pool.memset(mask_row[0:1, CHUNK:P], 0.0).then_inc(const_in, 1)
            pool.memset(mask_row[0:1, P:P + CHUNK], 1.0).then_inc(const_in, 1)
            pool.wait_ge(rel_ok, 1)
            pool.dma_start(bias_dram[:, :], rel_ext[:]).then_inc(rel_out, 16)
            pool.wait_ge(rel_out, 16)
            pool.dma_start(hankel[:], bass.AP(bias_dram, MAX_REL - P + 1, [[1, P], [768, B_HEADS], [1, S]])).then_inc(rel_back, 16)

            def low(stage):
                n = width(stage)

                def one(pos):
                    pool.wait_ge(high_done, pos.u + 1)
                    pool.tensor_tensor(WL[pos.slot][:, 0:stage.kt, 0:n], raw[pos.slot][:, 0:stage.kt, 0:n],
                                       WH[pos.slot][:, 0:stage.kt, 0:n].bitcast(F32),
                                       ALU.subtract).then_inc(low_done, 1)
                each_unit(pool, stage, one)
            for stage in stages:
                low(stage)


        @block.scalar
        def _(act):
            own = Own(act, own_a)
            act.wait_ge(const_in, CONSTS_IN)
            def high(s_, slot, turn, result=None, value=None):
                act.wait_ge(slab_in[slot], turn * 16 + 16)
                if value is not None:
                    act.wait_ge(result or unit_done, value)
                n = width(s_)
                act.activation(WH[slot][:, 0:s_.kt, 0:n], raw[slot][:, 0:s_.kt, 0:n],
                               ACT.Copy).then_inc(high_done, 1)

            def follow(stage, after=None, result=None, lo=0):
                def inner(pos):
                    high(stage, pos.slot, pos.turn + 1, result, pos.u + 1)
                    if after:
                        after(pos)
                inside = max(lo, stage.n - SLOTS)
                if inside > lo and stage.n > SLOTS:
                    each_unit(act, stage, inner, lo, inside)
                for i in range(max(inside, lo), stage.n):
                    pos = Pos(stage, i // stage.unroll, i % stage.unroll, 0)
                    high_at(stage.base + i + SLOTS, result)
                    if after:
                        after(pos)

            def high_at(u, result=None):
                if u < len(all_units):
                    high(all_units[u][0], u % SLOTS, u // SLOTS, result, u - SLOTS + 1)

            def prep_tile(n, n0, k, dst, squares):
                act.wait_ge(x_t, n0 + k + 1)
                if k >= 2:
                    act.wait_ge(x_acc, n0 + k - 1)
                act.activation(dst, bank(3 + k % 2, n), ACT.Copy).then_inc(x_c, 1)
                act.wait_ge(x_c, n0 + k + 1)
                act.activation(squares[k % 2][:, 0:n], dst, ACT.Square).then_inc(x_sq, 1)

            def prep(tiles, n0, keep):
                for k in range(DT):
                    prep_tile(tiles * P, n0, k, keep[:, k, :], tmp[2:4])

            def root_table():
                own.step(act.activation(warm[:], ones[:, 0:1], ACT.Sqrt))

            def stat(name, dst, n=S):
                root_table()
                act.wait_ge(stat_v, stat_no[name] + 1)
                act.activation(dst[:, 0:n], tmp[3][:, 0:n], ACT.Sqrt).then_inc(stat_r, 1)

            def finish(stat_name):
                stat(stat_name, r)
                for k in range(DT):
                    act.wait_ge(fin_t, k + 1)
                    act.activation(final[:, :, k * P:(k + 1) * P],
                                   bank(3 + k % 2).rearrange("p (t c) -> p t c", c=P), ACT.Copy).then_inc(fin_c, 1)

            prep(ST, 0, x)
            stat("x", r)
            for u in range(SLOTS):
                high(st["rope"], u, 0)
            for h in range(B_HEADS):
                act.wait_ge(rel_mm, h + 1)
                act.activation(bias_t[:, h, :], bank(5 + h % 2), ACT.Copy, scale=float(B_DH) ** 0.5).then_inc(bias_ok, 1)
            act.wait_ge(vec_ok, 1)
            act.activation(cS[:, :, 0], vec[:, VEC_AT["c_2"]:VEC_AT["c_2"] + DT], ACT.Silu).then_inc(silu_c, 1)
            act.activation(cS[:, :, 1], vec[:, VEC_AT["c_ctx_2"]:VEC_AT["c_ctx_2"] + DT], ACT.Silu).then_inc(silu_c, 1)
            act.wait_ge(lam_ok, 2)
            act.activation(lam_s[:, 2:4], lam_s[:, 0:2], ACT.Exp).then_inc(lam_exp, 1)
            follow(st["rope"])

            def keep_v(dst, n0, which, tt=ST):
                def one(i):
                    act.wait_ge(v_turned, n0 + i + 1)
                    act.activation(dst[:, 0:tt, i * P:(i + 1) * P],
                                   bank(5 + (n0 + i) % 2, tt * P).rearrange("p (t c) -> p t c", c=P),
                                   ACT.Copy).then_inc(v_kept, 1)
                return one

            def values(stage, dst, n0, tt=ST):
                one = keep_v(dst, n0, stage, tt)
                for i in range(stage.n):
                    high_at(stage.base + i + SLOTS)
                    if i >= 1:
                        one(i - 1)
                one(stage.n - 1)

            values(st["va"], vA, 0)
            follow(st["qkb"])
            values(st["vb"], vB, 4)

            def sigmoid(pos):
                act.activation(gates[:, bass.ds(pos.i, 1), :], tmp[pos.slot][:], ACT.Sigmoid).then_inc(sig_done, 1)
            follow(st["gate"], sigmoid, bank_free)

            def ada_step(i):
                high_at(st["ada"].base + i + SLOTS)
                if i % 4 == 3:
                    b = i // 4
                    if b >= 4:
                        act.wait_ge(row_out[b % 4], 16 * (b // 4))
                    act.activation(rows[b % 4][:], bank(1, S, 4), ACT.Copy).then_inc(bank_free, 4)
                    act.wait_ge(bank_free, st["ada"].base + 4 * b + 4)
                    act.dma_start(mod_dram[:, b * S:(b + 1) * S], rows[b % 4][:]).then_inc(row_out[b % 4], 16)

            def attend(kind):
                items, lag, ahead = ATT[kind]
                comps = 2 if kind == "a" else 1
                for s_ in range(items + lag):
                    if s_ < items:
                        n, qt = s_, s_ % ST
                        nk = keys_of(kind, qt) * P
                        act.wait_ge(maxed[kind], n + 1)
                        for c in range(comps):
                            j = 2 * (n % 2) + c
                            if kind == "a":
                                src, dst = bank(3 + j, nk), pA[n % 2][:, c, 0:nk]
                                if n >= 2:
                                    act.wait_ge(turned["a"], n - 1)
                                scale = A_DK ** -0.5
                            elif kind == "b":
                                src, dst, scale = pB[n % 4][:, 0:nk], pB[n % 4][:, 0:nk], 1.0
                            else:
                                src, dst, scale = bank(3 + n % 4, nk), pC[n % 4][:, 0:nk], 1.0 / 16
                                if n >= 4:
                                    act.wait_ge(turned["c"], n - 3)
                            k = 2 * (n % 4) + c
                            ins = act.activation(dst, src, ACT.Exp, bias=tiny[:, k:k + 1], scale=scale,
                                                 accum_out=tiny[:, 8 + k:9 + k])
                        ins.then_inc(exped[kind], 1)
                        if kind != "c":
                            ada_step(s_ + (0 if kind == "a" else A_HEADS * ST))
                    m = s_ - lag
                    if m >= 0:
                        h, qt = m // ST, m % ST
                        kn = keys_of(kind, qt)
                        act.wait_ge(turned[kind], m + 1)
                        if h >= 2:
                            act.wait_ge(pv_done[kind], h - 1)
                        dst = (pcT if kind == "c" else attT)[h % 2]
                        act.activation(dst[:, 0:kn, qt * P:(qt + 1) * P],
                                       bank((7, 2)[m % 2], kn * P).rearrange("p (t c) -> p t c", c=P),
                                       ACT.Copy).then_inc(kept[kind], 1)
                    if kind == "b" and s_ % ST == 0 and s_ // ST < A_HEADS:
                        h = s_ // ST
                        act.wait_ge(head_v, h + 1)
                        act.activation(tmp[h][:], tmp[h][:], ACT.Sqrt).then_inc(head_r, 1)
            attend("a")
            attend("b")
            act.wait_ge(pv_out["b"], B_HEADS // 2)
            act.wait_ge(head_n, 1)
            for k in range(DT):
                act.activation(hH[:, k, :], (qA if k < 4 else qB)[:, k % 4, :], ACT.Copy).then_inc(y_high, 1)
            for i in range(4):
                act.wait_ge(row_out[i], 16 * 3)
            act.dma_start(mod_rows[:], mod_dram[:, :].rearrange("c (m p) -> m c p", p=P)).then_inc(mod_in, 16)
            for i in range(2 * DT):
                high_at(st["up"].base + i + SLOTS)
                if i % 2 and i > 1:
                    prep_tile(MEM, 8, i // 2 - 1, mem_t[(i // 2 - 1) % 2][:], mem_sq)
            prep_tile(MEM, 8, DT - 1, mem_t[(DT - 1) % 2][:], mem_sq)
            stat("mem", rm, MEM)
            follow(st["out"])
            for i in range(SLOTS):
                high_at(st["mk"].base + i + SLOTS)
            stat("cross", r)
            follow(st["mk"], lo=SLOTS)
            values(st["mv"], vc, 8, 2)
            for i in range(DT):
                high_at(st["cq"].base + i + SLOTS)
                if i:
                    prep_tile(MEM, 16, i - 1, ctxT[:, i - 1, :], tmp[2:4])
            prep_tile(MEM, 16, DT - 1, ctxT[:, DT - 1, :], tmp[2:4])
            stat("ctx", rc, MEM)
            attend("c")
            follow(st["co"])
            stat("ffn", r)

            def silu(pos):
                if (pos.lo + pos.j) % 2 == 0:
                    act.wait_ge(bank_free, pos.u + 1)
                    act.activation(tmp[pos.slot][:], tmp[pos.slot][:], ACT.Silu).then_inc(silu_done, 1)
            follow(st["gu"], silu)
            for name in ("dn0", "dn1", "dn2"):
                follow(st[name])
            root_table()
            act.wait_ge(stat_v, stat_no["fin1"] + 1)
            act.activation(r[:], tmp[2][:], ACT.Sqrt).then_inc(stat_r, 1)
            act.wait_ge(stat_v, stat_no["mix2"] + 1)
            act.activation(r2[:], tmp[3][:], ACT.Sqrt).then_inc(stat_r, 1)

            def modulate(n0, n, shift, dh):
                for k in range(DT):
                    act.wait_ge(md_t, n0 + k + 1)
                    act.activation(dh[:, k, :], tmp[k % 3][:, 0:n], ACT.Identity, bias=shift(k)).then_inc(md_h, 1)
            modulate(0, S, lambda k: mod[:, k, 0:1], hH)
            for i in range(SLOTS):
                high_at(st["hyp"].base + i + SLOTS)
            modulate(8, MEM, lambda k: mod[:, k, 1:2], cH)
            follow(st["hyp"], lo=SLOTS)
            follow(st["grp"])

            def soft(g):
                a = cum[g]
                act.wait_ge(g_y, g + 1)
                own.step(act.activation(a[:], lg[g % 2][:], ACT.Abs))
                own.step(act.activation(a[:], a[:], ACT.Exp, scale=-1.0))
                act.activation(a[:], a[:], ACT.Ln, bias=ones[:, 0:1]).then_inc(g_ln, 1)
            for g in range(4):
                high_at(st["qp"].base + g + SLOTS)
                soft(g)

            def keep_gla_v(i):
                act.wait_ge(v_turned, 16 + i + 1)
                c = slice(i * P, (i + 1) * P)
                act.activation(vG[:, :, c], bank(6).rearrange("p (t c) -> p t c", c=P), ACT.Copy)
                act.activation(vGc[:, :, c], bank(7, MEM).rearrange("p (t c) -> p t c", c=P), ACT.Copy).then_inc(v_kept, 1)
            for i in range(4):
                high_at(st["vp"].base + i + SLOTS)
                if i >= 1:
                    keep_gla_v(i - 1)
            keep_gla_v(3)

            def silu_og(pos):
                own.mark(act.activation(og[:, pos.i, :], og[:, pos.i, :], ACT.Silu))
            follow(st["ogp"], silu_og, bank_free)
            def exps(g):
                a, fwd, e = cum[g], g < 2, 2 * (g % 2)
                if g >= 2:
                    act.wait_ge(g_qk, g - 1)
                act.activation(ex[e][:], a[:, 0:S], ACT.Exp, scale=LOG_SCALE)
                act.activation(ex[e + 1][:], a[:, 0:S], ACT.Exp, scale=-LOG_SCALE).then_inc(g_ex, 1)
                if fwd:
                    act.activation(kendc[g][:], a[:, S:S + MEM], ACT.Exp, scale=-LOG_SCALE, bias=tot[:, g:g + 1])
                else:
                    act.activation(kendc[g][:], a[:, S:S + MEM], ACT.Exp, scale=LOG_SCALE)
                edge = CHUNK - 1 if fwd else 0
                act.activation(last[:, g, :], a[:, 0:S].rearrange("p (n c) -> p n c", c=CHUNK)[:, :, edge],
                               ACT.Exp, scale=LOG_SCALE)
                act.wait_ge(g_arg, g + 1)
                act.activation(arg[g % 2][:], arg[g % 2][:], ACT.Exp, scale=LOG_SCALE).then_inc(g_ex2, 1)

            def keep_kend(g):
                act.wait_ge(kend_mm, g + 1)
                act.activation(kendT[g][:], bank(7).rearrange("p (t c) -> p t c", c=P), ACT.Copy)
                act.activation(kendcT[g][:], bank(0, MEM).rearrange("p (t c) -> p t c", c=P), ACT.Copy).then_inc(kend_kept, 1)
            act.wait_ge(g_cum, 4)
            exps(0)
            exps(1)
            keep_kend(0)
            exps(2)
            keep_kend(1)
            exps(3)
            keep_kend(2)
            keep_kend(3)
            for s_ in range(1, G_HEADS + 2):
                h = s_ - 1
                if h < G_HEADS:
                    act.wait_ge(o_mm, h + 1)
                    own.step(act.activation(oG[h][:], bank(h % 2), ACT.Copy))
                    if h >= 2:
                        act.wait_ge(gh_y, h - 1)
                    act.activation(tmp[2 + h % 2][:], oG[h][:], ACT.Square).then_inc(o_sq, 1)
                if s_ <= 3:
                    act.wait_ge(f_arg, s_)
                    act.activation(fh[(s_ - 1) % 2][:], ft[0][:], ACT.Sin).then_inc(f_sin, 1)
                h = s_ - 2
                if 0 <= h:
                    act.wait_ge(gh_v, h + 1)
                    act.activation(tmp[2 + h % 2][:], tmp[2 + h % 2][:], ACT.Sqrt).then_inc(gh_r, 1)

            for tt in range(HT):
                act.wait_ge(ab_done, tt + 1)
                act.activation(tmp[tt][:], ab[:, 0, tt, :], ACT.Square)
                act.activation(decay[:, tt, :], ab[:, 1, tt, :], ACT.Square).then_inc(ab_sq, 1)
                for j in range(2):
                    ins = act.activation(abH[:, j, tt, :], ab[:, j, tt, :], ACT.Copy)
                ins.then_inc(ab_h, 1)
            follow(st["sa"])
            follow(st["sb"])
            act.wait_ge(nrm_v, 1)
            act.activation(nrm[:], nrm[:], ACT.Sqrt).then_inc(nrm_r, 1)
            for tt in range(HT):
                act.wait_ge(wt_mm, tt + 1)
                act.activation(wtH[:, tt, :], bank(3 + tt), ACT.Copy).then_inc(wt_h, 1)
            for i in range(8):
                high_at(st["uu"].base + i + SLOTS)
                if i >= 4:
                    k = i - 4
                    act.wait_ge(y_t, k + 1)
                    act.activation(YH[:, k, :], tmp[2 * (k % 2)][:], ACT.Copy)
                    act.activation(YH[:, HT + k, :], tmp[2 * (k % 2) + 1][:], ACT.Copy).then_inc(y_h, 1)
            for k in range(HT):
                act.activation(yH[:, HT + k, :], og[:, k, :], ACT.Copy).then_inc(og_h, 1)
            follow(st["inv"])
            for c in range(HT):
                act.wait_ge(yc_ok, c + 1)
                act.activation(yH[:, c, :], tmp[2 + c % 2][:], ACT.Copy).then_inc(yc_h, 1)
            follow(st["wo"])
            stat("mlp2", r)
            modulate(16, S, lambda k: mod[:, 24 + k, 0:1], hH)
            for name in ("m1_0", "m1_1", "m2_0", "m1_2", "m2_1", "m1_3", "m2_2", "m2_3"):
                follow(st[name])
            finish("fin2")

        @block.tensor
        def _(pe):
            def prep_tile(src, tiles, n0, k):
                if k >= 2:
                    pe.wait_ge(x_c, n0 + k - 1)
                for i in range(tiles):
                    ins = pe.transpose(ps[:, 3 + k % 2, i * P:(i + 1) * P], src[:, i, k * P:(k + 1) * P], ident[:])
                ins.then_inc(x_t, 1)

            def prep(src, tiles, n0):
                for k in range(DT):
                    prep_tile(src, tiles, n0, k)

            def stat(name, ready, value, n=S):
                pe.wait_ge(ready, value)
                pe.matmul(bank(7, n), ones[:], acc[:, 0:n], start=True, stop=True).then_inc(stat_sum, 1)

            def unit(pos, stage, rh, rl, n=S, m=P, extra=None):
                pe.wait_ge(low_done, pos.u + 1)
                if not isinstance(pos.u, int) or pos.u >= SLOTS:
                    pe.wait_ge(bank_free, pos.u - (SLOTS - 1))
                for dst, rh_, rl_, n_ in [(bank(pos.slot, n, m), rh, rl, n)] + ([extra(pos)] if extra else []):
                    k = 0
                    for w, a in ((WH, rh_), (WH, rl_), (WL, rh_)):
                        for q in range(stage.kt):
                            ins = pe.matmul(dst, w[pos.slot][:, q, 0:m], a[:, q, :], start=(k == 0),
                                            stop=(k == 3 * stage.kt - 1))
                            k += 1
                ins.then_inc(unit_done, 1)

            def opening(name, rh, rl, order, ready, group):
                stage = st[name]
                first = [Pos(stage, 0, j, 0) for j in range(group)]
                pe.wait_ge(low_done, stage.base + group)
                if stage.base:
                    pe.wait_ge(bank_free, stage.base - SLOTS + group)
                for c, (value, q) in enumerate(order):
                    if value:
                        pe.wait_ge(ready, value)
                    for pos in first:
                        for e, (w, a) in enumerate(((WH, rh), (WH, rl), (WL, rh))):
                            ins = pe.matmul(bank(pos.slot), w[pos.slot][:, q, :], a[:, q, :],
                                            start=(c == 0 and e == 0), stop=(c == stage.kt - 1 and e == 2))
                        if c == stage.kt - 1:
                            ins.then_inc(unit_done, 1)

            def after_opening(name, rh, rl, order, ready, group=1):
                opening(name, rh, rl, order, ready, group)
                units(name, rh, rl, S, group)

            def tiles(n0=0, n=DT):
                return [(n0 + k + 1, k) for k in range(n)]

            def units(name, rh, rl, n=S, lo=0, hi=None):
                stage = st[name]
                each_unit(pe, stage, lambda pos: unit(pos, stage, rh, rl, n), lo, hi)

            def finish(stat_name):
                for k in range(DT):
                    pe.wait_ge(fin_h, k + 1)
                    if k >= 2:
                        pe.wait_ge(fin_c, k - 1)
                    for i in range(ST):
                        ins = pe.transpose(ps[:, 3 + k % 2, i * P:(i + 1) * P], tmp[k % 2][:, i * P:(i + 1) * P], ident[:])
                    ins.then_inc(fin_t, 1)

            pe.wait_ge(tok_in, 32)
            prep(tok, ST, 0)
            pe.wait_ge(const_in, CONSTS_IN)
            pe.wait_ge(vec_in, 16 * len(VEC_ROWS))
            pe.transpose(ps[:, 0, 0:VEC_SPLIT], vecload[0:VEC_SPLIT, 0, :], ident[0:VEC_SPLIT, 0:VEC_SPLIT])
            n = VECS - VEC_SPLIT
            pe.transpose(ps[:, 1, 0:n], vecload[0:n, 1, :], ident[0:n, 0:n]).then_inc(vec_t, 1)
            stat("x", x_acc, DT)
            pe.wait_ge(rel_back, 16)
            for h in range(B_HEADS):
                if h >= 2:
                    pe.wait_ge(bias_ok, h - 1)
                for b in range(ST):
                    d = ST - 1 - b
                    ins = pe.matmul(ps[:, 5 + h % 2, b * P:(b + 1) * P], hankel[:, h, d * P:(d + 1) * P],
                                    anti[:], start=(b == 0), stop=True, skip_group_check=True)
                ins.then_inc(rel_mm, 1)
            stage = st["rope"]
            for i in range(stage.n + 1):
                if i == 0:
                    opening("rope", hH, hL, tiles(), h_ok, 2)
                elif 1 < i < stage.n:
                    unit(Pos(stage, 0, i, 0), stage, hH, hL)
                if i >= 1:
                    pe.wait_ge(bank_free, stage.base + i)
                    if i >= 3:
                        pe.wait_ge(roped, i - 2)
                    pe.matmul(bank(3 + (i - 1) % 2), swap[:], tmp[(i - 1) % 2][:], start=True, stop=True).then_inc(rot_done, 1)

            def turn_v(n0, i, tt=ST, src=None):
                pe.wait_ge(bank_free, n0[0] + i + 1)
                c = n0[1] + i
                if c >= 2:
                    pe.wait_ge(v_kept, c - 1)
                for q in range(tt):
                    ins = pe.transpose(ps[:, 5 + c % 2, q * P:(q + 1) * P], tmp[i % 2][:, q * P:(q + 1) * P], ident[:])
                ins.then_inc(v_turned, 1)

            def values(name, rh, rl, c0, n=S):
                stage = st[name]
                for i in range(stage.n + 1):
                    if i < stage.n:
                        unit(Pos(stage, 0, i, 0), stage, rh, rl, n)
                    if i >= 1:
                        turn_v((stage.base, c0), i - 1, n // P)

            values("va", hH, hL, 0)
            units("qkb", hH, hL)
            values("vb", hH, hL, 4)
            units("gate", hH, hL)

            def ada(i):
                u = st["ada"].base + i
                pe.wait_ge(low_done, u + 1)
                if i % 4 == 0 and i:
                    pe.wait_ge(bank_free, u)
                for q in range(2):
                    for w in (WH, WL):
                        k = 2 * (i % 4) + q
                        ins = pe.matmul(bank(1, S, 4), cR[:, k, :], wide(w[u % SLOTS])[:, q, :],
                                        start=(k == 0 and w is WH), stop=(k == DT - 1 and w is WL))
                ins.then_inc(unit_done, 1)

            def attend(kind):
                items, lag, _ahead = ATT[kind]
                for s_ in range(items + lag + 2):
                    if s_ < items:
                        n, h, qt = s_, s_ // ST, s_ % ST
                        nk = keys_of(kind, qt) * P
                        q = slice(qt * P, (qt + 1) * P)
                        if kind == "a":
                            if n >= 2:
                                pe.wait_ge(exped["a"], n - 1)
                            for c in range(2):
                                rows = slice(64 * c, 64 * c + 64)
                                dst = ps[:, 3 + 2 * (n % 2) + c, 0:nk]
                                pe.matmul(dst, qA[rows, h, q], kA[rows, h, 0:nk], start=True, stop=True)
                                ins = pe.matmul(dst[:, nk - CHUNK:nk], mask_row[0:1, 0:P], mask_row[0:1, P:P + CHUNK],
                                                start=False, stop=True, skip_group_check=True)
                        elif kind == "b":
                            if n >= 4:
                                pe.wait_ge(maxed["b"], n - 3)
                            rows = slice(64 * (h % 2), 64 * (h % 2) + 64)
                            ins = pe.matmul(bank(3 + n % 4, nk), qB[rows, h // 2, q], kB[rows, h // 2, 0:nk],
                                            start=True, stop=True)
                        else:
                            if n >= 4:
                                pe.wait_ge(exped["c"], n - 3)
                            for j in range(2):
                                ins = pe.matmul(bank(3 + n % 4, nk), qc[:, 2 * h + j, q], kc[:, 2 * h + j, :],
                                                start=(j == 0), stop=(j == 1))
                        ins.then_inc(scored[kind], 1)
                        head = s_ // ST if kind == "b" and s_ % ST == 0 and s_ // ST < A_HEADS else None
                        if head is not None:
                            pe.wait_ge(head_sq, head + 1)
                            pe.wait_ge(bank_free, st["ada"].base + A_HEADS * ST + s_)
                            pe.matmul(bank(1), ones[:], tmp[head][:], start=True, stop=True).then_inc(head_mm, 1)
                        elif kind != "c":
                            ada(s_ + (0 if kind == "a" else A_HEADS * ST))
                    m = s_ - lag
                    if 0 <= m < items:
                        pe.wait_ge(normed[kind], m + 1)
                        if m >= 2:
                            pe.wait_ge(kept[kind], m - 1)
                        src = {"a": lambda c: pA[m % 2][:, 0, c], "b": lambda c: pB[m % 4][:, c],
                               "c": lambda c: pC[m % 4][:, c]}[kind]
                        for b in range(keys_of(kind, m % ST)):
                            ins = pe.transpose(ps[:, (7, 2)[m % 2], b * P:(b + 1) * P], src(slice(b * P, (b + 1) * P)), ident[:])
                        ins.then_inc(turned[kind], 1)
                    if m >= ST and m % ST == 1:
                        h = m // ST - 1
                        pe.wait_ge(kept[kind], ST * (h + 1))
                        if kind == "c":
                            if h >= 1:
                                pe.wait_ge(pv_out["c"], 2 * h)
                            for j in range(2):
                                c = slice((2 * h + j) * P, (2 * h + j + 1) * P)
                                for b in range(2):
                                    ins = pe.matmul(bank(j), vc[:, b, c], pcT[h % 2][:, b, :], start=(b == 0), stop=(b == 1))
                        else:
                            if kind == "a":
                                if h >= 1:
                                    pe.wait_ge(pv_out["a"], h)
                                v, c, rows = vA, slice(h * P, (h + 1) * P), slice(0, P)
                            else:
                                if h >= 2 and h % 2 == 0:
                                    pe.wait_ge(pv_out["b"], h // 2)
                                v, c, rows = vB, slice(h * B_DH, (h + 1) * B_DH), slice(64 * (h % 2), 64 * (h % 2) + 64)
                            for b in range(ST):
                                ins = pe.matmul(ps[rows, 0, b * P:S], v[:, b, c], attT[h % 2][:, b, b * P:S],
                                                start=(b == 0), stop=True, skip_group_check=True)
                        ins.then_inc(pv_done[kind], 1)
                    if s_ < items and head is not None:
                        pe.wait_ge(head_v, head + 1)
                        ada(A_HEADS * ST + s_)

            pe.wait_ge(bank_free, st["ada"].base)
            pe.wait_ge(roped, 8)
            pe.wait_ge(v_kept, 8)
            pe.wait_ge(bias_ok, B_HEADS + 1)
            pe.wait_ge(cond_ok, 1)
            attend("a")
            pe.wait_ge(pv_out["a"], A_HEADS)
            attend("b")
            stage = st["up"]
            for i in range(2 * DT):
                c = slice(4 * (i % 2), 4 * (i % 2) + 4)
                if i == 0:
                    opening("up", hH[:, c], hL[:, c], tiles(0, 4), y_ok, 1)
                    continue
                if i == 1:
                    pe.wait_ge(y_ok, DT)
                    pe.wait_ge(mem_in, 16)
                unit(Pos(stage, i // 6, i % 6, 0), stage, hH[:, c], hL[:, c])
                if i % 2:
                    prep_tile(memtok, 2, 8, i // 2)
            pe.wait_ge(mod_in, 16)
            for c in range(4):
                ins = pe.transpose(ps[:, 5, c * 48:(c + 1) * 48], mod_rows[:, c, :], ident[0:48, 0:48])
            ins.then_inc(mod_mm, 1)
            opening("out", mgH, mgL, tiles(), res["up"], 1)
            pe.wait_ge(x_acc, 2 * DT)
            pe.matmul(bank(6, MEM), ones[:], mem_acc[:], start=True, stop=True).then_inc(stat_sum, 1)
            units("out", mgH, mgL, S, 1)
            units("mk", memH, memL, MEM, 0, 3)
            stat("cross", res["out"], DT)
            units("mk", memH, memL, MEM, 3)
            values("mv", memH, memL, 8, MEM)
            for i in range(DT):
                unit(Pos(st["cq"], i // 3, i % 3, 0), st["cq"], hH, hL)
                if i == 1:
                    pe.wait_ge(ctx_in, 16)
                if i:
                    prep_tile(ctxtok, 2, 16, i - 1)
            prep_tile(ctxtok, 2, 16, DT - 1)
            stat("ctx", x_acc, 3 * DT, MEM)
            pe.wait_ge(bank_free, st["co"].base)
            pe.wait_ge(v_kept, 16)
            attend("c")
            pe.wait_ge(pv_out["c"], 2 * X_HEADS)
            units("co", oH, oL)
            opening("gu", hH, hL, tiles(), res["co"], 1)
            stat("ffn", res["co"], DT)
            units("gu", hH, hL, S, 1)
            pe.wait_ge(res["gu"], 15)
            units("dn0", fH[:, 0:8], fL[:, 0:8])
            units("dn1", fH[:, 8:15], fL[:, 8:15])
            pe.wait_ge(res["gu"], FT)
            units("dn2", fH[:, 15:22], fL[:, 15:22])
            stat("fin1", res["dn2"], DT)
            pe.matmul(bank(6), ones[:], acc2[:], start=True, stop=True).then_inc(stat_sum, 1)
            after_opening("hyp", hH, hL, tiles(), md_ok, 2)
            pe.wait_ge(md_ok, 2 * DT)

            def with_context(name):
                stage = st[name]
                return lambda pos: unit(pos, stage, hH, hL, S, width(stage),
                                        lambda pos: (bank(3 + pos.slot, MEM, width(stage)), cH, cL, MEM))
            def gate_mm(g):
                if g:
                    pe.wait_ge(g_y, g)
                w = gate_w[:, g // 2, (g % 2) * P:(g % 2 + 1) * P]
                pe.matmul(bank(6), w, gr[:, 0:S], start=True, stop=True)
                pe.matmul(bank(7, MEM), w, gr[:, S:S + MEM], start=True, stop=True).then_inc(g_mm, 1)
            each_unit(pe, st["grp"], with_context("grp"))
            pe.wait_ge(gate_in, 32)
            for i in range(2):
                unit(Pos(st["qp"], 0, i, 0), st["qp"], hH, hL)
                if i == 0:
                    pe.wait_ge(bank_free, st["qp"].base)
                gate_mm(i)
            for i in range(2):
                with_context("kp")(Pos(st["kp"], 0, i, 0))
                gate_mm(2 + i)
            pe.wait_ge(g_y, 4)
            stage = st["vp"]
            one = with_context("vp")
            for i in range(stage.n + 1):
                if i < stage.n:
                    one(Pos(stage, 0, i, 0))
                if i >= 1:
                    c = i - 1
                    pe.wait_ge(bank_free, stage.base + c + 1)
                    pe.wait_ge(v_kept, 16 + c)
                    for q in range(ST):
                        pe.transpose(ps[:, 6, q * P:(q + 1) * P], vfT[c % 2][:, q * P:(q + 1) * P], ident[:])
                    for q in range(2):
                        ins = pe.transpose(ps[:, 7, q * P:(q + 1) * P], vfTc[c % 2][:, q * P:(q + 1) * P], ident[:])
                    ins.then_inc(v_turned, 1)
            units("ogp", hH, hL)
            pe.wait_ge(bank_free, st["sa"].base)
            pe.wait_ge(v_kept, 20)
            for g in range(4):
                pe.wait_ge(g_done, g + 1)
                if g >= 1:
                    pe.wait_ge(kend_kept, g)
                for q in range(ST):
                    pe.transpose(ps[:, 7, q * P:(q + 1) * P], kend[g][:, q * P:(q + 1) * P], ident[:])
                for q in range(2):
                    ins = pe.transpose(ps[:, 0, q * P:(q + 1) * P], kendc[g][:, q * P:(q + 1) * P], ident[:])
                ins.then_inc(kend_mm, 1)
            for g in range(4):
                pe.wait_ge(kend_kept, g + 1)
                if g >= 2:
                    pe.wait_ge(state_ok, g - 1)
                for half in range(2):
                    h = 2 * (g % 2) + half
                    rows = slice(64 * half, 64 * half + 64)
                    dv = slice(h * P, (h + 1) * P)
                    for b in range(2):
                        pe.matmul(ps[rows, 1 + g % 2, 0:P], kendcT[g][:, b, rows], vGc[:, b, dv],
                                  start=(b == 0), stop=(b == 1), skip_group_check=True)
                    for n in range(NCH):
                        tok_rows = slice(64 * (n % 2), 64 * (n % 2) + 64)
                        c = n // 2
                        ins = pe.matmul(ps[rows, 3 + 2 * (g % 2) + n % 2, c * P:(c + 1) * P],
                                        kendT[g][tok_rows, n // 2, rows], vG[tok_rows, n // 2, dv],
                                        start=True, stop=True, skip_group_check=True)
                ins.then_inc(state_mm, 1)
            pe.wait_ge(state_ok, 4)
            for s_ in range(G_HEADS + 2):
                if s_ < G_HEADS:
                    h = s_
                    rows = slice(64 * (h % 2), 64 * (h % 2) + 64)
                    if h >= 2:
                        pe.wait_ge(att_ok, h - 1)
                    for d in range(2):
                        g = 2 * d + h // 2
                        for b in range(ST):
                            c = slice(b * P, (b + 1) * P)
                            ins = pe.matmul(ps[:, 3 + 2 * (h % 2) + d, c], kin[g][rows, c], qin[g][rows, c],
                                            start=True, stop=True, skip_group_check=True)
                    ins.then_inc(fb_mm, 1)
                h = s_ - 1
                if 0 <= h < G_HEADS:
                    rows = slice(64 * (h % 2), 64 * (h % 2) + 64)
                    pe.wait_ge(att_ok, h + 1)
                    if h >= 2:
                        pe.wait_ge(o_sq, h - 1)
                    for b in range(ST):
                        pe.matmul(ps[:, h % 2, b * P:(b + 1) * P], vG[:, b, h * P:(h + 1) * P],
                                  att[h % 2][:, b * P:(b + 1) * P], start=True, stop=True, skip_group_check=True)
                        for n in (2 * b, 2 * b + 1):
                            c = slice(n * CHUNK, (n + 1) * CHUNK)
                            for d in range(2):
                                g = 2 * d + h // 2
                                ins = pe.matmul(ps[:, h % 2, c], state[g][rows, n, :], qin[g][rows, c],
                                                start=False, stop=True, skip_group_check=True)
                    ins.then_inc(o_mm, 1)
                h = s_ - 2
                if 0 <= h < G_HEADS:
                    pe.wait_ge(o_sq, h + 1)
                    if h >= 1:
                        pe.wait_ge(gh_v, h)
                    pe.matmul(bank(7), ones[:], tmp[2 + h % 2][:], start=True, stop=True).then_inc(gh_mm, 1)
                if s_ == 0:
                    pe.wait_ge(filt_in, 16 * 10)
                    pe.matmul(bank(2, S, HID), fw[0:EMB, 0, :], zT[:], start=True, stop=True).then_inc(f_mm, 1)
                elif s_ <= 2:
                    pe.wait_ge(f_sin, s_)
                    pe.matmul(bank(2, S, HID), fw[:, s_, :], fh[(s_ - 1) % 2][:], start=True, stop=True).then_inc(f_mm, 1)

            pe.wait_ge(f_sin, 3)
            for tt in range(HT):
                if tt >= 2:
                    pe.wait_ge(ab_done, tt - 1)
                for j in range(2):
                    ins = pe.matmul(bank(3 + 2 * (tt % 2) + j), fh[0][:, tt * P:(tt + 1) * P],
                                    fout[:, j * D_HY:(j + 1) * D_HY], start=True, stop=True)
                ins.then_inc(f_out, 1)
            after_opening("sa", abH[:, 0], abL[:, 0], tiles(0, HT), ab_l, 2)
            units("sb", abH[:, 1], abL[:, 1])
            pe.wait_ge(gh_v, G_HEADS)
            pe.wait_ge(ab_sq, HT)
            for c in range(HT):
                for tt in range(HT):
                    for j in range(2):
                        src = (tmp[tt][:] if j == 0 else decay[:, tt, :])[:, c * P:(c + 1) * P]
                        ins = pe.matmul(ps[:, 7, c:c + 1], src, ones[:, 0:1], start=(tt == 0 and j == 0),
                                        stop=(tt == HT - 1 and j == 1), skip_group_check=True)
            ins.then_inc(nrm_mm, 1)
            pe.wait_ge(w_ok, HT)
            for tt in range(HT):
                for i in range(HT):
                    ins = pe.transpose(ps[:, 3 + tt, i * P:(i + 1) * P], wk[:, i, tt * P:(tt + 1) * P], ident[:])
                ins.then_inc(wt_mm, 1)
            pe.wait_ge(wt_l, HT)
            units("uu", wtH, wtL)
            after_opening("inv", YH, YL, [(k + 1 if not j else 0, HT * j + k) for k in range(HT) for j in range(2)], y_l, 2)
            pe.wait_ge(bank_free, st["wo"].base)
            for c in range(HT):
                for tt in range(HT):
                    ins = pe.transpose(ps[:, 3 + c, tt * P:(tt + 1) * P], yt[:, tt, c * P:(c + 1) * P], ident[:])
                ins.then_inc(yt_mm, 1)
            after_opening("wo", yH, yL, [(k + 1, (k + HT) % DT) for k in range(DT)], y2_ok, 2)
            stat("mlp2", res["wo"], DT)
            for name, q in (("m1_0", 0), ("m1_1", 1), ("m2_0", 0), ("m1_2", 2), ("m2_1", 1), ("m1_3", 3),
                            ("m2_2", 2), ("m2_3", 3)):
                if name == "m1_0":
                    after_opening(name, hH, hL, tiles(2 * DT), md_ok, 2)
                elif name[1] == "1":
                    units(name, hH, hL)
                else:
                    after_opening(name, mH[q % 2], mL[q % 2], tiles(DT * q), res["m1"])
            stat("fin2", res["m2_3"], DT)
            finish("fin2")

        @block.vector
        def _(dve):
            own = Own(dve, own_v)

            def taken(u):
                dve.wait_ge(bank_free, u + 1)

            def stat(name, n=S, at=7):
                dve.wait_ge(stat_sum, stat_no[name] + 1)
                own.step(dve.tensor_scalar(tmp[3][:, 0:n], bank(at, n), 1.0 / D, EPS, ALU.mult, ALU.add))
                dve.reciprocal(tmp[3][:, 0:n], tmp[3][:, 0:n]).then_inc(stat_v, 1)

            def split(src, dh, dl):
                own.step(dve.tensor_scalar(dh, src, 1.0, None, ALU.mult))
                return dve.tensor_tensor(dl, src, dh.bitcast(F32), ALU.subtract)

            def prep(tiles, n0):
                n = tiles * P
                own.step(dve.memset(acc[:], 0.0))
                for k in range(DT):
                    dve.wait_ge(x_sq, n0 + k + 1)
                    dve.tensor_tensor(acc[:, 0:n], acc[:, 0:n], tmp[2 + k % 2][:, 0:n], ALU.add).then_inc(x_acc, 1)
                    dve.wait_ge(x_acc, n0 + k + 1)

            def finish(stat_name, g):
                stat(stat_name)
                dve.wait_ge(stat_r, stat_no[stat_name] + 1)
                for k in range(DT):
                    if k >= 2:
                        dve.wait_ge(fin_t, k - 1)
                    dve.scalar_tensor_tensor(tmp[k % 2][:], x[:, k, :], vcol(g, k), r[:], ALU.mult, ALU.mult).then_inc(fin_h, 1)

            dve.wait_ge(rel_in, 16)
            dve.tensor_copy(rel_ext[:, REL:768], rel_ext[:, REL - 1:REL].to_broadcast([B_HEADS, 768 - REL])).then_inc(rel_ok, 1)
            prep(ST, 0)
            stat("x")
            dve.wait_ge(vec_t, 1)
            own.step(dve.tensor_copy(vec[:, 0:VEC_SPLIT], ps[:, 0, 0:VEC_SPLIT]))
            own.step(dve.tensor_copy(vec[:, VEC_SPLIT:VECS], ps[:, 1, 0:VECS - VEC_SPLIT]))
            dve.tensor_scalar(vcol("subln_g"), vcol("subln_g"), 1.0 - LAM_INIT, None, ALU.mult).then_inc(vec_ok, 1)
            dve.wait_ge(vec_ok, 1)
            for k in range(DT):
                if k >= 2:
                    dve.wait_ge(h_ok, k - 1)
                own.step(dve.tensor_scalar(tmp[k % 2][:], x[:, k, :], vcol("norm_mix_g", k), None, ALU.mult))
                split(tmp[k % 2][:], hH[:, k, :], hL[:, k, :]).then_inc(h_ok, 1)
            dve.wait_ge(h_ok, DT)
            dve.wait_ge(lam_in, 64)
            for c in range(2):
                own.step(dve.tensor_tensor(lam_parts[:, 2 * c, :], lam_parts[:, 2 * c, :], lam_parts[:, 2 * c + 1, :], ALU.mult))
                dve.reduce_sum(lam_s[:, c:c + 1], lam_parts[:, 2 * c, :], AX.X).then_inc(lam_ok, 1)
            dve.wait_ge(lam_exp, 1)
            own.step(dve.tensor_tensor(lam_s[:, 6:7], lam_s[:, 3:4], lam_s[:, 2:3], ALU.subtract))
            own.step(dve.tensor_scalar(lam_s[:, 7:8], lam_s[:, 6:7], -LAM_INIT, None, ALU.add))
            dve.wait_ge(bias_ok, B_HEADS)
            dve.memset(bias_t[0:CHUNK, :, S - CHUNK:S], NEG * float(B_DH) ** 0.5).then_inc(bias_ok, 1)
            dve.wait_ge(stat_r, 1)
            dve.wait_ge(rope_in, 16)
            stage = st["rope"]
            for i in range(stage.n + 1):
                if i < stage.n:
                    u = stage.base + i
                    dve.wait_ge(unit_done, u + 1)
                    dve.tensor_tensor(tmp[i % 2][:], bank(u % SLOTS), r[:], ALU.mult).then_inc(bank_free, 1)
                    taken(u)
                if i >= 1:
                    k = i - 1
                    dve.wait_ge(rot_done, k + 1)
                    own.mark(dve.tensor_tensor(tmp[2][:], bank(3 + k % 2), rope[:, 1, :], ALU.mult))
                    own.step(dve.tensor_tensor(tmp[3][:], tmp[k % 2][:], rope[:, 0, :], ALU.mult))
                    dve.tensor_tensor((qA if k < 4 else kA)[:, k % 4, :], tmp[2][:], tmp[3][:], ALU.add).then_inc(roped, 1)
                    dve.wait_ge(roped, k + 1)

            def times_r(stage, dst, rr=r, n=S, buffers=None):
                def one(pos):
                    dve.wait_ge(unit_done, pos.u + 1)
                    if buffers:
                        buffers(pos)
                    dve.tensor_tensor(dst(pos), bank(pos.slot, n), rr[:, 0:n], ALU.mult).then_inc(bank_free, 1)
                return one

            def values(name, c0, rr=r, n=S):
                stage = st[name]
                for i in range(stage.n):
                    u = stage.base + i
                    dve.wait_ge(unit_done, u + 1)
                    if i >= 2:
                        dve.wait_ge(v_turned, c0 + i - 1)
                    dve.tensor_tensor(tmp[i % 2][:, 0:n], bank(u % SLOTS, n), rr[:, 0:n], ALU.mult).then_inc(bank_free, 1)
                dve.wait_ge(v_turned, c0 + stage.n)

            dve.wait_ge(silu_c, 2)
            own.step(dve.tensor_scalar(cR[:, :, 0:2], cS[:], 1.0, None, ALU.mult))
            dve.tensor_tensor(cR[:, :, 2:4], cS[:], cR[:, :, 0:2].bitcast(F32), ALU.subtract).then_inc(cond_ok, 1)
            values("va", 0)
            for half, dst in ((0, qB), (4, kB)):
                for i in range(4):
                    u = st["qkb"].base + half + i
                    dve.wait_ge(unit_done, u + 1)
                    dve.tensor_tensor(dst[:, i, :], bank(u % SLOTS), r[:], ALU.mult).then_inc(bank_free, 1)
            values("vb", 4)

            stage = st["gate"]

            def gate_buffer(pos):
                if not isinstance(pos.i, int) or pos.i >= SLOTS:
                    dve.wait_ge(sig_done, pos.i - (SLOTS - 1))
            each_unit(dve, stage, times_r(stage, lambda pos: tmp[pos.slot][:], buffers=gate_buffer), 0, 3)
            each_unit(dve, stage, times_r(stage, lambda pos: tmp[pos.slot][:], buffers=gate_buffer), 3)

            def attend(kind):
                items, lag, _ahead = ATT[kind]
                for s_ in range(items + lag + 5):
                    if s_ < items:
                        n, h, qt = s_, s_ // ST, s_ % ST
                        nk = keys_of(kind, qt) * P
                        k = 2 * (n % 4)
                        dve.wait_ge(scored[kind], n + 1)
                        if kind == "a":
                            own.step(dve.tensor_reduce(tiny[:, k:k + 2], ps[:, 3 + 2 * (n % 2):5 + 2 * (n % 2), 0:nk], AX.X, ALU.max))
                            dve.tensor_scalar(tiny[:, k:k + 2], tiny[:, k:k + 2], -(A_DK ** -0.5), None, ALU.mult).then_inc(maxed[kind], 1)
                        elif kind == "b":
                            if n >= 4:
                                dve.wait_ge(turned["b"], n - 3)
                            own.step(dve.tensor_tensor_reduce(
                                out=pB[n % 4][:, 0:nk], in0=bank(3 + n % 4, nk), in1=bias_t[:, h, S - nk:S],
                                scale=float(B_DH) ** -0.5, scalar=-3.0e38, op0=ALU.add, op1=ALU.max,
                                accum_out=tiny[:, k:k + 1]))
                            dve.tensor_scalar(tiny[:, k:k + 1], tiny[:, k:k + 1], -1.0, None, ALU.mult).then_inc(maxed[kind], 1)
                        else:
                            own.step(dve.tensor_reduce(tiny[:, k:k + 1], bank(3 + n % 4, nk), AX.X, ALU.max))
                            dve.tensor_scalar(tiny[:, k:k + 1], tiny[:, k:k + 1], -1.0 / 16, None, ALU.mult).then_inc(maxed[kind], 1)
                    n = s_ - 1
                    if 0 <= n < items:
                        nk = keys_of(kind, n % ST) * P
                        k = 2 * (n % 4)
                        dve.wait_ge(exped[kind], n + 1)
                        if kind == "a":
                            own.step(dve.reciprocal(tiny[:, 8 + k:10 + k], tiny[:, 8 + k:10 + k]))
                            own.step(dve.tensor_scalar(pA[n % 2][:, 1, 0:nk], pA[n % 2][:, 1, 0:nk], tiny[:, 9 + k:10 + k],
                                                       lam_s[:, 7:8], ALU.mult, ALU.mult))
                            dve.scalar_tensor_tensor(pA[n % 2][:, 0, 0:nk], pA[n % 2][:, 0, 0:nk], tiny[:, 8 + k:9 + k],
                                                     pA[n % 2][:, 1, 0:nk], ALU.mult, ALU.add).then_inc(normed[kind], 1)
                        else:
                            own.step(dve.reciprocal(tiny[:, 8 + k:9 + k], tiny[:, 8 + k:9 + k]))
                            p = (pB if kind == "b" else pC)[n % 4][:, 0:nk]
                            dve.tensor_scalar(p, p, tiny[:, 8 + k:9 + k], None, ALU.mult).then_inc(normed[kind], 1)
                    if kind == "b" and s_ % ST == 0 and s_ // ST < A_HEADS:
                        h = s_ // ST
                        dve.wait_ge(head_mm, h + 1)
                        own.step(dve.tensor_scalar(tmp[h][:], bank(1), 1.0 / P, EPS, ALU.mult, ALU.add))
                        dve.reciprocal(tmp[h][:], tmp[h][:]).then_inc(head_v, 1)
                    if kind == "b" and s_ % ST == 2 and s_ // ST < A_HEADS:
                        h = s_ // ST
                        dve.wait_ge(head_r, h + 1)
                        ins = dve.scalar_tensor_tensor(qA[:, h, :], qA[:, h, :], vcol("subln_g"), tmp[h][:], ALU.mult, ALU.mult)
                        if h == A_HEADS - 1:
                            ins.then_inc(head_n, 1)
                    m = s_ - lag - 3
                    if m >= ST and m % ST == 1 and m // ST <= items // ST:
                        h = m // ST - 1
                        if kind == "a":
                            dve.wait_ge(pv_done["a"], h + 1)
                            dve.tensor_copy(qA[:, h, :], bank(0)).then_inc(pv_out["a"], 1)
                        elif kind == "b" and h % 2 == 1:
                            dve.wait_ge(pv_done["b"], h + 1)
                            dve.tensor_copy(qB[:, h // 2, :], bank(0)).then_inc(pv_out["b"], 1)
                        elif kind == "c":
                            dve.wait_ge(pv_done["c"], h + 1)
                            for j in range(2):
                                own.step(dve.tensor_copy(tmp[j][:], bank(j)))
                                own.step(dve.tensor_scalar(oH[:, 2 * h + j, :], tmp[j][:], 1.0, None, ALU.mult))
                                dve.tensor_tensor(oL[:, 2 * h + j, :], tmp[j][:], oH[:, 2 * h + j, :].bitcast(F32),
                                                  ALU.subtract).then_inc(pv_out["c"], 1)
            attend("a")
            dve.wait_ge(pv_out["a"], A_HEADS)
            for h in range(A_HEADS):
                dve.tensor_tensor(tmp[h][:], qA[:, h, :], qA[:, h, :], ALU.mult).then_inc(head_sq, 1)
            attend("b")
            for k in range(DT):
                dve.wait_ge(y_high, k + 1)
                dve.tensor_tensor(hL[:, k, :], (qA if k < 4 else qB)[:, k % 4, :], hH[:, k, :].bitcast(F32),
                                  ALU.subtract).then_inc(y_ok, 1)
            dve.wait_ge(y_ok, DT)
            def memory_tile(k):
                m = mem_t[k % 2][:]
                dve.wait_ge(x_sq, 8 + k + 1)
                own.mark(dve.tensor_scalar(m, m, vcol("norm_mem_g", k), None, ALU.mult))
                own.settle()
                own.step(split(m, memH[:, k, :], memL[:, k, :]))
                dve.tensor_tensor(mem_acc[:], mem_acc[:], mem_sq[k % 2][:], ALU.add).then_inc(x_acc, 1)
                dve.wait_ge(x_acc, 8 + k + 1)
            own.step(dve.memset(mem_acc[:], 0.0))
            for k in range(DT):
                for half in range(2):
                    u = st["up"].base + 2 * k + half
                    dve.wait_ge(unit_done, u + 1)
                    dve.tensor_tensor(tmp[2 * half][:], bank(u % SLOTS), gates[:, half * DT + k, :], ALU.mult).then_inc(bank_free, 1)
                    taken(u)
                own.step(dve.tensor_tensor(tmp[3][:], tmp[0][:], tmp[2][:], ALU.add))
                split(tmp[3][:], mgH[:, k, :], mgL[:, k, :]).then_inc(res["up"], 1)
                dve.wait_ge(res["up"], k + 1)
                if k:
                    memory_tile(k - 1)
            memory_tile(DT - 1)

            def residual(stage, scale=None, g=None, squares=True, done=None, second=None):
                per = (4 if g else 4 if second else 1) if squares else 0
                if squares:
                    own.step(dve.memset(acc[:], 0.0))
                n0 = own.n

                def one(pos):
                    own.group(n0, pos.i, per)
                    xm = x[:, bass.ds(pos.i, 1), :][:, 0]
                    dve.wait_ge(unit_done, pos.u + 1)
                    if scale is None:
                        dve.tensor_tensor(xm, bank(pos.slot), xm, ALU.add).then_inc(bank_free, 1)
                    else:
                        dve.scalar_tensor_tensor(xm, bank(pos.slot), scale(pos.i), xm, ALU.mult, ALU.add).then_inc(bank_free, 1)
                    taken(pos.u)
                    if not squares:
                        return
                    own.mark(dve.tensor_tensor(tmp[0][:], xm, xm, ALU.mult))
                    if second:
                        own.step(dve.tensor_scalar(tmp[1][:], xm, vcol(second, pos.i), None, ALU.mult))
                        own.step(dve.tensor_tensor(tmp[1][:], tmp[1][:], tmp[1][:], ALU.mult))
                        own.mark(dve.tensor_tensor(acc2[:], acc2[:], tmp[1][:], ALU.add))
                    if g is None:
                        own.settle()
                        dve.tensor_tensor(acc[:], acc[:], tmp[0][:], ALU.add).then_inc(res[done], 1)
                        dve.wait_ge(res[done], pos.i + 1)
                        return
                    own.step(dve.tensor_scalar(tmp[1][:], xm, vcol(g, pos.i), None, ALU.mult))
                    own.mark(dve.tensor_tensor(acc[:], acc[:], tmp[0][:], ALU.add))
                    h_, l_ = (y_[:, bass.ds(pos.i, 1), :][:, 0] for y_ in (hH, hL))
                    split(tmp[1][:], h_, l_).then_inc(res[done], 1)
                    dve.wait_ge(res[done], pos.i + 1)
                each_unit(dve, stage, one)
                own.leave(n0 + per * stage.n)

            dve.wait_ge(mod_mm, 1)
            for c in range(2):
                own.step(dve.tensor_tensor(mod[:, :, c], ps[:, 5, c * 48:(c + 1) * 48],
                                           vec[:, VEC_AT["b_ada_2"]:VEC_AT["b_ada_2"] + 48], ALU.add))
                ins = dve.tensor_tensor(mod[:, :, c], ps[:, 5, (2 + c) * 48:(3 + c) * 48], mod[:, :, c], ALU.add)
                if c == 0:
                    own.step(ins)
            ins.then_inc(mod_ok, 1)
            stat("mem", MEM, 6)
            dve.wait_ge(stat_r, 2)
            residual(st["out"], g="norm_cross_g", done="out")
            def context_tile(k):
                dve.wait_ge(x_sq, 16 + k + 1)
                dve.tensor_tensor(acc[:, 0:MEM], acc[:, 0:MEM], tmp[2 + k % 2][:, 0:MEM], ALU.add).then_inc(x_acc, 1)
                dve.wait_ge(x_acc, 16 + k + 1)

            stage = st["mk"]
            one = times_r(stage, lambda pos: kc[:, bass.ds(pos.i, 1), :][:, 0], rm, MEM)
            each_unit(dve, stage, one, 0, 3)
            stat("cross")
            each_unit(dve, stage, one, 3)
            values("mv", 8, rm, MEM)
            dve.wait_ge(stat_r, 3)
            stage = st["cq"]
            own.step(dve.memset(acc[:], 0.0))
            for i in range(DT + 1):
                if i < DT:
                    u = stage.base + i
                    dve.wait_ge(unit_done, u + 1)
                    dve.tensor_tensor(qc[:, i, :], bank(u % SLOTS), r[:], ALU.mult).then_inc(bank_free, 1)
                if i:
                    context_tile(i - 1)
            stat("ctx", MEM)
            dve.wait_ge(stat_r, stat_no["ctx"] + 1)
            attend("c")
            for c, (name, m, col) in enumerate((("norm_mix_2", 8, 0), ("norm_mix_2", 8, 1), ("norm_mlp_2", 32, 0))):
                own.mark(dve.scalar_tensor_tensor(gain[:, c, :], mod[:, m:m + DT, col], 1.0,
                                                  vec[:, VEC_AT[name]:VEC_AT[name] + DT], ALU.add, ALU.mult))
            own.settle()
            c = VEC_AT["norm_final_g"]
            own.step(dve.tensor_tensor(gain[:, 3, :], gain[:, 0, :], vec[:, c:c + DT], ALU.mult))
            residual(st["co"], g="norm_ffn_g", done="co")
            stat("ffn")
            dve.wait_ge(stat_r, stat_no["ffn"] + 1)
            n0 = own.n

            def swiglu(pos):
                dve.wait_ge(unit_done, pos.u + 1)
                if (pos.lo + pos.j) % 2 == 0:
                    dve.tensor_tensor(tmp[pos.slot][:], bank(pos.slot), r[:], ALU.mult).then_inc(bank_free, 1)
                else:
                    own.group(n0, pos.pair, 2)
                    dve.tensor_tensor(tmp[3][:], bank(pos.slot), r[:], ALU.mult).then_inc(bank_free, 1)
                    taken(pos.u)
                    dve.wait_ge(silu_done, pos.pair + 1)
                    own.step(dve.tensor_tensor(tmp[3][:], tmp[3][:], tmp[(pos.slot - 1) % SLOTS][:], ALU.mult))
                    h_, l_ = (y_[:, bass.ds(pos.pair, 1), :][:, 0] for y_ in (fH, fL))
                    split(tmp[3][:], h_, l_).then_inc(res["gu"], 1)
                    dve.wait_ge(res["gu"], pos.pair + 1)
            each_unit(dve, st["gu"], swiglu)
            own.leave(n0 + 2 * FT)
            residual(st["dn0"], squares=False)
            residual(st["dn1"], squares=False)
            own.step(dve.memset(acc2[:], 0.0))
            residual(st["dn2"], done="dn2", second="norm_final_g")
            dve.wait_ge(stat_sum, stat_no["mix2"] + 1)
            own.step(dve.tensor_scalar(tmp[2][:], bank(7), 1.0 / D, EPS, ALU.mult, ALU.add))
            dve.reciprocal(tmp[2][:], tmp[2][:]).then_inc(stat_v, 1)
            dve.wait_ge(stat_v, stat_no["fin1"] + 1)
            own.step(dve.scalar_tensor_tensor(tmp[3][:], bank(6), 1.0 / D, tmp[2][:], ALU.mult, ALU.mult))
            own.step(dve.tensor_scalar(tmp[3][:], tmp[3][:], EPS, None, ALU.add))
            dve.reciprocal(tmp[3][:], tmp[3][:]).then_inc(stat_v, 1)
            dve.wait_ge(stat_r, stat_no["mix2"] + 1)
            own.step(dve.tensor_tensor(acc[:], r[:], r2[:], ALU.mult))

            def modulate(n0, src, rr, n, which, shift, dh, dl):
                for k in range(DT + 1):
                    if k < DT:
                        if n0 + k >= 3:
                            dve.wait_ge(md_ok, n0 + k - 2)
                        dve.scalar_tensor_tensor(tmp[k % 3][:, 0:n], src[:, k, :], gain[:, which, k:k + 1], rr[:, 0:n],
                                                 ALU.mult, ALU.mult).then_inc(md_t, 1)
                    if k >= 1:
                        q = k - 1
                        dve.wait_ge(md_h, n0 + k)
                        dve.scalar_tensor_tensor(dl[:, q, :], tmp[q % 3][:, 0:n], shift(q), dh[:, q, :].bitcast(F32),
                                                 ALU.add, ALU.subtract).then_inc(md_ok, 1)
                dve.wait_ge(md_ok, n0 + DT)
            modulate(0, x, acc, S, 3, lambda k: mod[:, k, 0:1], hH, hL)
            def copies(name, dst, scale=1.0, also=None, lo=0, hi=None):
                def one(pos):
                    dve.wait_ge(unit_done, pos.u + 1)
                    ins = dve.tensor_scalar(dst(pos), bank(pos.slot, S, width(st[name])), scale, None, ALU.mult)
                    if also:
                        ins = dve.tensor_scalar(also(pos), bank(3 + pos.slot, MEM, width(st[name])), scale, None, ALU.mult)
                    ins.then_inc(bank_free, 1)
                each_unit(dve, st[name], one, lo, hi)
            copies("hyp", lambda pos: hy[:, bass.ds(pos.i, 1), :][:, 0], hi=SLOTS)
            for k in range(DT):
                own.mark(dve.scalar_tensor_tensor(x[:, k, :], x[:, k, :], vcol("norm_final_g", k), r[:], ALU.mult, ALU.mult))
            modulate(8, ctxT, rc, MEM, 1, lambda k: mod[:, k, 1:2], cH, cL)
            copies("hyp", lambda pos: hy[:, bass.ds(pos.i, 1), :][:, 0], lo=SLOTS)
            copies("grp", lambda pos: gr[:, 0:S], 1.0, lambda pos: gr[:, S:S + MEM])
            dve.wait_ge(gla_in, 32)

            def gate_in_(g):
                dve.wait_ge(g_mm, g + 1)
                bias = vcol("gk_b_fwd_2" if g < 2 else "gk_b_bwd_2", g % 2)
                if g >= 2:
                    dve.wait_ge(g_cum, g - 1)
                dve.tensor_scalar(lg[g % 2][:], ps[:, 6:8, :].rearrange("p a b -> p (a b)")[:, 0:S + MEM],
                                  bias, None, ALU.add).then_inc(g_y, 1)

            def sums(g):
                a, b = cum[g], lg[g % 2]
                dve.wait_ge(g_ln, g + 1)
                own.step(dve.scalar_tensor_tensor(b[:], b[:], 0.0, a[:], ALU.min, ALU.subtract))
                if g < 2:
                    own.mark(dve.tensor_tensor_scan(a[:, 0:S], reset[:], b[:, 0:S], 0.0, ALU.mult, ALU.add))
                else:
                    own.mark(dve.tensor_tensor_scan(a[:, 0:S][:, ::-1], reset[:], b[:, 0:S][:, ::-1], 0.0, ALU.mult, ALU.add))
                own.step(dve.tensor_tensor_scan(a[:, S:S + MEM], ones[:, 0:1].to_broadcast([P, MEM]), b[:, S:S + MEM],
                                                0.0, ALU.mult, ALU.add))
                if g < 2:
                    dve.tensor_scalar(tot[:, g:g + 1], a[:, S + MEM - 1:S + MEM], LOG_SCALE, None, ALU.mult).then_inc(g_cum, 1)
                else:
                    dve.tensor_tensor(a[:, S:S + MEM], a[:, S:S + MEM], b[:, S:S + MEM], ALU.subtract).then_inc(g_cum, 1)

            def copy_unit(name, i, dst, scale=1.0, also=None):
                u = st[name].base + i
                dve.wait_ge(unit_done, u + 1)
                ins = dve.tensor_scalar(dst, bank(u % SLOTS), scale, None, ALU.mult)
                if also is not None:
                    ins = dve.tensor_scalar(also, bank(3 + u % SLOTS, MEM), scale, None, ALU.mult)
                ins.then_inc(bank_free, 1)
            copy_unit("qp", 0, qG[:, 0, :], 64 ** -0.5)
            gate_in_(0)
            copy_unit("qp", 1, qG[:, 1, :], 64 ** -0.5)
            gate_in_(1)
            sums(0)
            copy_unit("kp", 0, kG[:, 0, :], 1.0, kGc[:, 0, :])
            gate_in_(2)
            sums(1)
            copy_unit("kp", 1, kG[:, 1, :], 1.0, kGc[:, 1, :])
            gate_in_(3)
            sums(2)
            def conv(tile):
                t_, src = tmp[tile % 4][:], hy[:, tile, :]
                t3, s3 = (a.rearrange("p (r c) -> p r c", c=CHUNK) for a in (t_, src))
                w = [vcol("conv_w_2", 12 * j + tile) for j in range(3)]
                b = vcol("conv_b_2", tile)
                own.mark(dve.tensor_scalar(t3[:, :, 1:CHUNK], s3[:, :, 0:CHUNK - 1], w[0], b, ALU.mult, ALU.add))
                own.step(dve.tensor_scalar(t3[:, :, 0:1], s3[:, :, 1:2], w[2], b, ALU.mult, ALU.add))
                own.step(dve.scalar_tensor_tensor(t3[:, :, 1:CHUNK - 1], s3[:, :, 2:CHUNK], w[2], t3[:, :, 1:CHUNK - 1], ALU.mult, ALU.add))
                own.step(dve.scalar_tensor_tensor(src, src, w[1], t_, ALU.mult, ALU.add))

            for i in range(4):
                if i >= 2:
                    dve.wait_ge(v_turned, 16 + i - 1)
                copy_unit("vp", i, vfT[i % 2][:], 1.0, vfTc[i % 2][:])
                if i == 0:
                    sums(3)
                conv(i)
                conv(4 + i)
            for i in range(4):
                copy_unit("ogp", i, og[:, i, :])
                conv(8 + i)
                dve.tensor_tensor(wk[:, i, :], wk[:, i, :], hy[:, 8 + i, :], ALU.mult).then_inc(w_ok, 1)

            def to_edge(g):
                edge = CHUNK - 1 if g < 2 else 0
                ac = cum[g][:, 0:S].rearrange("p (n c) -> p n c", c=CHUNK)
                dve.tensor_tensor(arg[g % 2][:].rearrange("p (n c) -> p n c", c=CHUNK),
                                  ac[:, :, edge:edge + 1].to_broadcast([P, NCH, CHUNK]), ac, ALU.subtract).then_inc(g_arg, 1)

            def gated(g):
                i, e = g % 2, 2 * (g % 2)
                dve.wait_ge(g_ex, g + 1)
                dve.tensor_tensor(qin[g][:], qG[:, i, :], ex[e][:], ALU.mult)
                dve.tensor_tensor(kin[g][:], kG[:, i, :], ex[e + 1][:], ALU.mult).then_inc(g_qk, 1)
                dve.wait_ge(g_ex2, g + 1)
                dve.tensor_tensor(kendc[g][:], kGc[:, i, :], kendc[g][:], ALU.mult)
                dve.tensor_tensor(kend[g][:], kG[:, i, :], arg[g % 2][:], ALU.mult).then_inc(g_done, 1)
                dve.wait_ge(g_done, g + 1)
            to_edge(0)
            to_edge(1)
            gated(0)
            to_edge(2)
            gated(1)
            to_edge(3)
            gated(2)
            gated(3)
            for g in range(4):
                dve.wait_ge(state_mm, g + 1)
                order = range(NCH) if g < 2 else range(NCH - 1, -1, -1)
                own.step(dve.tensor_copy(state[g][:, order[0], :], ps[:, 1 + g % 2, 0:P]))
                for n, nxt in zip(order, order[1:]):
                    ins = dve.scalar_tensor_tensor(state[g][:, nxt, :], state[g][:, n, :], last[:, g, n:n + 1],
                                                   ps[:, 3 + 2 * (g % 2) + n % 2, (n // 2) * P:(n // 2 + 1) * P],
                                                   ALU.mult, ALU.add)
                    if nxt != order[-1]:
                        own.step(ins)
                ins.then_inc(state_ok, 1)
            def filter_layer(i):
                dve.wait_ge(f_mm, i + 1)
                if i:
                    dve.wait_ge(f_sin, i)
                own.step(dve.tensor_scalar(ft[0][:], bank(2, S, HID), fvec[:, i:i + 1], fvec[:, 3:4], ALU.add, ALU.mult))
                own.step(dve.tensor_scalar(ft[1][:], ft[0][:], 1.0 / (2 * np.pi), ROUND, ALU.mult, ALU.add))
                own.step(dve.tensor_scalar(ft[1][:], ft[1][:], -ROUND, None, ALU.add))
                own.step(dve.scalar_tensor_tensor(ft[0][:], ft[1][:], -TWO_PI_HI, ft[0][:], ALU.mult, ALU.add))
                own.step(dve.scalar_tensor_tensor(ft[0][:], ft[1][:], -TWO_PI_LO, ft[0][:], ALU.mult, ALU.add))
                dve.tensor_scalar(ft[0][:], ft[0][:], PI_SAFE, -PI_SAFE, ALU.min, ALU.max).then_inc(f_arg, 1)

            for s_ in range(G_HEADS + 3):
                h = s_
                if h < G_HEADS:
                    dve.wait_ge(fb_mm, h + 1)
                    if h >= 2:
                        dve.wait_ge(o_mm, h - 1)
                    if h >= 1:
                        dve.wait_ge(att_ok, h)
                    for d in range(2):
                        ins = dve.tensor_tensor(tmp[d][:].rearrange("p (b c) -> p b c", c=P),
                                                bank(3 + 2 * (h % 2) + d).rearrange("p (b c) -> p b c", c=P),
                                                masks[:, d:d + 1, :].to_broadcast([P, ST, P]), ALU.mult)
                    own.step(ins)
                    dve.tensor_tensor(att[h % 2][:], tmp[0][:], tmp[1][:], ALU.add).then_inc(att_ok, 1)
                    if h < 3:
                        filter_layer(h)
                h = s_ - 2
                if 0 <= h < G_HEADS:
                    dve.wait_ge(gh_mm, h + 1)
                    own.step(dve.tensor_scalar(tmp[2 + h % 2][:], bank(7), 1.0 / P, EPS, ALU.mult, ALU.add))
                    dve.reciprocal(tmp[2 + h % 2][:], tmp[2 + h % 2][:]).then_inc(gh_v, 1)
                    dve.wait_ge(gh_r, h + 1)
                    own.step(dve.scalar_tensor_tensor(oG[h][:], oG[h][:], vcol("gla_norm_2"), tmp[2 + h % 2][:], ALU.mult, ALU.mult))
                    dve.tensor_tensor(og[:, h, :], og[:, h, :], oG[h][:], ALU.mult).then_inc(gh_y, 1)

            for tt in range(HT):
                dve.wait_ge(f_out, tt + 1)
                for j in range(2):
                    own.mark(dve.tensor_tensor(hb[j][:], bank(3 + 2 * (tt % 2) + j), decay[:, tt, :], ALU.mult))
                own.settle()
                if tt == 0:
                    own.step(dve.memset(hb[1][0:1, :], 0.0))
                dve.tensor_tensor(ab[:, 0, tt, :], hb[0][:], hb[1][:], ALU.add)
                dve.tensor_tensor(ab[:, 1, tt, :], hb[0][:], hb[1][:], ALU.subtract).then_inc(ab_done, 1)
                dve.wait_ge(ab_done, tt + 1)
            for tt in range(HT):
                dve.wait_ge(ab_h, tt + 1)
                for j in range(2):
                    ins = dve.tensor_tensor(abL[:, j, tt, :], ab[:, j, tt, :], abH[:, j, tt, :].bitcast(F32), ALU.subtract)
                ins.then_inc(ab_l, 1)
            def take(u, dst, m=P):
                dve.wait_ge(unit_done, u + 1)
                dve.tensor_copy(dst, bank(u % SLOTS, S, m)).then_inc(bank_free, 1)
            base = st["sa"].base
            for i in range(9):
                take(base + i, nyq[:] if i == 4 else spec[:, i - (i > 4), :], 1 if i == 4 else P)
            dve.wait_ge(nrm_mm, 1)
            own.step(dve.tensor_scalar(nrm[:], ps[:, 7, 0:HT], 0.5, EPS, ALU.mult, ALU.add))
            dve.reciprocal(nrm[:], nrm[:]).then_inc(nrm_v, 1)
            taken(base + 5)
            own.step(dve.memset(spec[0:1, HT, :], 0.0))
            for tt in range(HT):
                dve.wait_ge(wt_h, tt + 1)
                dve.tensor_tensor(wtL[:, tt, :], bank(3 + tt), wtH[:, tt, :].bitcast(F32), ALU.subtract).then_inc(wt_l, 1)

            def low_y(k):
                dve.wait_ge(y_h, k + 1)
                for j in range(2):
                    ins = dve.tensor_tensor(YL[:, HT * j + k, :], tmp[2 * (k % 2) + j][:], YH[:, HT * j + k, :].bitcast(F32), ALU.subtract)
                ins.then_inc(y_l, 1)
            base = st["uu"].base
            for i in range(8):
                take(base + i, U[:, i, :])
                k = i - 4
                if k >= 0:
                    taken(base + i)
                    if k >= 2:
                        dve.wait_ge(y_l, k - 1)
                    re, im = tmp[2 * (k % 2)], tmp[2 * (k % 2) + 1]
                    ur, us, kr, ks = U[:, k, :], U[:, HT + k, :], spec[:, k, :], spec[:, HT + k, :]
                    own.mark(dve.tensor_tensor(re[:], ur, kr, ALU.mult))
                    own.mark(dve.tensor_tensor(hb[0][:], us, ks, ALU.mult))
                    own.mark(dve.tensor_tensor(im[:], ur, ks, ALU.mult))
                    own.step(dve.tensor_tensor(hb[1][:], us, kr, ALU.mult))
                    own.mark(dve.tensor_tensor(re[:], re[:], hb[0][:], ALU.subtract))
                    ins = dve.tensor_tensor(im[:], im[:], hb[1][:], ALU.add)
                    if k == 0:
                        own.step(ins)
                        ins = dve.tensor_tensor(im[0:1, :], U[0:1, HT, :], nyq[:], ALU.mult)
                    ins.then_inc(y_t, 1)
                    if k >= 1:
                        low_y(k - 1)
            low_y(3)
            dve.wait_ge(y_l, HT)
            for k in range(HT):
                dve.wait_ge(og_h, k + 1)
                dve.tensor_tensor(yL[:, HT + k, :], og[:, k, :], yH[:, HT + k, :].bitcast(F32), ALU.subtract).then_inc(y2_ok, 1)
            base = st["inv"].base
            for i in range(4):
                take(base + i, yt[:, i, :])
            dve.wait_ge(nrm_r, 1)

            def low_half(c):
                dve.wait_ge(yc_h, c + 1)
                dve.tensor_tensor(yL[:, c, :], tmp[2 + c % 2][:], yH[:, c, :].bitcast(F32), ALU.subtract).then_inc(y2_ok, 1)
            for c in range(HT):
                if c >= 2:
                    dve.wait_ge(y2_ok, HT + c - 1)
                if c:
                    dve.wait_ge(yc_ok, c)
                own.step(dve.tensor_scalar(tmp[0][:], wk[:, c, :], vcol("hyena_bias_2", c), None, ALU.mult))
                dve.wait_ge(yt_mm, c + 1)
                own.step(dve.scalar_tensor_tensor(tmp[1][:], bank(3 + c), nrm[:, c:c + 1], tmp[0][:], ALU.mult, ALU.add))
                dve.tensor_tensor(tmp[2 + c % 2][:], tmp[1][:], x0c[:, c, :], ALU.mult).then_inc(yc_ok, 1)
                if c:
                    low_half(c - 1)
            low_half(HT - 1)
            dve.wait_ge(y2_ok, DT)
            residual(st["wo"], lambda i: mod[:, 16:24, 0][:, bass.ds(i, 1)], done="wo")
            stat("mlp2")
            dve.wait_ge(stat_r, stat_no["mlp2"] + 1)
            modulate(16, x, r, S, 2, lambda k: mod[:, 24 + k, 0:1], hH, hL)

            def hidden(q, n0):
                def one(pos):
                    dve.wait_ge(unit_done, pos.u + 1)
                    dve.tensor_scalar(tmp[pos.slot][:], bank(pos.slot), 0.0, None, ALU.max).then_inc(bank_free, 1)
                    taken(pos.u)
                    own.group(n0, pos.i, 2)
                    own.step(dve.tensor_tensor(tmp[3][:], tmp[pos.slot][:], tmp[pos.slot][:], ALU.mult))
                    h_, l_ = (y_[:, bass.ds(pos.i, 1), :][:, 0] for y_ in (mH[q % 2], mL[q % 2]))
                    split(tmp[3][:], h_, l_).then_inc(res["m1"], 1)
                    dve.wait_ge(res["m1"], pos.i + DT * q + 1)
                each_unit(dve, st[f"m1_{q}"], one)
                own.leave(n0 + 2 * DT)
            for name, q in (("m1_0", 0), ("m1_1", 1), ("m2_0", 0), ("m1_2", 2), ("m2_1", 1), ("m1_3", 3),
                            ("m2_2", 2), ("m2_3", 3)):
                if name[1] == "1":
                    hidden(q, own.n)
                else:
                    residual(st[name], lambda i: mod[:, 40:48, 0][:, bass.ds(i, 1)], squares=(q == 3),
                             done="m2_3" if q == 3 else None)
            finish("fin2", "norm_final_2")


def tables():
    i = np.arange(P)
    swap_m = np.zeros((P, P))
    swap_m[i ^ 32, i] = 1
    tri = (i[:, None] // CHUNK == i[None, :] // CHUNK) & (i[:, None] <= i[None, :])
    square = np.stack([np.eye(P), swap_m, np.eye(P)[::-1], tri, tri.T])
    inv_freq = 1.0 / (10000.0 ** (np.arange(0, A_DK, 2) / A_DK))
    angle = (np.arange(S)[:, None] * inv_freq[None, :]).T[i % 32]
    sign = np.where(i % 64 < 32, -1.0, 1.0)[:, None]
    rope_m = np.stack([np.cos(angle), sign * np.sin(angle)])
    tt, ff = np.arange(S), np.arange(S)
    turn = 2 * np.pi * ((tt[:, None] * ff[None, :]) % (2 * S)) / (2 * S)
    cos_m, sin_m = np.cos(turn), np.sin(turn)
    alt = (-1.0) ** tt
    sin_f = sin_m.copy()
    sin_f[:, 0] = alt
    dft = np.concatenate([cos_m, sin_f], axis=1)
    cos_i, sin_i = cos_m / S, sin_m / S
    cos_i[0] = 1 / (2 * S)
    sin_i[0] = alt / (2 * S)
    inverse = np.concatenate([cos_i, sin_i], axis=0)
    length = np.linspace(0.0, 1.0, S)[:, None]
    w = 2.0 * np.pi * np.arange(S) / S
    bands = (EMB - 1) // 2
    ang = w[:, None] * np.linspace(1e-4, bands - 1, bands)[None, :]
    z_m = np.concatenate([length, np.cos(ang), -np.sin(ang)], axis=1).T
    rates = np.abs(np.linspace(np.log(1e-2) / 1.5, np.log(1e-2) / 0.3, D_HY))
    decay_m = np.exp(-length * rates[None, :])
    reset_m = np.broadcast_to((np.arange(S) % CHUNK != 0), (P, S))
    f = lambda a: np.ascontiguousarray(a, dtype=np.float32)
    return {"k_square": f(square), "k_rope": f(rope_m), "k_dft": f(dft), "k_inv": f(inverse),
            "k_z": f(z_m), "k_decay": f(decay_m), "k_reset": f(reset_m)}


_INS = ["x", "mem", "norm_mix_g", "w_in", "lam_q1", "lam_k1", "lam_q2", "lam_k2", "subln_g",
        "rel_bias", "w_up_a", "w_up_b", "w_out", "norm_cross_g", "norm_mem_g", "w_cq", "w_ckv",
        "w_co", "norm_ffn_g", "w_gate_up", "w_down", "norm_final_g", "c_2", "ctx_2", "c_ctx_2",
        "w_ada_2", "b_ada_2", "norm_mix_2", "norm_mlp_2", "w_in_2", "conv_w_2", "conv_b_2",
        "filt_w1_2", "filt_b1_2", "filt_w2_2", "filt_b2_2", "filt_w3_2", "filt_b3_2",
        "filt_freq_2", "filt_wout_2", "hyena_bias_2", "gk_w_fwd_2", "gk_b_fwd_2", "gk_w_bwd_2",
        "gk_b_bwd_2", "gla_norm_2", "w_out_2", "w_mlp1_2", "w_mlp2_2", "norm_final_2"]
_OUTS = [((1, S, D), "float32")]


def kernel(**inputs):
    import numpy as _np
    import concourse.bacc as _bacc
    from concourse import mybir as _mybir
    from concourse.bass_utils import run_bass_kernel_spmd as _run

    nc = _bacc.Bacc("TRN2", target_bir_lowering=False, num_devices=1)
    given = {name: inputs[name] for name in _INS}
    given.update(tables())
    arrays, args = {}, {}
    for name, value in given.items():
        a = _np.ascontiguousarray(value)
        arrays[f"in_{name}_dram"] = a
        args[name] = nc.dram_tensor(f"in_{name}_dram", a.shape, _mybir.dt.from_np(a.dtype), kind="ExternalInput").ap()
    outs = []
    for i, (shape, dtype) in enumerate(_OUTS):
        dt = _mybir.dt.from_np(_np.dtype(dtype))
        outs.append(nc.dram_tensor(f"out_{i}_dram", shape, dt, kind="ExternalOutput").ap())
    build(nc, args, outs[0])
    r = _run(nc, [arrays], core_ids=[0])
    got = tuple(r.results[0][f"out_{i}_dram"] for i in range(len(_OUTS)))
    return got[0]
```
